# Optimizing a Trainium2 kernel written in Bass

```python
import jax
import jax.numpy as jnp
from jax import lax
import numpy as np
import math
import jax, jax.numpy as jnp

D_MODEL = 1024
BATCH = 1
SEQ = 256
DEPTH = 1

MEM_LEN = 256
MOBA_HEADS = 8
MOBA_HEAD_DIM = 64
MOBA_BLOCK = 256
MOBA_TOPK = 3
FOX_HEADS = 8
FOX_HEAD_DIM = 64
MEM_HEADS = 4
MEM_HEAD_DIM = 128
Q_BLOCK = 128
ROPE_THETA = 500000.0
ROPE_FRACTION_DIV = 4
N_BRANCHES = 3
D_FF = ((-((-8 * D_MODEL) // 3)) + 255) // 256 * 256
NORM_EPS = 1e-6
MOBA_WIDTH = MOBA_HEADS * MOBA_HEAD_DIM
FOX_WIDTH = FOX_HEADS * FOX_HEAD_DIM
MEM_WIDTH = MEM_HEADS * MEM_HEAD_DIM
IN_SIZES = (MOBA_WIDTH,) * 3 + (FOX_WIDTH,) * 3 + (FOX_HEADS, MEM_WIDTH) + (D_MODEL,) * N_BRANCHES
D_IN = sum(IN_SIZES)


def rms_norm(x, gain):
    xf = x.astype(jnp.float32)
    y = xf * lax.rsqrt(jnp.mean(xf * xf, axis=-1, keepdims=True) + NORM_EPS)
    return (y * gain.astype(jnp.float32)).astype(x.dtype)

def split_heads(t, n_heads):
    b, s, _ = t.shape
    return t.reshape(b, s, n_heads, -1).transpose(0, 2, 1, 3)

def merge_heads(t):
    b, h, s, d = t.shape
    return t.transpose(0, 2, 1, 3).reshape(b, s, h * d)

def partial_rope(t):
    seq, dim = t.shape[2], t.shape[3]
    rot = dim // ROPE_FRACTION_DIV
    half = rot // 2
    inv_freq = 1.0 / (ROPE_THETA ** (jnp.arange(half, dtype=jnp.float32) * 2.0 / rot))
    ang = jnp.arange(seq, dtype=jnp.float32)[:, None] * inv_freq[None, :]
    cos, sin = jnp.cos(ang), jnp.sin(ang)
    tf = t.astype(jnp.float32)
    x1, x2 = tf[..., :half], tf[..., half:rot]
    out = jnp.concatenate([x1 * cos - x2 * sin, x2 * cos + x1 * sin, tf[..., rot:]], axis=-1)
    return out.astype(t.dtype)

def moba_attention(q, k, v):
    b, h, s, d = q.shape
    scale = d ** -0.5
    n_blocks = -(-s // MOBA_BLOCK)
    pad = n_blocks * MOBA_BLOCK - s
    kp = jnp.pad(k, ((0, 0), (0, 0), (0, pad), (0, 0)))
    vp = jnp.pad(v, ((0, 0), (0, 0), (0, pad), (0, 0)))
    kb = kp.reshape(b, h, n_blocks, MOBA_BLOCK, d)
    vb = vp.reshape(b, h, n_blocks, MOBA_BLOCK, d)
    k_mean = jnp.mean(kb.astype(jnp.float32), axis=3)
    topk = min(MOBA_TOPK, n_blocks)
    b_idx = jnp.arange(b)[:, None, None, None]
    h_idx = jnp.arange(h)[None, :, None, None]
    key_off = jnp.arange(MOBA_BLOCK)
    q_off = jnp.arange(Q_BLOCK)
    block_ids = jnp.arange(n_blocks)

    def chunk(ci):
        t0 = ci * Q_BLOCK
        cur = t0 // MOBA_BLOCK
        qc = lax.dynamic_slice_in_dim(q, t0, Q_BLOCK, axis=2)
        gate = jnp.einsum('bhqd,bhnd->bhqn', qc.astype(jnp.float32), k_mean)
        gate = jnp.where(block_ids < cur, gate, -jnp.inf)
        _, sel = lax.top_k(gate, topk)
        sel_valid = sel < cur
        k_sel = kb[b_idx, h_idx, sel]
        v_sel = vb[b_idx, h_idx, sel]
        s_sel = jnp.einsum('bhqd,bhqnkd->bhqnk', qc, k_sel).astype(jnp.float32) * scale
        s_sel = jnp.where(sel_valid[..., None], s_sel, -jnp.inf)
        k_own = lax.dynamic_slice_in_dim(kp, cur * MOBA_BLOCK, MOBA_BLOCK, axis=2)
        v_own = lax.dynamic_slice_in_dim(vp, cur * MOBA_BLOCK, MOBA_BLOCK, axis=2)
        s_own = jnp.einsum('bhqd,bhkd->bhqk', qc, k_own).astype(jnp.float32) * scale
        causal = (key_off[None, :] + cur * MOBA_BLOCK) <= (q_off[:, None] + t0)
        s_own = jnp.where(causal, s_own, -jnp.inf)
        scores = jnp.concatenate([s_sel.reshape(b, h, Q_BLOCK, topk * MOBA_BLOCK), s_own], axis=-1)
        p = jax.nn.softmax(scores, axis=-1).astype(v.dtype)
        p_sel = p[..., :topk * MOBA_BLOCK].reshape(b, h, Q_BLOCK, topk, MOBA_BLOCK)
        p_own = p[..., topk * MOBA_BLOCK:]
        return (jnp.einsum('bhqnk,bhqnkd->bhqd', p_sel, v_sel)
                + jnp.einsum('bhqk,bhkd->bhqd', p_own, v_own))

    out = lax.map(chunk, jnp.arange(s // Q_BLOCK))
    return jnp.moveaxis(out, 0, 2).reshape(b, h, s, d)

def fox_attention(q, k, v, log_f):
    b, h, s, d = q.shape
    scale = d ** -0.5
    cum = jnp.cumsum(log_f, axis=-1)
    key_pos = jnp.arange(s)
    q_off = jnp.arange(Q_BLOCK)

    def chunk(ci):
        t0 = ci * Q_BLOCK
        qc = lax.dynamic_slice_in_dim(q, t0, Q_BLOCK, axis=2)
        cq = lax.dynamic_slice_in_dim(cum, t0, Q_BLOCK, axis=2)
        scores = (jnp.einsum('bhqd,bhkd->bhqk', qc, k).astype(jnp.float32) * scale
                  + cq[..., None] - cum[:, :, None, :])
        causal = key_pos[None, :] <= (q_off[:, None] + t0)
        scores = jnp.where(causal, scores, -jnp.inf)
        p = jax.nn.softmax(scores, axis=-1).astype(v.dtype)
        return jnp.einsum('bhqk,bhkd->bhqd', p, v)

    out = lax.map(chunk, jnp.arange(s // Q_BLOCK))
    return jnp.moveaxis(out, 0, 2).reshape(b, h, s, d)

def memory_attention(q, mk, mv):
    scale = q.shape[-1] ** -0.5
    scores = jnp.einsum('bhsd,bhmd->bhsm', q, mk).astype(jnp.float32) * scale
    p = jax.nn.softmax(scores, axis=-1).astype(mv.dtype)
    return jnp.einsum('bhsm,bhmd->bhsd', p, mv)

def first_inputs(seed: int = 0) -> dict:
    key = jax.random.key(seed)
    ks = jax.random.split(key, 24)
    L = DEPTH

    def normal(k, shape, scale):
        return jax.random.normal(k, shape, jnp.float32) * scale

    def gain(k, shape):
        return 1.0 + 0.1 * jax.random.normal(k, shape, jnp.float32)

    return {
        "x": normal(ks[0], (BATCH, SEQ, D_MODEL), 1.0),
        "mem": normal(ks[1], (BATCH, MEM_LEN, D_MODEL), 1.0),
        "g_mix": gain(ks[2], (L, D_MODEL)),
        "w_in": normal(ks[3], (L, D_MODEL, D_IN), D_MODEL ** -0.5),
        "b_forget": 4.0 + 0.5 * jax.random.normal(ks[4], (L, FOX_HEADS), jnp.float32),
        "g_q_moba": gain(ks[5], (L, MOBA_HEAD_DIM)),
        "g_k_moba": gain(ks[6], (L, MOBA_HEAD_DIM)),
        "g_q_fox": gain(ks[7], (L, FOX_HEAD_DIM)),
        "g_k_fox": gain(ks[8], (L, FOX_HEAD_DIM)),
        "g_q_mem": gain(ks[9], (L, MEM_HEAD_DIM)),
        "g_k_mem": gain(ks[10], (L, MEM_HEAD_DIM)),
        "g_mem": gain(ks[11], (L, D_MODEL)),
        "w_mem_kv": normal(ks[12], (L, D_MODEL, 2 * MEM_WIDTH), D_MODEL ** -0.5),
        "w_br_moba": normal(ks[13], (L, MOBA_WIDTH, D_MODEL), MOBA_WIDTH ** -0.5),
        "w_br_fox": normal(ks[14], (L, FOX_WIDTH, D_MODEL), FOX_WIDTH ** -0.5),
        "w_br_mem": normal(ks[15], (L, MEM_WIDTH, D_MODEL), MEM_WIDTH ** -0.5),
        "w_out": normal(ks[16], (L, D_MODEL, D_MODEL), D_MODEL ** -0.5),
        "g_ffn": gain(ks[17], (L, D_MODEL)),
        "w_gate": normal(ks[18], (L, D_MODEL, D_FF), D_MODEL ** -0.5),
        "w_up": normal(ks[19], (L, D_MODEL, D_FF), D_MODEL ** -0.5),
        "w_down": normal(ks[20], (L, D_FF, D_MODEL), D_FF ** -0.5),
    }

def first_block(x, mem, g_mix, w_in, b_forget, g_q_moba, g_k_moba, g_q_fox, g_k_fox, g_q_mem, g_k_mem,
              g_mem, w_mem_kv, w_br_moba, w_br_fox, w_br_mem, w_out, g_ffn, w_gate, w_up, w_down):
    split_points = np.cumsum(IN_SIZES)[:-1].tolist()
    for layer in range(DEPTH):
        h = rms_norm(x, g_mix[layer])
        proj = h @ w_in[layer]
        (q_m, k_m, v_m, q_f, k_f, v_f, f_logit, q_c, a_m, a_f, a_c) = jnp.split(proj, split_points, axis=-1)

        q_m = partial_rope(rms_norm(split_heads(q_m, MOBA_HEADS), g_q_moba[layer]))
        k_m = partial_rope(rms_norm(split_heads(k_m, MOBA_HEADS), g_k_moba[layer]))
        y_m = moba_attention(q_m, k_m, split_heads(v_m, MOBA_HEADS))

        log_f = jax.nn.log_sigmoid(f_logit.astype(jnp.float32)
                                   + b_forget[layer].astype(jnp.float32)).transpose(0, 2, 1)
        q_f = rms_norm(split_heads(q_f, FOX_HEADS), g_q_fox[layer])
        k_f = rms_norm(split_heads(k_f, FOX_HEADS), g_k_fox[layer])
        y_f = fox_attention(q_f, k_f, split_heads(v_f, FOX_HEADS), log_f)

        mkv = rms_norm(mem, g_mem[layer]) @ w_mem_kv[layer]
        mk, mv = jnp.split(mkv, 2, axis=-1)
        mk = rms_norm(split_heads(mk, MEM_HEADS), g_k_mem[layer])
        q_c = rms_norm(split_heads(q_c, MEM_HEADS), g_q_mem[layer])
        y_c = memory_attention(q_c, mk, split_heads(mv, MEM_HEADS))

        merged = (jax.nn.sigmoid(a_m) * (merge_heads(y_m) @ w_br_moba[layer])
                  + jax.nn.sigmoid(a_f) * (merge_heads(y_f) @ w_br_fox[layer])
                  + jax.nn.sigmoid(a_c) * (merge_heads(y_c) @ w_br_mem[layer]))
        x = x + merged @ w_out[layer]

        h2 = rms_norm(x, g_ffn[layer])
        x = x + (jax.nn.silu(h2 @ w_gate[layer]) * (h2 @ w_up[layer])) @ w_down[layer]
    return x


DEPTH_2 = 2

N_MIXERS = 4
N_HEADS = 8
HEAD_DIM = D_MODEL // N_HEADS
ROPE_THETA_2 = 10000.0
HG_CHUNK = 64
DA_HALF = HEAD_DIM // 2
NSA_GROUPS = 2
NSA_HPG = N_HEADS // NSA_GROUPS
CMP_BLOCK = 32
CMP_STRIDE = 16
SLC_BLOCK = 64
SLC_TOPK = 16
WINDOW = 512
NSA_Q_BLOCK = 64
D_FF_2 = 2816
N_EXPERTS = 8
TOP_K = 2
D_FF_EXPERT = 3584
MOE_BLOCK = 128
LN_EPS = 1e-5
NEG = -1e30
FORCE = 1e9
DEEPNORM_ALPHA = (2 * DEPTH_2) ** 0.25
DEEPNORM_BETA = (8 * DEPTH_2) ** -0.25


def layer_norm(x, g, b):
    xf = x.astype(jnp.float32)
    mu = jnp.mean(xf, axis=-1, keepdims=True)
    xc = xf - mu
    var = jnp.mean(xc * xc, axis=-1, keepdims=True)
    return (xc * lax.rsqrt(var + LN_EPS) * g.astype(jnp.float32) + b.astype(jnp.float32)).astype(x.dtype)

def rms_norm_2(x, g):
    xf = x.astype(jnp.float32)
    return xf * lax.rsqrt(jnp.mean(xf * xf, axis=-1, keepdims=True) + LN_EPS) * g.astype(jnp.float32)

def rope(x, pos):
    d = x.shape[-1]
    half = d // 2
    inv = ROPE_THETA_2 ** (-jnp.arange(half, dtype=jnp.float32) / half)
    ang = pos.astype(jnp.float32)[:, None] * inv[None, :]
    shp = (1, x.shape[1]) + (1,) * (x.ndim - 3) + (half,)
    cos = jnp.cos(ang).reshape(shp)
    sin = jnp.sin(ang).reshape(shp)
    xf = x.astype(jnp.float32)
    x1, x2 = xf[..., :half], xf[..., half:]
    return jnp.concatenate([x1 * cos - x2 * sin, x2 * cos + x1 * sin], axis=-1).astype(x.dtype)

def masked_softmax(s, mask):
    s = jnp.where(mask, s.astype(jnp.float32), NEG)
    p = jax.nn.softmax(s, axis=-1)
    return jnp.where(mask, p, 0.0)

def hgrn2_mixer(h, w_in, lb_logits, norm_g, w_out, layer):
    b, s, _ = h.shape
    nh, dk = N_HEADS, HEAD_DIM
    c = HG_CHUNK
    nc = s // c
    q, f, i, g = jnp.split(h @ w_in, 4, axis=-1)
    lb = jnp.cumsum(jax.nn.softmax(lb_logits.astype(jnp.float32), axis=0), axis=0)[layer]
    forget = lb + (1.0 - lb) * jax.nn.sigmoid(f.astype(jnp.float32))
    log_f = jnp.log(forget)
    k = 1.0 - forget
    q = jax.nn.silu(q.astype(jnp.float32))
    v = i.astype(jnp.float32)

    def to_chunks(t):
        return t.reshape(b, nc, c, nh, dk).transpose(1, 0, 3, 2, 4)

    tri = jnp.tril(jnp.ones((c, c), bool))[:, :, None]

    def step(state, inp):
        qc, kc, vc, lf = inp
        cum = jnp.cumsum(lf, axis=2)
        rel = jnp.where(tri, cum[:, :, :, None, :] - cum[:, :, None, :, :], -jnp.inf)
        scores = jnp.einsum('bhtd,bhsd,bhtsd->bhts', qc, kc, jnp.exp(rel))
        out = scores @ vc + jnp.einsum('bhtd,bhdv->bhtv', qc * jnp.exp(cum), state)
        last = cum[:, :, -1:, :]
        new_state = jnp.exp(last[:, :, 0, :, None]) * state + jnp.einsum('bhsd,bhsv->bhdv', kc * jnp.exp(last - cum), vc)
        return new_state, out

    state0 = jnp.zeros((b, nh, dk, dk), jnp.float32)
    _, o = lax.scan(step, state0, (to_chunks(q), to_chunks(k), to_chunks(v), to_chunks(log_f)))
    o = o.transpose(1, 0, 3, 2, 4).reshape(b, s, nh, dk)
    o = rms_norm_2(o, norm_g) * jax.nn.sigmoid(g.astype(jnp.float32)).reshape(b, s, nh, dk)
    return o.reshape(b, s, D_MODEL).astype(h.dtype) @ w_out

def diff_attention_mixer(h, w_in, lam, norm_g, w_out, pos, layer):
    b, s, _ = h.shape
    q, k, v = jnp.split(h @ w_in, 3, axis=-1)
    q = rope(q.reshape(b, s, N_HEADS, 2, DA_HALF), pos).transpose(0, 2, 3, 1, 4)
    k = rope(k.reshape(b, s, N_HEADS, 2, DA_HALF), pos).transpose(0, 2, 3, 1, 4)
    v = v.reshape(b, s, N_HEADS, HEAD_DIM).transpose(0, 2, 1, 3)
    lam_init = 0.8 - 0.6 * math.exp(-0.3 * layer)
    lf = lam.astype(jnp.float32)
    lmb = jnp.exp(jnp.sum(lf[0] * lf[1])) - jnp.exp(jnp.sum(lf[2] * lf[3])) + lam_init
    kpos = jnp.arange(s)
    scale = DA_HALF ** -0.5

    def block(bi):
        s0 = bi * Q_BLOCK
        qb = lax.dynamic_slice_in_dim(q, s0, Q_BLOCK, axis=3)
        sc = jnp.einsum('bhcqd,bhckd->bhcqk', qb, k).astype(jnp.float32) * scale
        mask = (s0 + jnp.arange(Q_BLOCK))[:, None] >= kpos[None, :]
        p = masked_softmax(sc, mask)
        attn = p[:, :, 0] - lmb * p[:, :, 1]
        return jnp.einsum('bhqk,bhkd->bqhd', attn.astype(v.dtype), v)

    o = lax.map(block, jnp.arange(s // Q_BLOCK))
    o = o.transpose(1, 0, 2, 3, 4).reshape(b, s, N_HEADS, HEAD_DIM)
    o = rms_norm_2(o, norm_g) * (1.0 - lam_init)
    return o.reshape(b, s, D_MODEL).astype(h.dtype) @ w_out

def nsa_mixer(h, w_in, cmp_pe, cmp_w1, cmp_w2, w_out, pos):
    b, s, _ = h.shape
    G, HG, dk = NSA_GROUPS, NSA_HPG, HEAD_DIM
    proj = h @ w_in
    q, kv, gates = jnp.split(proj, [D_MODEL, D_MODEL + 6 * G * dk], axis=-1)
    q = q.reshape(b, s, N_HEADS, dk)
    kv = kv.reshape(b, s, 6, G, dk)
    k_cmp, v_cmp, k_slc, v_slc, k_win, v_win = [kv[:, :, j] for j in range(6)]
    gates = jax.nn.sigmoid(gates.astype(jnp.float32)).reshape(b, s, N_HEADS, 3)
    q_rot = rope(q, pos)
    k_slc = rope(k_slc, pos)
    k_win = rope(k_win, pos)

    n_cmp = (s - CMP_BLOCK) // CMP_STRIDE + 1
    tok_idx = np.arange(n_cmp)[:, None] * CMP_STRIDE + np.arange(CMP_BLOCK)[None, :]

    def compress(t, j):
        blk = t[:, tok_idx] + cmp_pe[j][None, None, :, None, :]
        blk = blk.transpose(0, 3, 1, 2, 4).reshape(b, G, n_cmp, CMP_BLOCK * dk)
        return jax.nn.gelu(blk @ cmp_w1[j]) @ cmp_w2[j]

    kc = compress(k_cmp, 0)
    vc = compress(v_cmp, 1)
    cmp_end = jnp.asarray(np.arange(n_cmp) * CMP_STRIDE + CMP_BLOCK - 1)
    n_slc = s // SLC_BLOCK
    cs = np.arange(n_cmp) * CMP_STRIDE
    ss_ = np.arange(n_slc) * SLC_BLOCK
    ov = np.clip(np.minimum(cs[:, None] + CMP_BLOCK, ss_[None, :] + SLC_BLOCK) - np.maximum(cs[:, None], ss_[None, :]), 0, None) / CMP_BLOCK
    cmp_to_slc = jnp.asarray(ov, jnp.float32)
    n_sel = min(SLC_TOPK, n_slc)
    ks_blk = k_slc.transpose(0, 2, 1, 3).reshape(b, G, n_slc, SLC_BLOCK * dk)
    vs_blk = v_slc.transpose(0, 2, 1, 3).reshape(b, G, n_slc, SLC_BLOCK * dk)
    kw = jnp.pad(k_win.transpose(0, 2, 1, 3), ((0, 0), (0, 0), (WINDOW, 0), (0, 0)))
    vw = jnp.pad(v_win.transpose(0, 2, 1, 3), ((0, 0), (0, 0), (WINDOW, 0), (0, 0)))
    qg = q.reshape(b, s, G, HG, dk).transpose(0, 2, 3, 1, 4)
    qrg = q_rot.reshape(b, s, G, HG, dk).transpose(0, 2, 3, 1, 4)
    scale = dk ** -0.5
    blk_id = jnp.arange(n_slc)
    qb_n = NSA_Q_BLOCK

    def block(bi):
        s0 = bi * qb_n
        tq = s0 + jnp.arange(qb_n)
        qb = lax.dynamic_slice_in_dim(qg, s0, qb_n, axis=3)
        qrb = lax.dynamic_slice_in_dim(qrg, s0, qb_n, axis=3)
        sc = jnp.einsum('bgiqd,bgcd->bgiqc', qb, kc).astype(jnp.float32) * scale
        pc = masked_softmax(sc, cmp_end[None, :] <= tq[:, None])
        o_cmp = jnp.einsum('bgiqc,bgcd->bgiqd', pc.astype(vc.dtype), vc)
        imp = jnp.einsum('bgqc,cn->bgqn', pc.sum(axis=2), cmp_to_slc)
        cur = tq // SLC_BLOCK
        forced = (blk_id[None, :] == 0) | (blk_id[None, :] == cur[:, None]) | (blk_id[None, :] == cur[:, None] - 1)
        imp = jnp.where(forced, FORCE, imp)
        imp = jnp.where(blk_id[None, :] <= cur[:, None], imp, NEG)
        top_s, top_i = lax.top_k(imp, n_sel)
        sel_ok = top_s > 0.5 * NEG
        gidx = top_i.reshape(b, G, qb_n * n_sel, 1)
        kg = jnp.take_along_axis(ks_blk, gidx, axis=2).reshape(b, G, qb_n, n_sel * SLC_BLOCK, dk)
        vg = jnp.take_along_axis(vs_blk, gidx, axis=2).reshape(b, G, qb_n, n_sel * SLC_BLOCK, dk)
        tok = top_i[..., None] * SLC_BLOCK + jnp.arange(SLC_BLOCK)
        ms = (sel_ok[..., None] & (tok <= tq[None, None, :, None, None])).reshape(b, G, 1, qb_n, n_sel * SLC_BLOCK)
        sg = jnp.einsum('bgiqd,bgqmd->bgiqm', qrb, kg).astype(jnp.float32) * scale
        ps = masked_softmax(sg, ms)
        o_slc = jnp.einsum('bgiqm,bgqmd->bgiqd', ps.astype(vg.dtype), vg)
        kwb = lax.dynamic_slice_in_dim(kw, s0, qb_n + WINDOW, axis=2)
        vwb = lax.dynamic_slice_in_dim(vw, s0, qb_n + WINDOW, axis=2)
        kp = s0 - WINDOW + jnp.arange(qb_n + WINDOW)
        mw = (kp[None, :] <= tq[:, None]) & (kp[None, :] > tq[:, None] - WINDOW) & (kp[None, :] >= 0)
        sw = jnp.einsum('bgiqd,bgkd->bgiqk', qrb, kwb).astype(jnp.float32) * scale
        pw = masked_softmax(sw, mw)
        o_win = jnp.einsum('bgiqk,bgkd->bgiqd', pw.astype(vwb.dtype), vwb)
        o = jnp.stack([o_cmp, o_slc, o_win], axis=-2)
        return o.transpose(0, 3, 1, 2, 4, 5).reshape(b, qb_n, N_HEADS, 3, dk)

    o = lax.map(block, jnp.arange(s // qb_n))
    o = o.transpose(1, 0, 2, 3, 4, 5).reshape(b, s, N_HEADS, 3, dk)
    o = jnp.einsum('bshc,bshcd->bshd', gates.astype(o.dtype), o)
    return o.reshape(b, s, D_MODEL) @ w_out

def stick_breaking_mixer(h, w_in, w_out):
    b, s, _ = h.shape
    q, k, v = jnp.split(h @ w_in, 3, axis=-1)
    q = q.reshape(b, s, N_HEADS, HEAD_DIM).transpose(0, 2, 1, 3)
    k = k.reshape(b, s, N_HEADS, HEAD_DIM).transpose(0, 2, 1, 3)
    v = v.reshape(b, s, N_HEADS, HEAD_DIM).transpose(0, 2, 1, 3)
    kpos = jnp.arange(s)
    scale = HEAD_DIM ** -0.5

    def block(bi):
        s0 = bi * Q_BLOCK
        qb = lax.dynamic_slice_in_dim(q, s0, Q_BLOCK, axis=2)
        z = jnp.einsum('bhqd,bhkd->bhqk', qb, k).astype(jnp.float32) * scale
        tq = s0 + jnp.arange(Q_BLOCK)
        strict = kpos[None, :] < tq[:, None]
        log_keep = jnp.where(strict, jax.nn.log_sigmoid(-z), 0.0)
        after = lax.cumsum(log_keep, axis=3, reverse=True) - log_keep
        a = jnp.where(strict, jnp.exp(jax.nn.log_sigmoid(z) + after), 0.0)
        return jnp.einsum('bhqk,bhkd->bqhd', a.astype(v.dtype), v)

    o = lax.map(block, jnp.arange(s // Q_BLOCK))
    o = o.transpose(1, 0, 2, 3, 4).reshape(b, s, D_MODEL)
    return o @ w_out

def swiglu(h, w_gate, w_up, w_down):
    return (jax.nn.silu(h @ w_gate) * (h @ w_up)) @ w_down

def moe_swiglu(h, w_router, w_gate, w_up, w_down):
    b, s, d = h.shape
    t = b * s
    hf = h.reshape(t, d)
    logits = (hf @ w_router).astype(jnp.float32)
    top_val, top_idx = lax.top_k(logits, TOP_K)
    gates = jax.nn.softmax(top_val, axis=-1)
    n_assign = t * TOP_K
    flat_e = top_idx.reshape(n_assign)
    flat_tok = jnp.repeat(jnp.arange(t, dtype=jnp.int32), TOP_K)
    order = jnp.argsort(flat_e)
    sorted_e = flat_e[order]
    sorted_tok = flat_tok[order]
    counts = jnp.bincount(flat_e, length=N_EXPERTS)
    padded = (counts + MOE_BLOCK - 1) // MOE_BLOCK * MOE_BLOCK
    pad_end = jnp.cumsum(padded)
    pad_start = pad_end - padded
    grp_start = jnp.cumsum(counts) - counts
    dest = (pad_start[sorted_e] + jnp.arange(n_assign) - grp_start[sorted_e]).astype(jnp.int32)
    n_blocks = -(-n_assign // MOE_BLOCK) + N_EXPERTS
    n_slots = n_blocks * MOE_BLOCK
    slot_tok = jnp.zeros((n_slots,), jnp.int32).at[dest].set(sorted_tok)
    block_e = jnp.minimum(jnp.searchsorted(pad_end, jnp.arange(n_blocks) * MOE_BLOCK, side='right'), N_EXPERTS - 1)
    xs = hf[slot_tok].reshape(n_blocks, MOE_BLOCK, d)

    def expert_block(args):
        xb, e = args
        return (jax.nn.silu(xb @ w_gate[e]) * (xb @ w_up[e])) @ w_down[e]

    ys = lax.map(expert_block, (xs, block_e)).reshape(n_slots, d)
    slot_of_assign = jnp.zeros((n_assign,), jnp.int32).at[order].set(dest)
    y = ys[slot_of_assign].reshape(t, TOP_K, d)
    out = jnp.einsum('tk,tkd->td', gates.astype(y.dtype), y)
    return out.reshape(b, s, d)

def second_inputs(seed: int = 0) -> dict:
    key = jax.random.key(seed)
    ks = jax.random.split(key, 25)
    D = D_MODEL
    f32 = jnp.float32

    def nrm(k, shape, scale):
        return jax.random.normal(k, shape, f32) * scale

    nsa_in = D + 6 * NSA_GROUPS * HEAD_DIM + 3 * N_HEADS
    out_scale = DEEPNORM_BETA * D ** -0.5
    return {
        'x': nrm(ks[0], (BATCH, SEQ, D), 1.0),
        'hg_w_in': nrm(ks[1], (D, 4 * D), D ** -0.5),
        'hg_lb': nrm(ks[2], (DEPTH_2 + 1, D), 0.1),
        'hg_norm_g': 1.0 + nrm(ks[3], (HEAD_DIM,), 0.01),
        'hg_w_out': nrm(ks[4], (D, D), out_scale),
        'da_w_in': nrm(ks[5], (D, 3 * D), D ** -0.5),
        'da_lam': nrm(ks[6], (4, DA_HALF), 0.1),
        'da_norm_g': 1.0 + nrm(ks[7], (HEAD_DIM,), 0.01),
        'da_w_out': nrm(ks[8], (D, D), out_scale),
        'nsa_w_in': nrm(ks[9], (D, nsa_in), D ** -0.5),
        'nsa_cmp_pe': nrm(ks[10], (2, CMP_BLOCK, HEAD_DIM), 0.02),
        'nsa_cmp_w1': nrm(ks[11], (2, CMP_BLOCK * HEAD_DIM, HEAD_DIM), (CMP_BLOCK * HEAD_DIM) ** -0.5),
        'nsa_cmp_w2': nrm(ks[12], (2, HEAD_DIM, HEAD_DIM), HEAD_DIM ** -0.5),
        'nsa_w_out': nrm(ks[13], (D, D), out_scale),
        'sb_w_in': nrm(ks[14], (D, 3 * D), D ** -0.5),
        'sb_w_out': nrm(ks[15], (D, D), out_scale),
        'ffn_w_gate': nrm(ks[16], (DEPTH_2 // 2, D, D_FF_2), D ** -0.5),
        'ffn_w_up': nrm(ks[17], (DEPTH_2 // 2, D, D_FF_2), D ** -0.5),
        'ffn_w_down': nrm(ks[18], (DEPTH_2 // 2, D_FF_2, D), DEEPNORM_BETA * D_FF_2 ** -0.5),
        'moe_w_router': nrm(ks[19], (DEPTH_2 // 2, D, N_EXPERTS), D ** -0.5),
        'moe_w_gate': nrm(ks[20], (DEPTH_2 // 2, N_EXPERTS, D, D_FF_EXPERT), D ** -0.5),
        'moe_w_up': nrm(ks[21], (DEPTH_2 // 2, N_EXPERTS, D, D_FF_EXPERT), D ** -0.5),
        'moe_w_down': nrm(ks[22], (DEPTH_2 // 2, N_EXPERTS, D_FF_EXPERT, D), DEEPNORM_BETA * D_FF_EXPERT ** -0.5),
        'ln_g': 1.0 + nrm(ks[23], (DEPTH_2, 2, D), 0.01),
        'ln_b': nrm(ks[24], (DEPTH_2, 2, D), 0.01),
    }

def second_block(x, hg_w_in, hg_lb, hg_norm_g, hg_w_out, da_w_in, da_lam, da_norm_g, da_w_out,
              nsa_w_in, nsa_cmp_pe, nsa_cmp_w1, nsa_cmp_w2, nsa_w_out, sb_w_in, sb_w_out,
              ffn_w_gate, ffn_w_up, ffn_w_down, moe_w_router, moe_w_gate, moe_w_up, moe_w_down,
              ln_g, ln_b):
    pos = jnp.arange(x.shape[1])
    h = x
    for layer in range(DEPTH_2):
        m = layer % N_MIXERS
        if m == 0:
            y = hgrn2_mixer(h, hg_w_in, hg_lb, hg_norm_g, hg_w_out, layer)
        elif m == 1:
            y = diff_attention_mixer(h, da_w_in, da_lam, da_norm_g, da_w_out, pos, layer)
        elif m == 2:
            y = nsa_mixer(h, nsa_w_in, nsa_cmp_pe, nsa_cmp_w1, nsa_cmp_w2, nsa_w_out, pos)
        else:
            y = stick_breaking_mixer(h, sb_w_in, sb_w_out)
        h = layer_norm(DEEPNORM_ALPHA * h + y.astype(h.dtype), ln_g[layer, 0], ln_b[layer, 0])
        j = layer // 2
        if layer % 2 == 0:
            y = swiglu(h, ffn_w_gate[j], ffn_w_up[j], ffn_w_down[j])
        else:
            y = moe_swiglu(h, moe_w_router[j], moe_w_gate[j], moe_w_up[j], moe_w_down[j])
        h = layer_norm(DEEPNORM_ALPHA * h + y.astype(h.dtype), ln_g[layer, 1], ln_b[layer, 1])
    return h


def setup_inputs(seed=0):
    out = dict(first_inputs(seed))
    for name, value in second_inputs(seed + 1).items():
        if name != "x":
            out[name + "_2"] = value
    return out


def reference(
    x, mem, g_mix, w_in, b_forget, g_q_moba, g_k_moba, g_q_fox, g_k_fox, g_q_mem, g_k_mem,
    g_mem, w_mem_kv, w_br_moba, w_br_fox, w_br_mem, w_out, g_ffn, w_gate, w_up, w_down,
    hg_w_in_2, hg_lb_2, hg_norm_g_2, hg_w_out_2, da_w_in_2, da_lam_2, da_norm_g_2, da_w_out_2,
    nsa_w_in_2, nsa_cmp_pe_2, nsa_cmp_w1_2, nsa_cmp_w2_2, nsa_w_out_2, sb_w_in_2, sb_w_out_2,
    ffn_w_gate_2, ffn_w_up_2, ffn_w_down_2, moe_w_router_2, moe_w_gate_2, moe_w_up_2,
    moe_w_down_2, ln_g_2, ln_b_2,
):
    x = first_block(
        x, mem, g_mix, w_in, b_forget, g_q_moba, g_k_moba, g_q_fox, g_k_fox, g_q_mem, g_k_mem,
        g_mem, w_mem_kv, w_br_moba, w_br_fox, w_br_mem, w_out, g_ffn, w_gate, w_up, w_down,
    )
    return second_block(
        x, hg_w_in_2, hg_lb_2, hg_norm_g_2, hg_w_out_2, da_w_in_2, da_lam_2, da_norm_g_2,
        da_w_out_2, nsa_w_in_2, nsa_cmp_pe_2, nsa_cmp_w1_2, nsa_cmp_w2_2, nsa_w_out_2,
        sb_w_in_2, sb_w_out_2, ffn_w_gate_2, ffn_w_up_2, ffn_w_down_2, moe_w_router_2,
        moe_w_gate_2, moe_w_up_2, moe_w_down_2, ln_g_2, ln_b_2,
    )


_drawn_inputs = setup_inputs


def setup_inputs(seed=0):
    import zlib

    import numpy as np

    out = dict(_drawn_inputs(seed))
    spreads = {}
    factors = {'g_q_moba': 3.436,
     'g_k_moba': 3.294,
     'g_q_fox': 2.888,
     'g_k_fox': 3.195,
     'g_q_mem': 7.426,
     'g_k_mem': 5.38,
     'g_mem': 3.672,
     'hg_lb_2': 8.0,
     'hg_norm_g_2': 8.0,
     'da_norm_g_2': 8.0}
    for name, (base, spread) in spreads.items():
        noise = np.random.default_rng([zlib.crc32(name.encode()), seed]).standard_normal(out[name].shape)
        drawn = base * np.exp(spread * noise) if base else spread * noise
        out[name] = jnp.asarray(drawn.astype(out[name].dtype))
    for name, factor in factors.items():
        out[name] = (out[name] * factor).astype(out[name].dtype)
    return out
```

```python
import math
from contextlib import ExitStack

import numpy as np

import concourse.bass as bass
from concourse import mybir

F32 = mybir.dt.float32
FR = mybir.dt.float32r
U16 = mybir.dt.uint16
BF16 = mybir.dt.bfloat16
U32 = mybir.dt.uint32
ALU = mybir.AluOpType
ACT = mybir.ActivationFunctionType
AX = mybir.AxisListType

D = 1024
S = 256
FF = 2816
FFE = 3584
NE = 8
NEG = -1e30
ALPHA = 4.0 ** 0.25
LAM_INIT = 0.8 - 0.6 * math.exp(-0.3)
NSLOT = 3
CAP = 128
LIM = 128

C_ID = 0
C_TRIU = 128
C_CAUS = 256
C_RM = 384
C_RD = 448
C_TRI8 = 704
C_IOTA = 768
C_LEV = 896
C_KEEP = C_LEV
C_END = 1920

V_MIX, V_MEM, V_FFN, V_LNG, V_LNB, V_QF, V_KF, V_QC, V_KC, V_LB = 0, 8, 16, 24, 56, 88, 89, 90, 91, 92
V_END = 116


def constant_table():
    c = np.zeros((128, C_END), np.float32)
    r = np.arange(128)
    c[:, C_ID:C_ID + 128] = np.eye(128)
    c[:, C_TRIU:C_TRIU + 128] = r[:, None] <= r[None, :]
    c[:, C_CAUS:C_CAUS + 128] = np.where(r[None, :] > r[:, None], NEG, 0.0)
    for i, b in enumerate((64, 32, 16, 8, 4, 2, 1)):
        same = (r[:, None] // (2 * b)) == (r[None, :] // (2 * b))
        c[:, C_LEV + 128 * i:C_LEV + 128 * i + 128] = same & (r[:, None] % (2 * b) < b) & (r[None, :] % (2 * b) >= b)
    c[:, C_LEV + 896:C_LEV + 1024] = np.eye(128)
    pos = np.arange(S, dtype=np.float32)
    inv = (1.0 / (np.float32(500000.0) ** (np.arange(8, dtype=np.float32) * np.float32(2.0) / np.float32(16)))).astype(np.float32)
    ang = (pos[:, None] * inv[None, :]).astype(np.float64)
    inv2 = (np.float32(10000.0) ** (-np.arange(32, dtype=np.float32) / np.float32(32))).astype(np.float32)
    ang2 = (pos[:, None] * inv2[None, :]).astype(np.float64)
    for t in range(2):
        a = ang[128 * t:128 * t + 128]
        c[:, C_RM + 32 * t:C_RM + 32 * t + 32] = np.concatenate([np.cos(a), np.cos(a), -np.sin(a), np.sin(a)], 1)
        a = ang2[128 * t:128 * t + 128]
        c[:, C_RD + 128 * t:C_RD + 128 * t + 128] = np.concatenate([np.cos(a), np.cos(a), -np.sin(a), np.sin(a)], 1)
    c[:, C_IOTA:C_IOTA + 128] = np.where(r < LIM, r, -999)[None, :]
    i = np.arange(8)
    c[:, C_TRI8:C_TRI8 + 64] = (i[None, :] < i[:, None]).astype(np.float32).reshape(1, 64)
    return c


class Engine:

    def __init__(self, sem, e):
        self.sem, self.e, self.n, self.seen = sem, e, 0, {}

    def wait(self, *toks):
        for t in toks:
            if t is None:
                continue
            if isinstance(t, list):
                self.wait(*t)
                continue
            s, v = t
            if self.seen.get(s.name, 0) < v:
                self.seen[s.name] = v
                if self.e is not None:
                    self.e.wait_ge(s, v)

    def go(self, f, *waits):
        self.wait(*waits)
        self.n += 1
        if self.e is not None:
            f(self.e).then_inc(self.sem, 1)
        return (self.sem, self.n)

    def raw(self, f, *waits):
        self.wait(*waits)
        if self.e is not None:
            f(self.e)

    def last(self):
        return (self.sem, self.n) if self.n else None


class DmaSem:

    def __init__(self, sem):
        self.sem, self.n = sem, 0

    def start(self, eng, out, in_, *waits):
        self.n += 16
        eng.wait(*waits)
        if eng.e is not None:
            eng.e.dma_start(out, in_).then_inc(self.sem, 16)
        return (self.sem, self.n)


def build(nc, I, table, out):
    ctx = ExitStack()
    with ctx:
        def sb(name, shape, dt=F32):
            return ctx.enter_context(nc.sbuf_tensor(name, shape, dt))

        def sem(name):
            return ctx.enter_context(nc.semaphore(name))

        ring = sb("ring", [128, NSLOT, 4096])
        H = sb("H", [128, 2, D])
        XH = sb("XH", [128, 8, S], FR)
        XL = sb("XL", [128, 8, S], FR)
        CT = sb("CT", [128, C_KEEP])
        LEVM = sb("LEVM", [128, 1024], U16)
        VS = sb("VS", [128, 256])
        VT = sb("VT", [128, 128])
        IDB = sb("IDB", [128, 128], BF16)
        CSB = sb("CSB", [128, 256], BF16)
        BC = sb("BC", [128, 2, D])
        NG = sb("NG", [128, 2, 128])
        GM = sb("GM", [128, 2, 64])
        LAMB = sb("LAMB", [128, 256])
        BFG = sb("BFG", [128, 8])
        WFG = sb("WFG", [128, 8, 8])
        WRT = sb("WRT", [128, 8, 8])
        W8 = [sb(f"W8{i}", [128, 8, 8], FR) for i in range(4)]
        CNT = sb("CNT", [1, 1], mybir.dt.int32)
        MH = sb("MH", [128, 8])
        SM = sb("SM", [128, 1024])
        WHB = [sb(f"WHB{i}", [128, 2048], FR) for i in range(2)]
        WLB = [sb(f"WLB{i}", [128, 2048], FR) for i in range(2)]

        with ExitStack() as part:
            AR1 = part.enter_context(nc.sbuf_tensor("AR1", [128, 18 * 1024], F32))
            YH = part.enter_context(nc.sbuf_tensor("YH", [128, 4, S], FR))
            YL = part.enter_context(nc.sbuf_tensor("YL", [128, 4, S], FR))
        with ExitStack() as part:
            AR2 = part.enter_context(nc.sbuf_tensor("AR2", [128, 19 * 1024], F32))
        with ExitStack() as part:
            AR3 = part.enter_context(nc.sbuf_tensor("AR3", [128, 14 * 1024 + 512], F32))
        with ExitStack() as part:
            def pt(name, shape, dt=F32):
                return part.enter_context(nc.sbuf_tensor(name, shape, dt))

            HID = pt("HID", [128, 2, 512])
            HTH = pt("HTH", [128, 2, 512], FR)
            HTL = pt("HTL", [128, 2, 512], FR)
            WHX = [pt(f"WHX{i}", [128, 2048], FR) for i in range(2)]
            WLX = [pt(f"WLX{i}", [128, 2048], FR) for i in range(2)]
            HH = pt("HH", [128, 2, D], FR)
            HL = pt("HL", [128, 2, D], FR)
            with ExitStack() as part2:
                LZ = part2.enter_context(nc.sbuf_tensor("LZ", [128, 2, D], F32))
                LT = part2.enter_context(nc.sbuf_tensor("LT", [128, 2, 512], F32))
            EH = pt("EH", [128, 8, CAP], FR)
            EL = pt("EL", [128, 8, CAP], FR)
            ZH = pt("ZH", [128, D], FR)
            ZL = pt("ZL", [128, D], FR)
            PO = pt("PO", [128, 2, CAP], FR)
            POT = pt("POT", [128, 2, 128], FR)
        PS = [ctx.enter_context(nc.psum_tensor(f"PS{i}", [128, 512], F32)) for i in range(8)]

        sems = {n: sem(n) for n in ["s_pe", "s_dve", "s_act", "s_pool", "s_sp", "s_c", "s_x", "s_v", "s_b", "s_m", "s_ln", "s_out", "s_lv", "o_pe", "o_dve", "o_act", "o_w0", "o_w1", "o_w2"]
                + [f"s_w{i}" for i in range(NSLOT)]}

        def program(name_, e):
            pe, dve, act, pool, sp = (Engine(sems["s_" + n], e if n == name_ else None) for n in ("pe", "dve", "act", "pool", "sp"))

            ident = CT[:, C_ID:C_ID + 128]
            sm_at = [0]
            area = [AR1]

            def small(n):
                a = sm_at[0]
                if a + n > 512:
                    a = 0
                sm_at[0] = a + n
                return SM[:, a:a + n]

            def arena(at, n):
                return area[0][:, at:at + n]

            def join():
                toks = [e.last() for e in (pe, dve, act, pool)]
                for x in (pe, dve, act, pool):
                    x.wait(*toks)
                return toks

            def cols(name, c0, c1):
                return (name, c0, I[name].rearrange("(t p) n -> p t n", p=128)[:, :, c0:c1], 8, c1 - c0)

            def rows(name, t0, t1):
                return (name, t0, I[name].rearrange("(t p) n -> p t n", p=128)[:, t0:t1, :], t1 - t0, D)

            def ffn_list(jobs, n):
                ls, held = [], []
                for g, u, d in jobs:
                    for c in range(0, n, 512):
                        m = min(512, n - c)
                        ls += [cols(g, c, c + m), cols(u, c, c + m)] + held
                        held = [rows(d, c // 128, (c + m) // 128)]
                return ls + held

            WL = [cols("w_mem_kv", 0, 512), cols("w_mem_kv", 512, 1024)]
            WL += [cols("w_in", c, c + 512) for c in (3080, 0, 512, 1024, 5640, 6152)] + [rows("w_br_mem", 0, 4)]
            WL += [cols("w_in", c, c + 512) for c in (1536, 2048, 2560, 3592, 4104)] + [rows("w_br_moba", 0, 4)]
            WL += [cols("w_in", c, c + 512) for c in (4616, 5128)] + [rows("w_br_fox", 0, 4)]
            WL += [cols("w_out", 0, 512), cols("w_out", 512, 1024)]
            WL += ffn_list([("w_gate", "w_up", "w_down")], FF)
            WL += [cols("hg_w_in_2", c, c + 512) for c in (1024, 1536, 0, 512, 2048, 2560, 3072, 3584)]
            WL += [cols("hg_w_out_2", 0, 512), cols("hg_w_out_2", 512, 1024)]
            WL += ffn_list([("ffn_w_gate_2", "ffn_w_up_2", "ffn_w_down_2")], FF)
            WL += [cols("da_w_in_2", c, c + 512) for c in (0, 1024, 2048, 512, 1536, 2560)]
            WL += [cols("da_w_out_2", 0, 512), cols("da_w_out_2", 512, 1024)]
            WL += ffn_list([(f"moe_w_gate_2.{e}", f"moe_w_up_2.{e}", f"moe_w_down_2.{e}") for e in range(NE)], FFE)

            slot_sem = [DmaSem(sems[f"s_w{i}"]) for i in range(NSLOT)]
            arrived = {}

            def load(i, *waits):
                if i < len(WL):
                    _, _, src, t, n = WL[i]
                    dst = ring[:, i % NSLOT, 0:t * n].rearrange("p (t n) -> p t n", t=t)
                    arrived[i] = slot_sem[i % NSLOT].start(sp, dst, src, *waits)

            groups = {(0,): (0, 0), (1,): (0, 1024), (2,): (1, 0), (3,): (1, 1024), (0, 1): (0, 0), (2, 3): (1, 0), (4,): (2, 0), (5,): (3, 0)}
            store = [(WHB[i], WLB[i]) for i in range(2)] + [(WHX[i], WLX[i]) for i in range(2)]
            slot_free = [[] for _ in range(6)]
            slot_turn = [0] * 6
            extra_on = [False]
            keep_low = [0]
            piece_at = [0, 0]
            piece = {}
            low = []
            turn_n = [0]

            def in_ffn(i):
                return "gate" in WL[i][0] or "up" in WL[i][0] or "down" in WL[i][0]

            PIECES = [(i, j, 2 if in_ffn(i) else 4) for i in range(len(WL)) for j in range(2 if in_ffn(i) else 4)]

            def queue_low(keep):
                while len(low) > keep:
                    k, hi, lo, src, t_hi, t_w, fr = low.pop(0)
                    t = dve.go(lambda e: e.tensor_tensor(lo, src, hi.bitcast(F32), ALU.subtract), t_hi, t_w, fr)
                    piece[k][3].append(t)
                    i, j, np_ = PIECES[k]
                    if j == np_ - 1:
                        load(i + NSLOT, t, t_hi)

            def split_ahead():
                while piece_at[0] < len(PIECES):
                    k = piece_at[0]
                    i, j, np_ = PIECES[k]
                    if i not in arrived:
                        queue_low(0)
                        if i not in arrived:
                            return
                    able = ((0, 1), (2, 3)) if np_ == 2 else ((0,), (1,), (2,), (3,))
                    if np_ == 2 and extra_on[0]:
                        able += ((4,), (5,))
                    able = [g for g in able if all(slot_free[x] is not None for x in g)]
                    if not able:
                        return
                    g = min(able, key=lambda g: max(slot_turn[x] for x in g))
                    turn_n[0] += 1
                    fr = []
                    for x in g:
                        slot_turn[x] = turn_n[0]
                        fr = fr + slot_free[x]
                        slot_free[x] = None
                    _, _, _, t, n = WL[i]
                    m = t * n // np_
                    src = ring[:, i % NSLOT, j * m:j * m + m]
                    b, at = groups[g]
                    hi, lo = (x[:, at:at + m] for x in store[b])
                    t_hi = act.go(lambda e: e.activation(hi, src, ACT.Copy), arrived[i], fr)
                    piece[k] = (g, hi, lo, [t_hi])
                    low.append((k, hi, lo, src, t_hi, arrived[i], fr))
                    piece_at[0] += 1
                    queue_low(1 if extra_on[0] else 0)

            def parts():
                return PIECES[piece_at[1]][2]

            def take(name, c0):
                split_ahead()
                k = piece_at[1]
                piece_at[1] += 1
                if len(piece[k][3]) < 2:
                    queue_low(0)
                i, j, np_ = PIECES[k]
                assert WL[i][:2] == (name, c0), (WL[i][:2], name, c0)
                g, hi, lo, toks = piece[k]
                hi, lo = (x.rearrange("p (t n) -> p t n", t=WL[i][3] // np_) for x in (hi, lo))
                return hi, lo, toks, g

            def taken(g, tok):
                for x in g:
                    slot_free[x] = [tok]
                split_ahead()

            new, active = [], []
            steps = [None]

            def advance():
                for u in list(active):
                    u[1].pop(0)()
                    if not u[1]:
                        active.remove(u)

            def begin():
                u = new.pop(0)
                u[1].pop(0)()
                if u[1]:
                    active.append(u)

            def unit_hook(j):
                if j % 2:
                    advance()
                    if new:
                        n = len(active)
                        begin()
                        if new and len(active) == n:
                            begin()

            def step_hook(j):
                if j % 2 == 0 and steps[0] is not None and next(steps[0], "end") == "end":
                    steps[0] = None

            def drain(*banks):
                while any(not banks or u[0] in banks for u in new + active):
                    advance()
                    if new and any(not banks or u[0] in banks for u in new):
                        begin()

            def drain_steps():
                while steps[0] is not None:
                    if next(steps[0], "end") == "end":
                        steps[0] = None
                    advance()

            s_c, s_x, s_v, s_b, s_m, s_ln, s_o, s_lv = (DmaSem(sems["s_" + n]) for n in ("c", "x", "v", "b", "m", "ln", "out", "lv"))
            MEMR = arena(0, 2048).rearrange("p (a n) -> p a n", a=2)
            t_m = s_m.start(act, MEMR, I["mem"].rearrange("(a p) n -> p a n", p=128))
            z_vs = pool.go(lambda e: e.memset(VS[:, 0:128], 0.0))
            t_c = s_c.start(act, CT[:, :], table[:, 0:C_KEEP])
            for at, name, n in ((V_MIX, "g_mix", 8), (V_MEM, "g_mem", 8), (V_FFN, "g_ffn", 8), (V_LNG, "ln_g_2", 32),
                                (V_LNB, "ln_b_2", 32), (V_LB, "hg_lb_2", 24), (V_QC, "g_q_mem", 1), (V_KC, "g_k_mem", 1)):
                t_v = s_v.start(act, VS[at:at + n, 0:128], I[name].rearrange("(a b) -> a b", b=128), z_vs)
            for at, name in ((V_QF, "g_q_fox"), (V_KF, "g_k_fox")):
                for k in range(2):
                    t_v = s_v.start(act, VS[at:at + 1, 64 * k:64 * k + 64], I[name].rearrange("(a b) -> a b", a=1), z_vs)
            t_x = s_x.start(act, H[:, :, :], I["x"].rearrange("(a p) n -> p a n", p=128))
            load(0, t_m)
            for i in range(1, NSLOT):
                load(i, t_v)
            LEVS = arena(4096, 1024)
            t_c2 = s_lv.start(sp, LEVS, table[:, C_KEEP:C_END])

            def bcast(ap, n):
                return ap.rearrange("(a b) -> a b", a=1).to_broadcast([128, n])

            for dst, name, n in ((GM[:, 0, :], "g_q_moba", 64), (GM[:, 1, :], "g_k_moba", 64), (NG[:, 0, :], "hg_norm_g_2", 128),
                                 (NG[:, 1, :], "da_norm_g_2", 128), (LAMB[:, :], "da_lam_2", 256), (BFG[:, :], "b_forget", 8)):
                t_b = s_b.start(pool, dst, bcast(I[name], n))
            t_b = s_b.start(pool, WFG[:, :, :], I["w_in"].rearrange("(t p) n -> p t n", p=128)[:, :, 3072:3080])
            t_b = s_b.start(pool, WRT[:, :, :], I["moe_w_router_2"].rearrange("(t p) n -> p t n", p=128))
            t_mh = pool.go(lambda e: e.memset(MH[:, :], -0.5))

            t_idb = dve.go(lambda e: e.tensor_copy(IDB[:, :], ident), t_c)
            t_csb = dve.go(lambda e: e.memset(CSB[:, 0:128], 0.0))
            t_csb = dve.go(lambda e: e.tensor_copy(CSB[:, 128:256], CT[:, C_CAUS:C_CAUS + 128]), t_c)

            for i, w in enumerate((WFG, WRT)):
                t = dve.go(lambda e: e.tensor_copy(W8[2 * i][:, :, :], w[:, :, :]), t_b)
                t_w8 = dve.go(lambda e: e.tensor_tensor(W8[2 * i + 1][:, :, :], w[:, :, :], W8[2 * i][:, :, :].bitcast(F32), ALU.subtract), t)

            free = [[] for _ in range(8)]

            t = pe.go(lambda e: e.transpose(PS[0][:, 0:128], VS[:, 0:128], ident), t_v, t_c)
            t_vt = act.go(lambda e: e.activation(VT[:, :], PS[0][:, 0:128], ACT.Copy), t)
            free[0] = [t_vt]

            def rsqrt(x, n, scale, eps, *waits):
                v, r = small(n), small(n)
                t = dve.go(lambda e: e.tensor_scalar(v, x, scale, eps, ALU.mult, ALU.add), *waits)
                t = pool.go(lambda e: e.tensor_tensor(r, v, MH[:, 0:n], ALU.pow), t, t_mh)
                return r, t

            def mm3(o, xh, xl, wh, wl, start, stop, mark):
                pe.raw(lambda e: e.matmul(o, xh, wh, start=start, stop=False))
                pe.raw(lambda e: e.matmul(o, xh, wl, start=False, stop=False))
                f = lambda e: e.matmul(o, xl, wh, start=False, stop=stop)
                return pe.go(f) if mark else pe.raw(f)

            def token_mm(banks, name, c0, xh, xl, n, ready, between=None, after=None):
                out_ = []
                np_ = parts()
                if np_ == 4:
                    drain(*banks)
                for h2 in range(np_):
                    hi, lo, t_w, p = take(name, c0)
                    nk = hi.shape[1]
                    for tt, b in enumerate(banks):
                        pe.wait(*t_w, *ready)
                        if h2 == 0:
                            pe.wait(free[b])
                        for j in range(nk):
                            kt = nk * h2 + j
                            xs = slice(128 * tt, 128 * tt + 128)
                            t = mm3(PS[b][:, 0:n], xh[:, kt, xs], xl[:, kt, xs], hi[:, j, 0:n], lo[:, j, 0:n], h2 == 0 and j == 0,
                                    h2 == np_ - 1 and j == nk - 1, j == nk - 1)
                        if h2 == np_ - 1:
                            out_.append(t)
                    if h2 == np_ - 1 and after is not None:
                        after(out_)
                    if np_ == 4:
                        unit_hook(h2)
                    taken(p, t)
                    if np_ == 4:
                        step_hook(h2)
                    if between is not None and h2 == 0:
                        between()
                return out_

            def narrow_mm(bank, tt, i, *waits):
                pe.wait(free[bank], t_w8, *waits)
                for kt in range(8):
                    xs = slice(128 * tt, 128 * tt + 128)
                    t = mm3(PS[bank][:, 0:8], XH[:, kt, xs], XL[:, kt, xs], W8[2 * i][:, kt, :], W8[2 * i + 1][:, kt, :], kt == 0, kt == 7, kt == 7)
                return t

            def to_columns(src, ready, hi, lo, scale, shift, banks=(0, 1, 2, 3), tmp=None):
                done = []
                tfr = [[], []]
                for j in range(4):
                    b = banks[j % len(banks)]
                    pe.wait(free[b], t_c, *ready)
                    for a in range(2):
                        for tt in range(2):
                            kt = 2 * j + a
                            o = PS[b][:, 256 * a + 128 * tt:256 * a + 128 * tt + 128]
                            f = lambda e: e.transpose(o, src[:, tt, 128 * kt:128 * kt + 128], ident)
                            if a == 1 and tt == 1:
                                t = pe.go(f)
                            else:
                                pe.raw(f)
                    ps = PS[b][:, :].rearrange("p (a n) -> p a n", a=2)
                    h2, l2 = hi[:, 2 * j:2 * j + 2, :], lo[:, 2 * j:2 * j + 2, :]
                    w = [pe_hold[0]]
                    if shift is not None:
                        tm = tmp[:, j % 2, :].rearrange("p (a n) -> p a n", a=2)
                        tk = [dve.go(lambda e: e.tensor_scalar(tm[:, a, :], ps[:, a, :], scale[:, 2 * j + a:2 * j + a + 1], shift[:, 2 * j + a:2 * j + a + 1], ALU.mult, ALU.add),
                                     t, t_vt, tfr[j % 2]) for a in range(2)]
                        free[b] = tk
                        t1 = act.go(lambda e: e.activation(h2, tm, ACT.Copy), *tk, *w)
                        t2 = dve.go(lambda e: e.tensor_tensor(l2, tm, h2.bitcast(F32), ALU.subtract), t1, *w)
                        tfr[j % 2] = [t1, t2]
                        done += [t1, t2]
                    elif scale is not None:
                        t1 = [act.go(lambda e: e.activation(h2[:, a, :], ps[:, a, :], ACT.Copy, scale=scale[:, 2 * j + a:2 * j + a + 1]), t, t_vt, *w) for a in range(2)]
                        t2 = [dve.go(lambda e: e.scalar_tensor_tensor(out=l2[:, a, :], in0=ps[:, a, :], scalar=scale[:, 2 * j + a:2 * j + a + 1], in1=h2[:, a, :].bitcast(F32),
                                                                      op0=ALU.mult, op1=ALU.subtract), *t1, t_vt, *w) for a in range(2)]
                        free[b] = t1 + t2
                        done += t1 + t2
                    else:
                        t1 = act.go(lambda e: e.activation(h2, ps, ACT.Copy), t, *w)
                        t2 = dve.go(lambda e: e.tensor_tensor(l2, ps, h2.bitcast(F32), ALU.subtract), t1, *w)
                        free[b] = [t1, t2]
                        done += [t1, t2]
                return done

            pe_hold = [None]

            def hold():
                pe_hold[0] = pe.last()

            def rms_columns(src, tmp, hi, lo, gain, *waits):
                ss = small(2)
                tok = []
                for tt in range(2):
                    tok.append(act.go(lambda e, tt=tt: e.activation(tmp[:, tt, :], src[:, tt, :], ACT.Square, accum_out=ss[:, tt:tt + 1]), *waits))
                r, t = rsqrt(ss, 2, 1.0 / D, 1e-6, *tok)
                z = [dve.go(lambda e, tt=tt: e.tensor_scalar(tmp[:, tt, :], src[:, tt, :], r[:, tt:tt + 1], None, ALU.mult), t, *waits) for tt in range(2)]
                return z, lambda: to_columns(tmp, z, hi, lo, gain, None)

            tmpA = arena(6144, 2048).rearrange("p (a n) -> p a n", a=2)
            tmpB = arena(2048, 2048).rearrange("p (a n) -> p a n", a=2)
            _, mem_columns = rms_columns(MEMR, tmpB, XH, XL, VT[:, V_MEM:V_MEM + 8], t_m)
            mt = mem_columns()
            _, x_columns = rms_columns(H, tmpA, XH, XL, VT[:, V_MIX:V_MIX + 8], t_x)

            def ar(at, a, n):
                return arena(at, a * n).rearrange("p (a n) -> p a n", a=a)

            GATE = [ar(2048, 2, D), ar(0, 2, D), ar(0, 2, D)]
            MRG = ar(4096, 2, D)
            QT = {n: ar(6144 + 1024 * i, 4, S) for i, n in enumerate(("qm", "km", "qf", "kf", "qc", "kc"))}
            VR = {n: ar(12288 + 1024 * i, 2, 512) for i, n in enumerate(("vm", "vf", "vc"))}
            XN = ar(15360, 2, 512)
            SQ = ar(16384, 2, 512)
            PB = XN
            PTB = ar(17408, 2, 512)
            YR = BC[:, :, 0:512]
            xn_free, sq_free = [[], []], [[], []]
            unit = [0]
            tr_bank = 3
            col_done = {n: [] for n in QT}
            row_done = {n: [] for n in VR}

            def qk_unit(kind, nh, bank, tt, t_mm, gain_col, gain_row):
                dh = 512 // nh
                i = unit[0] % 2
                unit[0] += 1
                sq, xn = SQ[:, i, :], XN[:, i, :]
                ss = small(nh)
                t = act.go(lambda e: e.activation(sq, PS[bank][:, :], ACT.Square), t_mm, sq_free[i])
                t = dve.go(lambda e: e.tensor_reduce(ss, sq.rearrange("p (h d) -> p h d", h=nh), AX.X, ALU.add), t)
                r, t = rsqrt(ss, nh, 1.0 / dh, 1e-6, t)
                yield
                rb = r.unsqueeze(2).to_broadcast([128, nh, dh])
                t = dve.go(lambda e: e.tensor_tensor(xn.rearrange("p (h d) -> p h d", h=nh), PS[bank][:, :].rearrange("p (h d) -> p h d", h=nh), rb, ALU.mult),
                           t, xn_free[i])
                free[bank] = [t]
                sq_free[i] = [t]
                if gain_row is not None:
                    g = gain_row.unsqueeze(1).to_broadcast([128, 8, 64])
                    x3 = xn.rearrange("p (h d) -> p h d", h=8)
                    t = dve.go(lambda e: e.tensor_tensor(x3, x3, g, ALU.mult), t, t_b)
                    cs = CT[:, C_RM + 32 * tt:C_RM + 32 * tt + 16].unsqueeze(1).to_broadcast([128, 8, 16])
                    ns = CT[:, C_RM + 32 * tt + 16:C_RM + 32 * tt + 24].unsqueeze(1).to_broadcast([128, 8, 8])
                    sn = CT[:, C_RM + 32 * tt + 24:C_RM + 32 * tt + 32].unsqueeze(1).to_broadcast([128, 8, 8])
                    u = sq[:, 0:128].rearrange("p (h d) -> p h d", h=8)
                    w = sq[:, 128:256].rearrange("p (h d) -> p h d", h=8)
                    t1 = pool.go(lambda e: e.tensor_tensor(u[:, :, 0:8], x3[:, :, 8:16], ns, ALU.mult), t, t_c)
                    t1 = pool.go(lambda e: e.tensor_tensor(u[:, :, 8:16], x3[:, :, 0:8], sn, ALU.mult), t)
                    t2 = pool.go(lambda e: e.tensor_tensor(w, x3[:, :, 0:16], cs, ALU.mult), t)
                    t = pool.go(lambda e: e.tensor_tensor(x3[:, :, 0:16], w, u, ALU.add), t1, t2)
                    sq_free[i] = [t]
                yield
                b = tr_bank
                pe.wait(free[b], t, t_c)
                for j in range(4):
                    f = lambda e, j=j: e.transpose(PS[b][:, 128 * j:128 * j + 128], xn[:, 128 * j:128 * j + 128], ident)
                    if j < 3:
                        pe.raw(f)
                    else:
                        t = pe.go(f)
                xn_free[i] = [t]
                dst = QT[kind][:, :, 128 * tt:128 * tt + 128]
                src = PS[b][:, :].rearrange("p (j n) -> p j n", j=4)
                if gain_col is None:
                    t = act.go(lambda e: e.activation(dst, src, ACT.Copy), t)
                else:
                    t = act.go(lambda e: e.activation(dst, src, ACT.Copy, scale=VT[:, gain_col:gain_col + 1]), t, t_vt)
                free[b] = [t]
                col_done[kind].append(t)

            pj = [0]

            def pj_bank(banks=(0, 1, 2, 3)):
                b = banks[pj[0] % len(banks)]
                pj[0] += 1
                return b

            def two_tiles(name, c0, ready, then, bset=((0, 1), (6, 7))):
                bs = bset[pj[0] % 2]
                pj[0] += 1

                def after(toks):
                    for tt in range(2):
                        new.append([bs[tt], then(bs[tt], tt, toks[tt])])

                token_mm(bs, name, c0, XH, XL, 512, ready, after=after)

            def stages(n, gen):
                return [lambda: next(gen, None)] * n

            def v_unit(kind):
                def f(b, tt, t):
                    def s0():
                        t1 = act.go(lambda e: e.activation(VR[kind][:, tt, :], PS[b][:, :], ACT.Copy), t)
                        free[b] = [t1]
                        row_done[kind].append(t1)
                    return [s0]
                return f

            def q_unit(kind, nh, gc, gr):
                return lambda b, tt, t: stages(3, qk_unit(kind, nh, b, tt, t, gc, gr))

            def forget_unit():
                for tt in range(2):
                    t = narrow_mm(tr_bank, tt, 0, *xt)
                    z, a1, a2, a3 = small(8), small(8), small(8), small(8)
                    lg = SM[:, 960 + 8 * tt:968 + 8 * tt]
                    t = dve.go(lambda e: e.tensor_tensor(z, PS[tr_bank][:, 0:8], BFG[:, :], ALU.add), t, t_b)
                    free[tr_bank] = [t]
                    tn = dve.go(lambda e: e.tensor_scalar(a1, z, 0.0, None, ALU.min), t)
                    t = act.go(lambda e: e.activation(a2, z, ACT.Abs), t)
                    t = act.go(lambda e: e.activation(a2, a2, ACT.Exp, scale=-1.0), t)
                    t = act.go(lambda e: e.activation(a3, a2, ACT.Ln, bias=1.0), t)
                    LG.append((lg, dve.go(lambda e, lg=lg: e.tensor_tensor(lg, a1, a3, ALU.subtract), t, tn)))
                    yield
                b = tr_bank
                pe.wait(free[b], LG[0][1], LG[1][1], t_one, t_c)
                pe.raw(lambda e: e.matmul(PS[b][0:8, 0:128], LG[0][0], triu, start=True, stop=True))
                pe.raw(lambda e: e.matmul(PS[b][0:8, 128:256], LG[0][0], ONE, start=True, stop=False))
                pe.raw(lambda e: e.matmul(PS[b][0:8, 128:256], LG[1][0], triu, start=False, stop=True))
                pe.raw(lambda e: e.matmul(PS[b][:, 256:264], triu, LG[0][0], start=True, stop=True))
                pe.raw(lambda e: e.matmul(PS[b][:, 264:272], ONE, LG[0][0], start=True, stop=False))
                t = pe.go(lambda e: e.matmul(PS[b][:, 264:272], triu, LG[1][0], start=False, stop=True))
                cum["n"] = dve.go(lambda e: e.tensor_scalar(NCT, PS[b][0:8, 0:256], -8.0, None, ALU.mult), t)
                cum["r"] = dve.go(lambda e: e.tensor_copy(CUMR, PS[b][:, 256:272].rearrange("p (a h) -> p a h", a=2)), t)
                free[b] = [cum["n"], cum["r"]]

            LG, cum = [], {}
            triu = CT[:, C_TRIU:C_TRIU + 128]
            CUMR = SM[:, 980:996].rearrange("p (a h) -> p a h", a=2)
            NCT = VS[0:8, 0:256]
            ONE = arena(17408, 128)
            t_one = pool.go(lambda e: e.memset(ONE, 1.0))
            SEL = ar(16384, 8, 128)[0:8]

            gate_tok = {}

            gate_wait = [None]

            def gate_unit(i, c):
                def f(b, tt, t):
                    g = GATE[i][:, tt, 512 * c:512 * c + 512]
                    def s0():
                        t1 = act.go(lambda e: e.activation(g, PS[b][:, :], ACT.Exp, scale=-1.0), t, gate_wait[0])
                        free[b] = [t1]
                        gate_tok[(i, tt, c)] = pool.go(lambda e: e.tensor_scalar(g, g, 1.0, 0.0, ALU.add, ALU.add), t1)
                    def s1():
                        gate_tok[(i, tt, c)] = dve.go(lambda e: e.reciprocal(g, g), gate_tok[(i, tt, c)])
                    return [s0, s1]
                return f

            def gate(i, c):
                two_tiles("w_in", 3592 + 1024 * i + 512 * c, xt, gate_unit(i, c))

            m_tok = {}

            def branch(i, name):
                bs = {(0, 0): 0, (0, 1): 1, (1, 0): 6, (1, 1): 7}
                drain(0, 1, 6, 7)
                for h2 in range(4):
                    hi, lo, t_w, p = take(name, 0)
                    for tt in range(2):
                        for c in range(2):
                            b = bs[(tt, c)]
                            pe.wait(*t_w, yt_tok["y"])
                            if h2 == 0:
                                pe.wait(free[b])
                            xs = slice(128 * tt, 128 * tt + 128)
                            t = mm3(PS[b][:, :], YH[:, h2, xs], YL[:, h2, xs], hi[:, 0, 512 * c:512 * c + 512], lo[:, 0, 512 * c:512 * c + 512], h2 == 0, h2 == 3, True)
                            if h2 == 3:
                                g = GATE[i][:, tt, 512 * c:512 * c + 512]
                                m = MRG[:, tt, 512 * c:512 * c + 512]
                                if (tt, c) not in m_tok:
                                    t1 = dve.go(lambda e: e.tensor_tensor(m, PS[b][:, :], g, ALU.mult), t, gate_tok[(i, tt, c)], t_lev)
                                    m_tok[(tt, c)] = t1
                                else:
                                    t1 = dve.go(lambda e: e.tensor_tensor(g, PS[b][:, :], g, ALU.mult), t, gate_tok[(i, tt, c)])
                                    m_tok[(tt, c)] = pool.go(lambda e: e.tensor_tensor(m, m, g, ALU.add), t1, m_tok[(tt, c)])
                                free[b] = [t1]
                    unit_hook(h2)
                    taken(p, t)
                    step_hook(h2)
                yt_tok["read"] = t

            def blocks(causal):
                return [(0, 0, 1), (1, 0, 1), (1, 1, 1)] if causal else [(0, 0, 1), (0, 1, 1), (1, 0, 1), (1, 1, 1)]

            def attention(nh, causal, scores, values, comps, weight, out_banks, dv, PBs, PTs, sbank=(2,), tbank=(3,), free_in=(), can=lambda step: True):
                k0 = 128 if causal else 256
                width = k0 + 256
                nblk = 3 if causal else 4
                blk = [(0, 0), (1, 0), (1, 1)] if causal else [(0, 0), (0, 1), (1, 0), (1, 1)]
                ptok, pfree = {}, [list(free_in) for _ in PBs]
                ttok, tfree = {}, [list(free_in) for _ in PTs]
                stat = {}
                n = 0
                for step in range(nh + 2):
                    while not can(step):
                        yield
                    if 1 <= step <= nh:
                        h = step - 1
                        p, slot, ready = weight["combine"](h, stat[h], k0, width)
                        tb = tbank[h % len(tbank)]
                        pe.wait(free[tb], ready)
                        for j in range(nblk):
                            f = lambda e, j=j, p=p, tb=tb: e.transpose(PS[tb][:, 128 * j:128 * j + 128], p[:, 128 * j:128 * j + 128], ident)
                            if j < nblk - 1:
                                pe.raw(f)
                            else:
                                t = pe.go(f)
                        for (_, sl, _, _) in stat[h]:
                            pfree[sl] = [t]
                        pt = PTs[h % 2]
                        t = act.go(lambda e, pt=pt, tb=tb: e.activation(pt[:, 0:width], PS[tb][:, 0:width], ACT.Copy), t, tfree[h % 2])
                        free[tb] = [t]
                        ttok[h] = t
                    if step >= 2:
                        h = step - 2
                        pt = PTs[h % 2]
                        per = 512 // dv
                        ob = out_banks[h // per]
                        co = dv * (h % per)
                        if h % per == 0:
                            pe.wait(free[ob[0]], free[ob[1]])
                        pe.wait(ttok[h])
                        for j, (q, k) in enumerate(blk):
                            last = (j == nblk - 1)
                            v = values(h, k)
                            f = lambda e: e.matmul(
                                PS[ob[q]][:, co:co + dv], pt[:, 128 * j:128 * j + 128], v, start=(k == 0),
                                stop=(k == 1 or (causal and q == 0)))
                            if last:
                                t = pe.go(f)
                            else:
                                pe.raw(f)
                        tfree[h % 2] = [t]
                        if h % per == per - 1:
                            weight["done"](h // per, ob, t)
                    if step < nh:
                        h = step
                        p_list = []
                        for c in range(comps):
                            sbk = sbank[n % len(sbank)]
                            t = scores(h, c, sbk)
                            mx, rs = small(2), SM[:, 512 + 32 * (h % 8) + 2 * c:512 + 32 * (h % 8) + 2 * c + 2]
                            nm = small(2)
                            p = PBs[n % len(PBs)]
                            pf = pfree[n % len(PBs)]
                            t0 = dve.go(lambda e, mx=mx, sbk=sbk: e.tensor_reduce(mx[:, 0:1], PS[sbk][:, 0:k0], AX.X, ALU.max), t)
                            t1 = dve.go(lambda e, mx=mx, sbk=sbk: e.tensor_reduce(mx[:, 1:2], PS[sbk][:, k0:width], AX.X, ALU.max), t)
                            nm, scale, t0 = weight["bias"](h, mx, nm, t0, t1)
                            ta = []
                            for q, (a0, a1) in enumerate(((0, k0), (k0, width))):
                                ta.append(act.go(lambda e, p=p, a0=a0, a1=a1, sbk=sbk, nm=nm, rs=rs, q=q: e.activation(
                                    p[:, a0:a1], PS[sbk][:, a0:a1], ACT.Exp, bias=nm[:, q:q + 1], scale=scale, accum_out=rs[:, q:q + 1]), t0, pf))
                            free[sbk] = ta
                            p_list.append((p, n % len(PBs), ta, rs))
                            n += 1
                        stat[h] = p_list
                    yield

            def scaled_bias(scale):
                def f(h, mx, nm, t0, t1):
                    t = dve.go(lambda e: e.tensor_scalar(nm, mx, -scale, None, ALU.mult), t0, t1)
                    return nm, scale, t
                return f

            def keep_p(h, st, k0, width):
                p, slot, ta, rs = st[0]
                return p, slot, ta

            yt_tok = {}

            def head_scores(qk, kk, extra=None):
                def f(h, c, bank):
                    o, j = 64 * (h % 2), h // 2
                    q, k = QT[qk], QT[kk]
                    pe.wait(free[bank], col_done[qk], col_done[kk], t_idb, t_csb)
                    for a, b_, qt, n in ((0, 128, 0, 128), (128, 384, 1, 256)):
                        pe.raw(lambda e, a=a, b_=b_, qt=qt, n=n: e.matmul(PS[bank][:, a:b_], q[o:o + 64, j, 128 * qt:128 * qt + 128], k[o:o + 64, j, 0:n], start=True, stop=False))
                        if extra is not None:
                            extra(h, bank, a, b_, n)
                        g = lambda e: e.matmul(PS[bank][:, a:b_], IDB[:, :], CSB[:, 256 - n:256], start=False, stop=True)
                        if a:
                            t = pe.go(g)
                        else:
                            pe.raw(g)
                    return t
                return f

            def fox_extra(h, bank, a, b_, n):
                pe.wait(cum["sel"], cum["n"])
                pe.raw(lambda e: e.matmul(PS[bank][:, a:b_], SEL[:, h, :], NCT[:, 0:n], start=False, stop=False))

            def branch_done(i):
                def f(g, ob, t):
                    nh = 8 if i < 2 else 4
                    dh = 512 // nh
                    ri, rr = small(16), small(16)
                    rv = SM[:, 512:768].rearrange("p (h x) -> p h x", x=32)[:, 0:nh, 0:2]
                    rq = ri[:, 0:2 * nh].rearrange("p (h q) -> p h q", h=nh)
                    t0 = dve.go(lambda e: e.reciprocal(rq, rv), t)
                    tk = []
                    for q in range(2):
                        rb = rq[:, :, q:q + 1].to_broadcast([128, nh, dh])
                        tk.append(dve.go(lambda e, q=q, rb=rb: e.tensor_tensor(YR[:, q, :].rearrange("p (h d) -> p h d", h=nh), PS[ob[q]][:, :].rearrange("p (h d) -> p h d", h=nh), rb, ALU.mult), t0, yt_tok.get("yr")))
                        free[ob[q]] = [tk[-1]]
                    tr = []
                    ev = []
                    for half in range(2):
                        b = (2, 3)[half]
                        pe.wait(free[b], tk)
                        for a in range(2):
                            for tt in range(2):
                                j = 2 * half + a
                                f_ = lambda e, b=b, a=a, tt=tt, j=j: e.transpose(PS[b][:, 256 * a + 128 * tt:256 * a + 128 * tt + 128], YR[:, tt, 128 * j:128 * j + 128], ident)
                                if a and tt:
                                    t = pe.go(f_)
                                else:
                                    pe.raw(f_)
                        src = PS[b][:, :].rearrange("p (a n) -> p a n", a=2)
                        h2, l2 = YH[:, 2 * half:2 * half + 2, :], YL[:, 2 * half:2 * half + 2, :]
                        t1 = act.go(lambda e: e.activation(h2, src, ACT.Copy), t, yt_tok.get("read"))
                        t2 = dve.go(lambda e: e.tensor_tensor(l2, src, h2.bitcast(F32), ALU.subtract), t1)
                        free[b] = [t1, t2]
                        ev += [t1, t2]
                    yt_tok["yr"] = t
                    yt_tok["y"] = ev
                return f

            def fox_bias(h, mx, nm, t0, t1):
                cq = CUMR[:, :, h]
                w = small(2)
                t = dve.go(lambda e: e.scalar_tensor_tensor(out=w, in0=mx, scalar=0.125, in1=cq, op0=ALU.mult, op1=ALU.add), t0, t1, cum["r"])
                t = dve.go(lambda e: e.tensor_tensor(nm, cq, w, ALU.subtract), t)
                return nm, 0.125, t

            def mem_scores(h, c, bank):
                pe.wait(free[bank], col_done["qc"], col_done["kc"])
                for qt in range(2):
                    f = lambda e, qt=qt: e.matmul(PS[bank][:, 256 * qt:256 * qt + 256], QT["qc"][:, h, 128 * qt:128 * qt + 128], QT["kc"][:, h, :], start=True, stop=True)
                    if qt:
                        t = pe.go(f)
                    else:
                        pe.raw(f)
                return t

            def values(kind, dh):
                def f(h, k):
                    pe.wait(row_done[kind])
                    return VR[kind][:, k, dh * h:dh * h + dh]
                return f

            two_tiles("w_mem_kv", 0, mt, q_unit("kc", 4, V_KC, None))
            two_tiles("w_mem_kv", 512, mt, v_unit("vc"))
            hold()
            xt = x_columns()
            t_lev = pool.go(lambda e: e.tensor_copy(LEVM[:, :], LEVS), t_c2)
            two_tiles("w_in", 3080, xt, q_unit("qc", 4, V_QC, None))
            two_tiles("w_in", 0, xt, q_unit("qm", 8, None, GM[:, 0, :]))
            PM, PMT = ar(2048, 2, 512), ar(3072, 2, 512)
            PMs, PMTs = [PM[:, 0, :], PM[:, 1, :]], [PMT[:, 0, :], PMT[:, 1, :]]
            steps[0] = attention(4, False, mem_scores, values("vc", 128), 1,
                                 dict(bias=scaled_bias(128.0 ** -0.5), combine=keep_p, done=branch_done(2)), [(4, 5)], 128, PMs, PMTs,
                                 free_in=[pe.last()], can=lambda step: len(col_done["qc"]) == 2)
            two_tiles("w_in", 512, xt, q_unit("km", 8, None, GM[:, 1, :]))
            two_tiles("w_in", 1024, xt, v_unit("vm"))
            gate(2, 0)
            drain_steps()
            steps[0] = attention(8, True, head_scores("qm", "km"), values("vm", 64), 1,
                                 dict(bias=scaled_bias(0.125), combine=keep_p, done=branch_done(0)), [(4, 5)], 64, PMs, PMTs,
                                 free_in=[pe.last()], can=lambda step: len(col_done["km"]) == 2)
            gate(2, 1)
            drain()
            branch(2, "w_br_mem")
            two_tiles("w_in", 1536, xt, q_unit("qf", 8, V_QF, None))
            two_tiles("w_in", 2048, xt, q_unit("kf", 8, V_KF, None))
            new.append([None, stages(3, forget_unit())])
            two_tiles("w_in", 2560, xt, v_unit("vf"))
            drain_steps()
            gate_wait[0] = list(m_tok.values()) + [pe.last()]
            gate(0, 0)
            cum["sel"] = dve.go(lambda e: e.tensor_copy(SEL, CT[0:8, C_ID:C_ID + 8].unsqueeze(2).to_broadcast([8, 8, 128])), sq_free[0], sq_free[1], t_c)
            PBs = [PB[:, 0, :], PB[:, 1, :]]
            PTs = [PTB[:, 0, :], PTB[:, 1, :]]
            steps[0] = attention(8, True, head_scores("qf", "kf", fox_extra), values("vf", 64), 1,
                                 dict(bias=fox_bias, combine=keep_p, done=branch_done(1)), [(4, 5)], 64, PBs, PTs,
                                 free_in=[pe.last()], can=lambda step: len(col_done["kf"]) == 2 and "r" in cum)
            gate(0, 1)
            drain(6, 7, 0, 1)
            branch(0, "w_br_moba")
            gate(1, 0)
            gate(1, 1)
            drain_steps()
            drain()
            branch(1, "w_br_fox")
            hold()
            mg = to_columns(MRG, list(m_tok.values()), XH, XL, None, None, banks=(2, 3, 4, 5))

            def residual(name, ready, alpha):
                toks = []
                for c in range(2):
                    bs = ((0, 1), (6, 7))[c]
                    ts = token_mm(bs, name, 512 * c, XH, XL, 512, ready)
                    for tt, b in enumerate(bs):
                        x = H[:, tt, 512 * c:512 * c + 512]
                        toks.append(dve.go(lambda e: e.scalar_tensor_tensor(out=x, in0=x, scalar=alpha, in1=PS[b][:, :], op0=ALU.mult, op1=ALU.add), ts[tt], pool.last()))
                        free[b] = [toks[-1]]
                return toks

            x1 = residual("w_out", mg, 1.0)
            join()

            def swiglu(names, n, ready):
                g_n, u_n, d_n = names
                nch = -(-n // 512)
                hid_free, t_free = [[], []], [[], []]
                hid_tok, turned = [None, None], [None, None]

                def turn(c):
                    m = min(512, n - 512 * c)
                    for tt in range(2):
                        b = 6 + tt
                        pe.wait(free[b], hid_tok[tt])
                        for j in range(m // 128):
                            f = lambda e: e.transpose(PS[b][:, 128 * j:128 * j + 128], HID[:, tt, 128 * j:128 * j + 128], ident)
                            if j == m // 128 - 1:
                                t = pe.go(f)
                            else:
                                pe.raw(f)
                        hid_free[tt] = [t]
                        t1 = act.go(lambda e: e.activation(HTH[:, tt, 0:m], PS[b][:, 0:m], ACT.Copy), t, t_free[tt])
                        t2 = dve.go(lambda e: e.tensor_tensor(HTL[:, tt, 0:m], PS[b][:, 0:m], HTH[:, tt, 0:m].bitcast(F32), ALU.subtract), t1, t_free[tt])
                        free[b] = [t1, t2]
                        turned[tt] = [t1, t2]

                def down(c):
                    m = min(512, n - 512 * c)
                    for h2 in range(2):
                        hi, lo, t_w, p = take(d_n, 4 * c)
                        nj = hi.shape[1]
                        for tt in range(2):
                            pe.wait(*t_w, turned[tt])
                            if c == 0 and h2 == 0:
                                pe.wait(free[2 * tt], free[2 * tt + 1])
                            for jj in range(nj):
                                j = nj * h2 + jj
                                xs = slice(128 * j, 128 * j + 128)
                                for half_ in range(2):
                                    cs = slice(512 * half_, 512 * half_ + 512)
                                    t = mm3(PS[2 * tt + half_][:, :], HTH[:, tt, xs], HTL[:, tt, xs], hi[:, jj, cs], lo[:, jj, cs],
                                            c == 0 and j == 0, c == nch - 1 and j == m // 128 - 1, jj == nj - 1 and half_ == 1)
                            t_free[tt] = [t]
                        taken(p, t)
                    return t

                for c in range(nch + 1):
                    if c < nch:
                        m = min(512, n - 512 * c)
                        gt = token_mm((4, 5), g_n, 512 * c, XH, XL, m, ready, between=(lambda: turn(c - 1)) if c else None)
                        for tt in range(2):
                            t = act.go(lambda e: e.activation(HID[:, tt, 0:m], PS[4 + tt][:, 0:m], ACT.Silu), gt[tt], hid_free[tt])
                            free[4 + tt] = [t]
                            hid_tok[tt] = t
                        ut = token_mm((6, 7), u_n, 512 * c, XH, XL, m, ready)
                        for tt in range(2):
                            t = dve.go(lambda e: e.tensor_tensor(HID[:, tt, 0:m], PS[6 + tt][:, 0:m], HID[:, tt, 0:m], ALU.mult), ut[tt], hid_tok[tt])
                            free[6 + tt] = [t]
                            hid_tok[tt] = t
                    else:
                        turn(c - 1)
                    if c:
                        t = down(c - 1)
                return t

            xt = rms_columns(H, LZ, XH, XL, VT[:, V_FFN:V_FFN + 8], *x1)[1]()
            extra_on[0] = True
            t_last = swiglu(("w_gate", "w_up", "w_down"), FF, xt)
            extra_on[0] = False

            def add_out(t, alpha):
                toks = []
                for tt in range(2):
                    for c in range(2):
                        b = 2 * tt + c
                        x = H[:, tt, 512 * c:512 * c + 512]
                        toks.append(dve.go(lambda e, b=b, x=x: e.scalar_tensor_tensor(out=x, in0=x, scalar=alpha, in1=PS[b][:, :], op0=ALU.mult, op1=ALU.add), t, pool.last()))
                        free[b] = [toks[-1]]
                return toks

            xo = add_out(t_last, 1.0)
            join()

            xt = to_columns(H, xo, XH, XL, None, None)
            area[0] = AR2

            def tokens8(at):
                return ar(at, 8, S)

            SG, KK, LF, CC, QQ, QS, KS = (tokens8(2048 * i) for i in range(7))
            EE, DD = SG, LF
            STT = arena(14336, 3072).rearrange("p (a h n) -> p a h n", a=3, h=8)
            VV = ar(17408, 2, D)
            GN = BC
            lbm, lbe, lbs, lb, oml = small(8), SM[:, 880:904], small(8), SM[:, 904:912], SM[:, 912:920]
            L3 = VT[:, V_LB:V_LB + 24].rearrange("p (a h) -> p a h", a=3)
            E3 = lbe.rearrange("p (a h) -> p a h", a=3)
            t = dve.go(lambda e: e.tensor_tensor(lbm, L3[:, 0, :], L3[:, 1, :], ALU.max), t_vt)
            t = dve.go(lambda e: e.tensor_tensor(lbm, lbm, L3[:, 2, :], ALU.max), t)
            t = dve.go(lambda e: e.tensor_tensor(E3, L3, lbm.unsqueeze(1).to_broadcast([128, 3, 8]), ALU.subtract), t)
            t = act.go(lambda e: e.activation(lbe, lbe, ACT.Exp), t)
            t = dve.go(lambda e: e.tensor_tensor(lbs, E3[:, 0, :], E3[:, 1, :], ALU.add), t)
            t = dve.go(lambda e: e.tensor_tensor(lbs, lbs, E3[:, 2, :], ALU.add), t)
            t = dve.go(lambda e: e.reciprocal(lbs, lbs), t)
            t = dve.go(lambda e: e.tensor_tensor(lb, E3[:, 0, :], lbs, ALU.mult), t)
            t_lb = dve.go(lambda e: e.tensor_scalar(oml, lb, -1.0, 1.0, ALU.mult, ALU.add), t)

            def by_columns(name, c0, h0, then):
                bs = ((0, 1, 2, 3), (4, 5, 6, 7))[pj[0] % 2]
                pj[0] += 1
                out_ = []
                for h2 in range(4):
                    hi, lo, t_w, p = take(name, c0)
                    for a, b in enumerate(bs):
                        pe.wait(*t_w, *xt)
                        if h2 == 0:
                            pe.wait(free[b])
                        ws = slice(128 * a, 128 * a + 128)
                        for j in range(2):
                            kt = 2 * h2 + j
                            t = mm3(PS[b][:, 0:256], hi[:, j, ws], lo[:, j, ws], XH[:, kt, :], XL[:, kt, :], kt == 0, kt == 7, j == 1)
                        if h2 == 3:
                            out_.append(t)
                            then(b, h0 + a, t)
                    taken(p, t)
                    step_hook(h2)

            sg_tok = []

            def f_done(b, h, t):
                t = act.go(lambda e: e.activation(SG[:, h, :], PS[b][:, 0:256], ACT.Sigmoid), t)
                free[b] = [t]
                sg_tok.append(dve.go(lambda e: e.tensor_scalar(SG[:, h, :], SG[:, h, :], oml[:, h:h + 1], lb[:, h:h + 1], ALU.mult, ALU.add), t, t_lb))

            by_columns("hg_w_in_2", 1024, 0, f_done)
            by_columns("hg_w_in_2", 1536, 4, f_done)
            t_kk = pool.go(lambda e: e.tensor_scalar(KK, SG, -1.0, 1.0, ALU.mult, ALU.add), *sg_tok)
            RM = QS
            t_rm = pool.go(lambda e: e.memset(RM, 1.0))
            t_rm = pool.go(lambda e: e.memset(RM.rearrange("p h (a n) -> p (h a) n", a=2)[:, :, 0:1], 0.0), t_rm)
            t_ks0 = pool.go(lambda e: e.memset(KS, 0.0))
            t_st0 = pool.go(lambda e: e.memset(STT, 0.0))
            q_tok = []

            def q_done(b, h, t):
                q_tok.append(act.go(lambda e: e.activation(QQ[:, h, :], PS[b][:, 0:256], ACT.Silu), t))
                free[b] = [q_tok[-1]]

            t_lf = act.go(lambda e: e.activation(LF, SG, ACT.Ln), *sg_tok)
            by_columns("hg_w_in_2", 0, 0, q_done)
            flat = lambda x: x.rearrange("p h n -> p (h n)")
            t_cc = dve.go(lambda e: e.tensor_tensor_scan(flat(CC), flat(RM), flat(LF), 0.0, ALU.mult, ALU.add), t_lf, t_rm)
            t_qs0 = pool.go(lambda e: e.memset(QS, 0.0), t_cc)

            vg_tok, g_tok = [], {}

            def v_unit2(c):
                def f(b, tt, t):
                    def s0():
                        t1 = act.go(lambda e: e.activation(VV[:, tt, 512 * c:512 * c + 512], PS[b][:, :], ACT.Copy), t)
                        free[b] = [t1]
                        vg_tok.append(t1)
                    return [s0]
                return f

            def g_unit(c):
                def f(b, tt, t):
                    g = GN[:, tt, 512 * c:512 * c + 512]
                    g4 = g.rearrange("p (h d) -> p h d", h=4)
                    tok = {}

                    def s0():
                        t1 = act.go(lambda e: e.activation(g, PS[b][:, :], ACT.Exp, scale=-1.0), t)
                        free[b] = [t1]
                        tok["a"] = pool.go(lambda e: e.tensor_scalar(g, g, 1.0, 0.0, ALU.add, ALU.add), t1)

                    def s1():
                        t1 = dve.go(lambda e: e.reciprocal(g, g), tok["a"])
                        g_tok[(tt, c)] = pool.go(lambda e: e.tensor_tensor(g4, g4, NG[:, 0, :].unsqueeze(1).to_broadcast([128, 4, 128]), ALU.mult), t1, t_b)
                    return [s0, s1]
                return f

            st_tok = [t_st0]
            mb = [4, 5, 6, 7]
            L = {"n": 0, "qs": [t_qs0], "ks": [t_ks0], "dd": [t_cc], "ee": [t_kk, t_lf]}

            def views(b2, *xs):
                return [flat(x).rearrange("p (y x b) -> p y x b", x=2, b=b2) for x in xs]

            def level_exps(b2):
                cv, dv_, ev = views(b2, CC, DD, EE)
                if b2 == 128:
                    ref = cv[:, :, 0, 127:128].to_broadcast([128, 8, 128])
                    t_d = dve.go(lambda e: e.tensor_tensor(dv_[:, :, 0, :], cv[:, :, 0, :], ref, ALU.subtract), t_cc, *L["dd"])
                    t_el = act.go(lambda e: e.activation(ev[:, :, 0, :], dv_[:, :, 0, :], ACT.Exp, scale=-1.0), t_d, *L["ee"])
                    t_er = act.go(lambda e: e.activation(ev[:, :, 1, :], cv[:, :, 1, :], ACT.Exp), t_cc, *L["ee"])
                else:
                    c3, d3 = (flat(x).rearrange("p (y z) -> p y z", z=2 * b2) for x in (CC, DD))
                    ref = c3[:, :, b2 - 1:b2].to_broadcast([128, 1024 // b2, 2 * b2])
                    t_d = dve.go(lambda e: e.tensor_tensor(d3, c3, ref, ALU.subtract), t_cc, *L["dd"])
                    t_el = act.go(lambda e: e.activation(ev[:, :, 0, :], dv_[:, :, 0, :], ACT.Exp, scale=-1.0), t_d, *L["ee"])
                    t_er = act.go(lambda e: e.activation(ev[:, :, 1, :], dv_[:, :, 1, :], ACT.Exp), t_d, *L["ee"])
                L["dd"] = [t_el, t_er]

            def level_operands(b2):
                ev, qv, kv, qsv, ksv = views(b2, EE, QQ, KK, QS, KS)
                t_q = dve.go(lambda e: e.tensor_tensor(qsv[:, :, 1, :], qv[:, :, 1, :], ev[:, :, 1, :], ALU.mult), *L["dd"], *q_tok, *L["qs"])
                t_k = pool.go(lambda e: e.tensor_tensor(ksv[:, :, 0, :], kv[:, :, 0, :], ev[:, :, 0, :], ALU.mult), *L["dd"], *L["ks"])
                L["ee"] = [t_q, t_k]
                L["rd"] = [t_q, t_k, t_qs0, t_ks0]

            def level_scores(b2, i):
                a_q, a_k, rd = (QS, KS, L["rd"]) if b2 else (QQ, KK, [*q_tok, t_kk])
                for s_t, t_t in ([(0, 1)] if b2 == 128 else [(0, 0), (1, 1)]):
                    for g in range(2):
                        b = mb[L["n"] % 4]
                        L["n"] += 1
                        pe.wait(free[b], *rd)
                        for j in range(4):
                            h = 4 * g + j
                            f = lambda e: e.matmul(PS[b][:, 128 * j:128 * j + 128], a_k[:, h, 128 * s_t:128 * s_t + 128], a_q[:, h, 128 * t_t:128 * t_t + 128], start=True, stop=True)
                            if j == 3:
                                t = pe.go(f)
                            else:
                                pe.raw(f)
                        src = PS[b][:, :].rearrange("p (j n) -> p j n", j=4)
                        if b2 == 128:
                            t1 = act.go(lambda e: e.activation(STT[:, 2, 4 * g:4 * g + 4, :], src, ACT.Copy), t, t_st0)
                        elif b2 == 64:
                            t1 = act.go(lambda e: e.activation(STT[0:64, s_t, 4 * g:4 * g + 4, 64:128], src[0:64, :, 64:128], ACT.Copy), t, t_st0)
                        else:
                            mk = LEVM[:, 128 * i:128 * i + 128].unsqueeze(1).to_broadcast([128, 4, 128])
                            t1 = dve.go(lambda e: e.copy_predicated(STT[:, s_t, 4 * g:4 * g + 4, :], mk, src), t, t_st0, *st_tok[-4:])
                        free[b] = [t1]
                        st_tok.append(t1)
                L["qs"] = L["ks"] = [t]

            def levels():
                before = None
                for i, b2 in enumerate((128, 64, 32, 16, 8, 4, 2, 1, 0)):
                    if b2:
                        level_exps(b2)
                    if before is not None:
                        level_scores(*before)
                    while len(q_tok) < 8:
                        yield
                    if b2:
                        level_operands(b2)
                    before = (b2, i - 1)
                    yield
                level_scores(*before)

            steps[0] = levels()
            by_columns("hg_w_in_2", 512, 4, q_done)
            for c in range(2):
                two_tiles("hg_w_in_2", 2048 + 512 * c, xt, v_unit2(c), bset=((0, 1), (2, 3)))
            for c in range(2):
                two_tiles("hg_w_in_2", 3072 + 512 * c, xt, g_unit(c), bset=((0, 1), (2, 3)))
            drain()
            drain_steps()
            OR = ar(4096, 2, D)
            SQ2 = ar(0, 2, D)
            o_tok = []
            for tt in range(2):
                for g in range(2):
                    b = pj_bank((0, 1, 2, 3))
                    pe.wait(free[b], *st_tok, *vg_tok)
                    for j in range(4):
                        h = 4 * g + j
                        v0, v1 = VV[:, 0, 128 * h:128 * h + 128], VV[:, 1, 128 * h:128 * h + 128]
                        o = PS[b][:, 128 * j:128 * j + 128]
                        if tt == 0:
                            f = lambda e, o=o, h=h, v0=v0, v1=v1: e.matmul(o, STT[:, 0, h, :], v0, start=True, stop=True)
                        else:
                            pe.raw(lambda e, o=o, h=h, v0=v0, v1=v1: e.matmul(o, STT[:, 2, h, :], v0, start=True, stop=False))
                            f = lambda e, o=o, h=h, v0=v0, v1=v1: e.matmul(o, STT[:, 1, h, :], v1, start=False, stop=True)
                        if j == 3:
                            t = pe.go(f)
                        else:
                            pe.raw(f)
                    sq = SQ2[:, tt, 512 * g:512 * g + 512]
                    ss = small(4)
                    t = act.go(lambda e, sq=sq, b=b: e.activation(sq, PS[b][:, :], ACT.Square), t, *L["ee"])
                    t = dve.go(lambda e, sq=sq, ss=ss: e.tensor_reduce(ss, sq.rearrange("p (h d) -> p h d", h=4), AX.X, ALU.add), t)
                    r, t = rsqrt(ss, 4, 1.0 / 128, 1e-5, t)
                    ov = OR[:, tt, 512 * g:512 * g + 512]
                    t = dve.go(lambda e, ov=ov, b=b, r=r: e.tensor_tensor(ov.rearrange("p (h d) -> p h d", h=4), PS[b][:, :].rearrange("p (h d) -> p h d", h=4),
                                                                         r.unsqueeze(2).to_broadcast([128, 4, 128]), ALU.mult), t, *L["dd"])
                    free[b] = [t]
                    o_tok.append(dve.go(lambda e, ov=ov, tt=tt, g=g: e.tensor_tensor(ov, ov, GN[:, tt, 512 * g:512 * g + 512], ALU.mult), t, g_tok[(tt, g)]))
            hold()
            ot = to_columns(OR, o_tok, XH, XL, None, None, banks=(4, 5, 6, 7))
            h1 = residual("hg_w_out_2", ot, ALPHA)
            join()

            def layer_norm(k, ready):
                z = LZ
                hold()
                for j, nm_ in enumerate(("ln_g_2", "ln_b_2")):
                    t_ln = s_ln.start(sp_ln, BC[:, j, :], bcast(I[nm_][k * D:k * D + D], D), *ready, ln_free[0])
                zt = []
                for tt in range(2):
                    st, mv, nb = small(12), small(2), small(1)
                    ta = [dve.go(lambda e, c=c, tt=tt, st=st: e.bn_stats(st[:, 6 * c:6 * c + 6], H[:, tt, 512 * c:512 * c + 512]), *ready) for c in range(2)]
                    t = dve.go(lambda e, st=st, mv=mv: e.bn_aggr(mv, st), *ta)
                    r, t = rsqrt(mv[:, 1:2], 1, 1.0, 1e-5, t)
                    t2 = dve.go(lambda e, mv=mv, r=r, nb=nb: e.scalar_tensor_tensor(out=nb, in0=mv[:, 0:1], scalar=-1.0, in1=r, op0=ALU.mult, op1=ALU.mult), t)
                    zt.append(dve.go(lambda e, tt=tt, r=r, nb=nb: e.tensor_scalar(z[:, tt, :], H[:, tt, :], r, nb, ALU.mult, ALU.add), t2))
                cols_ = to_columns(z, zt, XH, XL, VT[:, V_LNG + 8 * k:V_LNG + 8 * k + 8], VT[:, V_LNB + 8 * k:V_LNB + 8 * k + 8], tmp=LT)
                rows_ = []
                for tt in range(2):
                    t = pool.go(lambda e, tt=tt: e.tensor_tensor(H[:, tt, :], z[:, tt, :], BC[:, 0, :], ALU.mult), t_ln, *zt)
                    rows_.append(pool.go(lambda e, tt=tt: e.tensor_tensor(H[:, tt, :], H[:, tt, :], BC[:, 1, :], ALU.add), t))
                ln_free[0] = rows_
                return cols_, rows_

            sp_ln = act
            ln_free = [[]]
            xt, rt = layer_norm(0, h1)
            extra_on[0] = True
            t_last = swiglu(("ffn_w_gate_2", "ffn_w_up_2", "ffn_w_down_2"), FF, xt)
            extra_on[0] = False
            xo = add_out(t_last, ALPHA)
            join()
            xt, rt = layer_norm(1, xo)

            area[0] = AR3
            QD, KD = tokens8(0), tokens8(2048)
            VD = ar(4096, 2, D)
            RX = ar(6144, 2, 512)
            RU = ar(7168, 2, 512)
            OD = ar(8192, 2, D)
            lp, ls, le, nl = SM[:, 768:896], small(2), small(2), SM[:, 920:921]
            L4 = LAMB[:, :].rearrange("p (a b d) -> p a b d", a=2, b=2)
            t = dve.go(lambda e: e.tensor_tensor(lp.rearrange("p (a d) -> p a d", a=2), L4[:, :, 0, :], L4[:, :, 1, :], ALU.mult), t_b)
            t = dve.go(lambda e: e.tensor_reduce(ls, lp.rearrange("p (a d) -> p a d", a=2), AX.X, ALU.add), t)
            t = act.go(lambda e: e.activation(le, ls, ACT.Exp), t)
            t = dve.go(lambda e: e.tensor_tensor(nl, le[:, 1:2], le[:, 0:1], ALU.subtract), t)
            t_nl = dve.go(lambda e: e.tensor_scalar(nl, nl, -LAM_INIT, None, ALU.add), t)
            t_ng = dve.go(lambda e: e.tensor_scalar(NG[:, 1, :], NG[:, 1, :], 1.0 - LAM_INIT, None, ALU.mult), t_b)
            rx_free = [[], []]
            qd_tok = [[], []]

            def rope_unit(dst, tt, c, b, t, i):
                x, u = RX[:, i, :].rearrange("p (g d) -> p g d", g=8), RU[:, i, :].rearrange("p (g d) -> p g d", g=8)
                ps = PS[b][:, :].rearrange("p (g d) -> p g d", g=8)
                a = C_RD + 128 * tt
                cs = CT[:, a:a + 64].unsqueeze(1).to_broadcast([128, 8, 64])
                ns = CT[:, a + 64:a + 96].unsqueeze(1).to_broadcast([128, 8, 32])
                sn = CT[:, a + 96:a + 128].unsqueeze(1).to_broadcast([128, 8, 32])
                t1 = dve.go(lambda e: e.tensor_tensor(x, ps, cs, ALU.mult), t, rx_free[i])
                t2 = dve.go(lambda e: e.tensor_tensor(u[:, :, 0:32], ps[:, :, 32:64], ns, ALU.mult), t)
                t3 = dve.go(lambda e: e.tensor_tensor(u[:, :, 32:64], ps[:, :, 0:32], sn, ALU.mult), t)
                free[b] = [t1, t2, t3]
                t = pool.go(lambda e: e.tensor_tensor(x, x, u, ALU.add), t1, t2, t3)
                yield
                tb = 2 + i
                pe.wait(free[tb], t)
                for j in range(4):
                    f = lambda e, j=j: e.transpose(PS[tb][:, 128 * j:128 * j + 128], RX[:, i, 128 * j:128 * j + 128], ident)
                    if j == 3:
                        t = pe.go(f)
                    else:
                        pe.raw(f)
                rx_free[i] = [t]
                t = act.go(lambda e: e.activation(dst[:, 4 * c:4 * c + 4, 128 * tt:128 * tt + 128], PS[tb][:, :].rearrange("p (j n) -> p j n", j=4), ACT.Copy), t)
                free[tb] = [t]
                qd_tok[c].append(t)

            vd_tok = [[], []]

            def da_in(k, c):
                def v_stage(b, tt, t):
                    t1 = act.go(lambda e: e.activation(VD[:, tt, 512 * c:512 * c + 512], PS[b][:, :], ACT.Copy), t)
                    free[b] = [t1]
                    vd_tok[c].append(t1)

                def then(b, tt, t):
                    if k == 2:
                        return [lambda: v_stage(b, tt, t)]
                    return stages(2, rope_unit((QD, KD)[k], tt, c, b, t, tt))
                two_tiles("da_w_in_2", 1024 * k + 512 * c, xt, then)

            def da_scores(h, c, bank):
                o = 64 * c
                pe.wait(free[bank], *qd_tok[h // 4])
                for a, b_, qt, n in ((0, 128, 0, 128), (128, 384, 1, 256)):
                    pe.raw(lambda e, a=a, b_=b_, qt=qt, n=n: e.matmul(PS[bank][:, a:b_], QD[o:o + 64, h, 128 * qt:128 * qt + 128], KD[o:o + 64, h, 0:n], start=True, stop=False))
                    g = lambda e: e.matmul(PS[bank][:, a:b_], IDB[:, :], CSB[:, 256 - n:256], start=False, stop=True)
                    if a:
                        t = pe.go(g)
                    else:
                        pe.raw(g)
                return t

            def da_combine(h, st, k0, width):
                (p0, s0, ta0, rs0), (p1, s1, ta1, rs1) = st
                r0, r1 = small(2), small(2)
                t = dve.go(lambda e: e.reciprocal(r0, rs0), *ta0)
                t1 = dve.go(lambda e: e.reciprocal(r1, rs1), *ta1)
                t1 = dve.go(lambda e: e.tensor_scalar(r1, r1, nl, None, ALU.mult), t1, t_nl)
                out_ = []
                for q, (a, b_) in enumerate(((0, k0), (k0, width))):
                    t2 = dve.go(lambda e, q=q, a=a, b_=b_: e.tensor_scalar(p1[:, a:b_], p1[:, a:b_], r1[:, q:q + 1], None, ALU.mult), t1)
                    out_.append(dve.go(lambda e, q=q, a=a, b_=b_: e.scalar_tensor_tensor(out=p0[:, a:b_], in0=p0[:, a:b_], scalar=r0[:, q:q + 1], in1=p1[:, a:b_], op0=ALU.mult, op1=ALU.add), t, t2))
                return p0, s0, out_

            od_tok = []

            def da_done(g, ob, t):
                for q in range(2):
                    sq = TQ[:, q, :]
                    ss = small(4)
                    b = ob[q]
                    t1 = act.go(lambda e, sq=sq, b=b: e.activation(sq, PS[b][:, :], ACT.Square), t, tq_free[q])
                    t1 = dve.go(lambda e, sq=sq, ss=ss: e.tensor_reduce(ss, sq.rearrange("p (h d) -> p h d", h=4), AX.X, ALU.add), t1)
                    tq_free[q] = [t1]
                    r, t1 = rsqrt(ss, 4, 1.0 / 128, 1e-5, t1)
                    ov = OD[:, q, 512 * g:512 * g + 512].rearrange("p (h d) -> p h d", h=4)
                    t1 = dve.go(lambda e, ov=ov, b=b, r=r: e.tensor_tensor(ov, PS[b][:, :].rearrange("p (h d) -> p h d", h=4), r.unsqueeze(2).to_broadcast([128, 4, 128]), ALU.mult), t1)
                    free[b] = [t1]
                    od_tok.append(dve.go(lambda e, ov=ov: e.tensor_tensor(ov, ov, NG[:, 1, :].unsqueeze(1).to_broadcast([128, 4, 128]), ALU.mult), t1, t_ng))

            TQ = ar(10240, 2, 512)
            tq_free = [[], []]
            DP = [ar(11264, 2, 512), ar(12288, 2, 512)]
            DPT = ar(13312, 2, 512)
            def da_values(h, k):
                pe.wait(*vd_tok[h // 4])
                return VD[:, k, 128 * h:128 * h + 128]

            sbank, tbank = [3, 2], [2]
            for c in range(2):
                da_in(0, c)
                da_in(1, c)
                da_in(2, c)
                if c == 0:
                    drain()
                    steps[0] = attention(8, True, da_scores, da_values, 2,
                                         dict(bias=scaled_bias(0.125), combine=da_combine, done=da_done), [(4, 5), (4, 5)], 128,
                                         [DP[0][:, 0, :], DP[0][:, 1, :], DP[1][:, 0, :], DP[1][:, 1, :]], [DPT[:, 0, :], DPT[:, 1, :]], sbank, tbank,
                                         can=lambda step: (step < 4 or len(qd_tok[1]) == 4) and (step < 6 or len(vd_tok[1]) == 2))
            drain()
            sbank[:], tbank[:] = [0, 1, 3, 6], [2, 7]
            drain_steps()
            hold()
            ot = to_columns(OD, od_tok, XH, XL, None, None, banks=(2, 3, 4, 5))
            h1 = residual("da_w_out_2", ot, ALPHA)
            join()
            xt, rt = layer_norm(2, h1)

            G = SM[:, 928:944].rearrange("p (a e) -> p a e", a=2)
            MK = SM[:, 944:960].rearrange("p (a e) -> p a e", a=2)
            g_tok2 = []
            for tt in range(2):
                b = 4 + tt
                t = narrow_mm(b, tt, 1, *xt)
                lg, mx, cmp_, rk, nm, e2 = small(8), small(8), SM[:, 768 + 0:768 + 64], MK[:, tt, :], small(1), small(1)
                eq = SM[:, 832:896]
                t = dve.go(lambda e, b=b, lg=lg: e.tensor_copy(lg, PS[b][:, 0:8]), t)
                free[b] = [t]
                tm = dve.go(lambda e, lg=lg, mx=mx: e.max(mx, lg), t)
                oth = lg.unsqueeze(1).to_broadcast([128, 8, 8])
                own = lg.unsqueeze(2).to_broadcast([128, 8, 8])
                c3, q3 = (x.rearrange("p (a b) -> p a b", a=8) for x in (cmp_, eq))
                tri = CT[:, C_TRI8:C_TRI8 + 64].rearrange("p (a b) -> p a b", a=8)
                prev = g_tok2[-1] if g_tok2 else None
                t1 = dve.go(lambda e, c3=c3, oth=oth, own=own: e.tensor_tensor(c3, oth, own, ALU.is_gt), t, prev)
                t2 = dve.go(lambda e, q3=q3, oth=oth, own=own: e.tensor_tensor(q3, oth, own, ALU.is_equal), t)
                t2 = dve.go(lambda e, q3=q3: e.tensor_tensor(q3, q3, tri, ALU.mult), t2)
                t2 = dve.go(lambda e, c3=c3, q3=q3: e.tensor_tensor(c3, c3, q3, ALU.add), t2, t1)
                t2 = dve.go(lambda e, c3=c3, rk=rk: e.tensor_reduce(rk, c3, AX.X, ALU.add), t2)
                t2 = dve.go(lambda e, rk=rk: e.tensor_scalar(rk, rk, 2.0, None, ALU.is_lt), t2)
                t3 = dve.go(lambda e, nm=nm, mx=mx: e.tensor_scalar(nm, mx[:, 0:1], -1.0, None, ALU.mult), tm)
                t4 = act.go(lambda e, e2=e2, mx=mx, nm=nm: e.activation(e2, mx[:, 1:2], ACT.Exp, bias=nm), t3)
                t5 = act.go(lambda e, lg=lg, nm=nm: e.activation(lg, lg, ACT.Exp, bias=nm), t3, t2)
                t4 = dve.go(lambda e, e2=e2: e.tensor_scalar(e2, e2, 1.0, None, ALU.add), t4)
                t4 = dve.go(lambda e, e2=e2: e.reciprocal(e2, e2), t4)
                g_tok2.append(dve.go(lambda e, tt=tt, lg=lg, e2=e2, rk=rk: e.scalar_tensor_tensor(out=G[:, tt, :], in0=lg, scalar=e2, in1=rk, op0=ALU.mult, op1=ALU.mult), t4, t5, t2))
            t_hh = act.go(lambda e: e.activation(HH[:, :, :], H[:, :, :], ACT.Copy), *rt)
            t_hl = dve.go(lambda e: e.tensor_tensor(HL[:, :, :], H[:, :, :], HH[:, :, :].bitcast(F32), ALU.subtract), t_hh, *rt)
            t_h = dve.go(lambda e: e.tensor_scalar(H[:, :, :], H[:, :, :], ALPHA, None, ALU.mult), t_hh, t_hl)
            ones_m = HID[:, 0, 0:128]
            t_on = pool.go(lambda e: e.memset(ones_m, 1.0), *xt)
            POS = SM[:, 976:992].rearrange("p (a e) -> p a e", a=2)
            pe.wait(free[4], t_on, *g_tok2)
            pe.raw(lambda e: e.matmul(PS[4][:, 0:8], triu, MK[:, 0, :], start=True, stop=True))
            pe.raw(lambda e: e.matmul(PS[4][:, 8:16], ones_m, MK[:, 0, :], start=True, stop=False))
            pe.raw(lambda e: e.matmul(PS[4][:, 8:16], triu, MK[:, 1, :], start=False, stop=True))
            pe.raw(lambda e: e.matmul(PS[4][0:1, 16:24], ones_m[:, 0:1], MK[:, 0, :], start=True, stop=False))
            t_cnt = pe.go(lambda e: e.matmul(PS[4][0:1, 16:24], ones_m[:, 0:1], MK[:, 1, :], start=False, stop=True))
            most = small(1)
            t = dve.go(lambda e: e.tensor_reduce(most[0:1, :], PS[4][0:1, 16:24], AX.X, ALU.max), t_cnt)
            t_most = dve.go(lambda e: e.tensor_copy(CNT[:, :], most[0:1, :]), t)
            t = dve.go(lambda e: e.tensor_tensor(POS, PS[4][:, 0:16].rearrange("p (a e) -> p a e", a=2), MK, ALU.mult), t_cnt)
            free[4] = [t]
            t_pos = dve.go(lambda e: e.tensor_scalar(POS, POS, -1.0, None, ALU.add), t)
            iota = CT[:, C_IOTA:C_IOTA + CAP]
            extra_on[0] = True
            M = {"po_free": [], "pot_free": [], "e_free": [], "hid_free": [[], []], "t_free": [[], []], "hid": [None, None],
                 "turned": [None, None], "n": 0, "z_free": [], "h": {}}

            def lists(ex):
                M["po"] = [dve.go(lambda e: e.tensor_scalar(PO[:, tt, :], iota, POS[:, tt, ex:ex + 1], None, ALU.is_equal), t_pos, M["po_free"]) for tt in range(2)]

            def gather(ex):
                pe.wait(M["po"], t_hh, t_hl)
                out_ = []
                for src, dst in ((HH, EH), (HL, EL)):
                    for q in range(2):
                        b = 6 + q
                        pe.wait(free[b])
                        for j in range(4):
                            d = 4 * q + j
                            for tt in range(2):
                                f = lambda e: e.matmul(PS[b][:, 128 * j:128 * j + CAP], src[:, tt, 128 * d:128 * d + 128], PO[:, tt, :], start=(tt == 0), stop=(tt == 1))
                                if j == 3 and tt == 1:
                                    t = pe.go(f)
                                else:
                                    pe.raw(f)
                        ps = PS[b][:, :].rearrange("p (j n) -> p j n", j=4)
                        if q:
                            t = act.go(lambda e: e.activation(dst[:, 4 * q:4 * q + 4, :], ps, ACT.Copy), t, M["e_free"])
                        else:
                            t = dve.go(lambda e: e.tensor_copy(dst[:, 4 * q:4 * q + 4, :], ps), t, M["e_free"])
                        free[b] = [t]
                        out_.append(t)
                M["e"] = out_

            def scatter_lists(ex):
                pe.wait(free[7], M["po"], *g_tok2)
                for tt in range(2):
                    pe.raw(lambda e: e.transpose(PS[7][:, 128 * tt:128 * tt + 128], PO[:, tt, :].bitcast(F32), ident))
                pe.raw(lambda e: e.matmul(PS[7][:, 256:257], PO[:, 0, :].bitcast(F32), G[:, 0, ex:ex + 1], start=True, stop=False))
                t = pe.go(lambda e: e.matmul(PS[7][:, 256:257], PO[:, 1, :].bitcast(F32), G[:, 1, ex:ex + 1], start=False, stop=True))
                M["po_free"] = [t]
                M["pot"] = dve.go(lambda e: e.tensor_copy(POT[:, :, :], PS[7][:, 0:256].rearrange("p (a n) -> p a n", a=2)), t, M["pot_free"])
                GS = SM[:, 992 + ex:993 + ex]
                M["gs"] = dve.go(lambda e: e.tensor_copy(GS, PS[7][:, 256:257]), t)
                free[7] = [M["pot"], M["gs"]]

            def moe_mm(b, name, c0):
                for h2 in range(2):
                    hi, lo, t_w, p = take(name, c0)
                    pe.wait(*t_w, *M["e"])
                    if h2 == 0:
                        pe.wait(free[b])
                    for j in range(4):
                        kt = 4 * h2 + j
                        t = mm3(PS[b][:, :], EH[:, kt, :], EL[:, kt, :], hi[:, j, :], lo[:, j, :], kt == 0, kt == 7, j == 3)
                    taken(p, t)
                M["e_free"] = [t]
                return t

            def moe_turn():
                i = (M["n"] - 1) % 2
                pe.wait(free[6], M["hid"][i])
                for j in range(4):
                    f = lambda e: e.transpose(PS[6][:, 128 * j:128 * j + 128], HID[:, i, 128 * j:128 * j + 128], ident)
                    if j == 3:
                        t = pe.go(f)
                    else:
                        pe.raw(f)
                M["hid_free"][i] = [t]
                t1 = act.go(lambda e: e.activation(HTH[:, i, :], PS[6][:, :], ACT.Copy), t, M["t_free"][i])
                t2 = dve.go(lambda e: e.tensor_tensor(HTL[:, i, :], PS[6][:, :], HTH[:, i, :].bitcast(F32), ALU.subtract), t1, M["t_free"][i])
                free[6] = [t1, t2]
                M["turned"][i] = [t1, t2]

            def moe_down(ex, c, i):
                for h2 in range(2):
                    hi, lo, t_w, p = take(f"moe_w_down_2.{ex}", 4 * c)
                    pe.wait(*t_w, M["turned"][i])
                    if c == 0 and h2 == 0:
                        pe.wait(free[4], free[5])
                    for jj in range(2):
                        j = 2 * h2 + jj
                        xs = slice(128 * j, 128 * j + 128)
                        for q in range(2):
                            cs = slice(512 * q, 512 * q + 512)
                            t = mm3(PS[4 + q][:, :], HTH[:, i, xs], HTL[:, i, xs], hi[:, jj, cs], lo[:, jj, cs], c == 0 and j == 0, c == 6 and j == 3, jj == 1 and q == 1)
                    taken(p, t)
                M["t_free"][i] = [t]
                if c == 6:
                    GS = SM[:, 992 + ex:993 + ex]
                    M["z"] = []
                    for q in range(2):
                        cs = slice(512 * q, 512 * q + 512)
                        t1 = act.go(lambda e: e.activation(ZH[:, cs], PS[4 + q][:, :], ACT.Copy, scale=GS), t, M["gs"], M["z_free"])
                        t2 = dve.go(lambda e: e.scalar_tensor_tensor(out=ZL[:, cs], in0=PS[4 + q][:, :], scalar=GS, in1=ZH[:, cs].bitcast(F32), op0=ALU.mult, op1=ALU.subtract),
                                    t1, M["gs"], M["z_free"])
                        free[4 + q] = [t1, t2]
                        M["z"] += [t1, t2]

            def combine(k):
                tt, q = k // 2, k % 2
                cs = slice(512 * q, 512 * q + 512)
                pe.wait(free[7], M["z"], M["pot"])
                pe.raw(lambda e: e.matmul(PS[7][:, :], POT[:, tt, :], ZH[:, cs], start=True, stop=False))
                t = pe.go(lambda e: e.matmul(PS[7][:, :], POT[:, tt, :], ZL[:, cs], start=False, stop=True))
                if k == 3:
                    M["z_free"] = [t]
                    M["pot_free"] = [t]
                x = H[:, tt, cs]
                M["h"][k] = dve.go(lambda e: e.tensor_tensor(x, x, PS[7][:, :], ALU.add), t, t_h, M["h"].get(k))
                free[7] = [M["h"][k]]

            lists(0)
            gather(0)
            prev = None
            for ex in range(NE):
                for c in range(7):
                    i = M["n"] % 2
                    gb, ub = i, 2 + i
                    gt = moe_mm(gb, f"moe_w_gate_2.{ex}", 512 * c)
                    t = act.go(lambda e: e.activation(HID[:, i, :], PS[gb][:, :], ACT.Silu), gt, M["hid_free"][i], t_cnt)
                    free[gb] = [t]
                    if prev is not None:
                        moe_turn()
                    ut = moe_mm(ub, f"moe_w_up_2.{ex}", 512 * c)
                    t = dve.go(lambda e: e.tensor_tensor(HID[:, i, :], PS[ub][:, :], HID[:, i, :], ALU.mult), ut, t)
                    free[ub] = [t]
                    M["hid"][i] = t
                    if c == 6 and ex < NE - 1:
                        gather(ex + 1)
                    if ex and 1 <= c <= 4:
                        combine(c - 1)
                    if c == 5:
                        scatter_lists(ex)
                        if ex < NE - 1:
                            lists(ex + 1)
                    if prev is not None:
                        moe_down(*prev)
                    prev = (ex, c, i)
                    M["n"] += 1
            moe_turn()
            moe_down(*prev)
            for k in range(4):
                combine(k)
            xo = list(M["h"].values())

            def second_pass():
                e_, d_, a_, w_ = (Engine(sems["o_" + n], x.e) for n, x in (("pe", pe), ("dve", dve), ("act", act), ("w0", sp)))
                ws = [DmaSem(sems[f"o_w{i}"]) for i in range(3)]
                before = [x.last() for x in (pe, dve, act, pool)]
                for x in (e_, d_, a_, w_):
                    x.wait(*before)
                XO = LZ[:, 0, :].rearrange("p (k n) -> p k n", k=8)
                ZO = LZ[:, 1, :]
                HO, TO = LT[:, 0, :], LT[:, 1, :]
                P2 = HID[:, 0, 0:256].rearrange("p (a n) -> p a n", a=2)
                P2T = HID[:, 0, 256:512].rearrange("p (a n) -> p a n", a=2)
                GO = HID[:, 1, 0:1]
                POS2 = HID[:, 1, 8:24].rearrange("p (a n) -> p a n", a=2)
                t_pos2 = d_.go(lambda e: e.tensor_scalar(POS2, POS[:, :, :], float(-LIM), None, ALU.add))

                def chain(x, fs, *waits):
                    x.wait(*waits)
                    for f in fs[:-1]:
                        x.raw(f)
                    return x.go(fs[-1])

                def mm(o, l, r, a, b):
                    return lambda e: e.matmul(o, l, r, start=a, stop=b)

                used_ = [None, None, None]
                for ex in range(NE):
                    for tt in range(2):
                        t = d_.go(lambda e: e.tensor_scalar(P2[:, tt, :], iota, POS2[:, tt, ex:ex + 1], None, ALU.is_equal), t_pos2, e_.last())
                    ms = []
                    for k in range(8):
                        o = PS[k // 4][:, 128 * (k % 4):128 * (k % 4) + 128]
                        ks = slice(128 * k, 128 * k + 128)
                        for n, (src, tt) in enumerate(((HH, 0), (HL, 0), (HH, 1), (HL, 1))):
                            ms.append(mm(o, src[:, tt, ks].bitcast(F32), P2[:, tt, :], n == 0, n == 3))
                    for tt in range(2):
                        ms.append(lambda e, tt=tt: e.transpose(PS[2][:, 128 * tt:128 * tt + 128], P2[:, tt, :], ident))
                    for tt in range(2):
                        ms.append(mm(PS[2][:, 256:257], P2[:, tt, :], G[:, tt, ex:ex + 1], tt == 0, tt == 1))
                    t = chain(e_, ms, t)
                    for q in range(2):
                        d_.go(lambda e: e.tensor_copy(XO[:, 4 * q:4 * q + 4, :], PS[q][:, :].rearrange("p (j n) -> p j n", j=4)), t)
                    d_.go(lambda e: e.tensor_copy(P2T, PS[2][:, 0:256].rearrange("p (a n) -> p a n", a=2)), t)
                    t_g = d_.go(lambda e: e.tensor_copy(GO, PS[2][:, 256:257]), t)
                    for c in range(7):
                        n0 = 512 * c
                        srcs = [I[f"moe_w_gate_2.{ex}"].rearrange("(t p) n -> p t n", p=128)[:, :, n0:n0 + 512],
                                I[f"moe_w_up_2.{ex}"].rearrange("(t p) n -> p t n", p=128)[:, :, n0:n0 + 512],
                                I[f"moe_w_down_2.{ex}"].rearrange("(t p) n -> p t n", p=128)[:, 4 * c:4 * c + 4, :]]
                        wv = [ring[:, i, :].rearrange("p (t n) -> p t n", t=8 if i < 2 else 4) for i in range(3)]
                        tw = [ws[i].start(w_, wv[i], srcs[i], used_[i]) for i in range(3)]
                        tk = []
                        for i in range(2):
                            tk.append(chain(e_, [mm(PS[3 + i][:, :], XO[:, k, :], wv[i][:, k, :], k == 0, k == 7) for k in range(8)], tw[i], t_g))
                            used_[i] = tk[i]
                        t = a_.go(lambda e: e.activation(HO, PS[3][:, :], ACT.Silu), tk[0])
                        t = d_.go(lambda e: e.tensor_tensor(HO, PS[4][:, :], HO, ALU.mult), t, tk[1])
                        t = chain(e_, [lambda e, j=j: e.transpose(PS[5][:, 128 * j:128 * j + 128], HO[:, 128 * j:128 * j + 128], ident) for j in range(4)], t)
                        t = a_.go(lambda e: e.activation(TO, PS[5][:, :], ACT.Copy), t)
                        t = chain(e_, [mm(PS[6 + q][:, :], TO[:, 128 * j:128 * j + 128], wv[2][:, j, 512 * q:512 * q + 512], c == 0 and j == 0, c == 6 and j == 3)
                                       for j in range(4) for q in range(2)], t, tw[2])
                        used_[2] = t
                    for q in range(2):
                        t1 = d_.go(lambda e: e.tensor_scalar(ZO[:, 512 * q:512 * q + 512], PS[6 + q][:, :], GO, None, ALU.mult), t)
                    for k in range(4):
                        tt, cs = k // 2, slice(512 * (k % 2), 512 * (k % 2) + 512)
                        t = e_.go(lambda e: e.matmul(PS[k][:, :], P2T[:, tt, :], ZO[:, cs], start=True, stop=True), t1)
                        x = H[:, tt, cs]
                        d_.go(lambda e: e.tensor_tensor(x, x, PS[k][:, :], ALU.add), t)
                    e_.wait(d_.last())
                    a_.wait(d_.last())
                for x in (e_, d_, a_, w_):
                    x.wait(d_.last(), e_.last(), a_.last())

            for x in (pe, dve, act, sp):
                x.wait(t_most)
            live = [x for x in (pe, dve, act, sp) if x.e is not None]
            if live:
                n_most = live[0].e.value_load(CNT[0:1, 0:1], min_val=0, max_val=S)
                with live[0].e.If(n_most > LIM):
                    second_pass()
            join()
            xt, rt = layer_norm(3, xo)
            t = s_o.start(act, out.rearrange("(a p) n -> p a n", p=128), H[:, :, :], *rt)
            act.wait(t)
            for x in (pe, dve, pool, sp):
                x.wait(t)

        block = ctx.enter_context(nc.Block())

        @block.sync
        def _(e):
            program("sp", e)

        @block.scalar
        def _(e):
            program("act", e)

        @block.gpsimd
        def _(e):
            program("pool", e)

        @block.tensor
        def _(e):
            program("pe", e)

        @block.vector
        def _(e):
            program("dve", e)


_FLAT = ("g_mix", "b_forget", "g_q_moba", "g_k_moba", "g_q_fox", "g_k_fox", "g_q_mem", "g_k_mem", "g_mem", "g_ffn",
         "hg_lb_2", "hg_norm_g_2", "da_lam_2", "da_norm_g_2", "ln_g_2", "ln_b_2")
_ROWS = ("x", "mem", "w_in", "w_mem_kv", "w_br_moba", "w_br_fox", "w_br_mem", "w_out", "w_gate", "w_up", "w_down",
         "hg_w_in_2", "hg_w_out_2", "da_w_in_2", "da_w_out_2", "ffn_w_gate_2", "ffn_w_up_2", "ffn_w_down_2",
         "moe_w_router_2")
_EXPERT = ("moe_w_gate_2", "moe_w_up_2", "moe_w_down_2")


def kernel(**inputs):
    import concourse.bacc as _bacc
    from concourse.bass_utils import run_bass_kernel_spmd as _run

    nc = _bacc.Bacc("TRN2", target_bir_lowering=False, num_devices=1)
    arrays, I = {}, {}
    for name in _FLAT + _ROWS + _EXPERT:
        a = np.ascontiguousarray(inputs[name])
        if name in _FLAT:
            a = a.reshape(-1)
        elif name in _ROWS:
            a = a.reshape(a.shape[-2], a.shape[-1])
        else:
            a = a.reshape(a.shape[-3], a.shape[-2], a.shape[-1])
        arrays["in_" + name] = a
        ap = nc.dram_tensor("in_" + name, a.shape, mybir.dt.from_np(a.dtype), kind="ExternalInput").ap()
        I[name] = ap
        if name in _EXPERT:
            for e in range(NE):
                I[f"{name}.{e}"] = ap[e, :, :]
    c = constant_table()
    arrays["in_table"] = c
    table = nc.dram_tensor("in_table", c.shape, F32, kind="ExternalInput").ap()
    out = nc.dram_tensor("out_0", (S, D), F32, kind="ExternalOutput").ap()
    build(nc, I, table, out)
    r = _run(nc, [arrays], core_ids=[0])
    return np.asarray(r.results[0]["out_0"]).reshape(1, S, D)
```

```python
import math
from contextlib import ExitStack

import numpy as np

import concourse.bass as bass
from concourse import mybir

F32 = mybir.dt.float32
FR = mybir.dt.float32r
U16 = mybir.dt.uint16
BF16 = mybir.dt.bfloat16
U32 = mybir.dt.uint32
ALU = mybir.AluOpType
ACT = mybir.ActivationFunctionType
AX = mybir.AxisListType

D = 1024
S = 256
FF = 2816
FFE = 3584
NE = 8
NEG = -1e30
ALPHA = 4.0 ** 0.25
LAM_INIT = 0.8 - 0.6 * math.exp(-0.3)
NSLOT = 3
CAP = 128
LIM = 128

C_ID = 0
C_TRIU = 128
C_CAUS = 256
C_RM = 384
C_RD = 448
C_TRI8 = 704
C_IOTA = 768
C_LEV = 896
C_KEEP = C_LEV
C_END = 1920

V_MIX, V_MEM, V_FFN, V_LNG, V_LNB, V_QF, V_KF, V_QC, V_KC, V_LB = 0, 8, 16, 24, 56, 88, 89, 90, 91, 92
V_END = 116


def constant_table():
    c = np.zeros((128, C_END), np.float32)
    r = np.arange(128)
    c[:, C_ID:C_ID + 128] = np.eye(128)
    c[:, C_TRIU:C_TRIU + 128] = r[:, None] <= r[None, :]
    c[:, C_CAUS:C_CAUS + 128] = np.where(r[None, :] > r[:, None], NEG, 0.0)
    for i, b in enumerate((64, 32, 16, 8, 4, 2, 1)):
        same = (r[:, None] // (2 * b)) == (r[None, :] // (2 * b))
        c[:, C_LEV + 128 * i:C_LEV + 128 * i + 128] = same & (r[:, None] % (2 * b) < b) & (r[None, :] % (2 * b) >= b)
    c[:, C_LEV + 896:C_LEV + 1024] = np.eye(128)
    pos = np.arange(S, dtype=np.float32)
    inv = (1.0 / (np.float32(500000.0) ** (np.arange(8, dtype=np.float32) * np.float32(2.0) / np.float32(16)))).astype(np.float32)
    ang = (pos[:, None] * inv[None, :]).astype(np.float64)
    inv2 = (np.float32(10000.0) ** (-np.arange(32, dtype=np.float32) / np.float32(32))).astype(np.float32)
    ang2 = (pos[:, None] * inv2[None, :]).astype(np.float64)
    for t in range(2):
        a = ang[128 * t:128 * t + 128]
        c[:, C_RM + 32 * t:C_RM + 32 * t + 32] = np.concatenate([np.cos(a), np.cos(a), -np.sin(a), np.sin(a)], 1)
        a = ang2[128 * t:128 * t + 128]
        c[:, C_RD + 128 * t:C_RD + 128 * t + 128] = np.concatenate([np.cos(a), np.cos(a), -np.sin(a), np.sin(a)], 1)
    c[:, C_IOTA:C_IOTA + 128] = np.where(r < LIM, r, -999)[None, :]
    i = np.arange(8)
    c[:, C_TRI8:C_TRI8 + 64] = (i[None, :] < i[:, None]).astype(np.float32).reshape(1, 64)
    return c


class Engine:

    def __init__(self, sem, e):
        self.sem, self.e, self.n, self.seen = sem, e, 0, {}

    def wait(self, *toks):
        for t in toks:
            if t is None:
                continue
            if isinstance(t, list):
                self.wait(*t)
                continue
            s, v = t
            if self.seen.get(s.name, 0) < v:
                self.seen[s.name] = v
                if self.e is not None:
                    self.e.wait_ge(s, v)

    def go(self, f, *waits):
        self.wait(*waits)
        self.n += 1
        if self.e is not None:
            f(self.e).then_inc(self.sem, 1)
        return (self.sem, self.n)

    def raw(self, f, *waits):
        self.wait(*waits)
        if self.e is not None:
            f(self.e)

    def last(self):
        return (self.sem, self.n) if self.n else None


class DmaSem:

    def __init__(self, sem):
        self.sem, self.n = sem, 0

    def start(self, eng, out, in_, *waits):
        self.n += 16
        eng.wait(*waits)
        if eng.e is not None:
            eng.e.dma_start(out, in_).then_inc(self.sem, 16)
        return (self.sem, self.n)


def build(nc, I, table, out):
    ctx = ExitStack()
    with ctx:
        def sb(name, shape, dt=F32):
            return ctx.enter_context(nc.sbuf_tensor(name, shape, dt))

        def sem(name):
            return ctx.enter_context(nc.semaphore(name))

        ring = sb("ring", [128, NSLOT, 4096])
        H = sb("H", [128, 2, D])
        XH = sb("XH", [128, 8, S], FR)
        XL = sb("XL", [128, 8, S], FR)
        CT = sb("CT", [128, C_KEEP])
        LEVM = sb("LEVM", [128, 1024], U16)
        VS = sb("VS", [128, 256])
        VT = sb("VT", [128, 128])
        IDB = sb("IDB", [128, 128], BF16)
        CSB = sb("CSB", [128, 256], BF16)
        BC = sb("BC", [128, 2, D])
        NG = sb("NG", [128, 2, 128])
        GM = sb("GM", [128, 2, 64])
        LAMB = sb("LAMB", [128, 256])
        BFG = sb("BFG", [128, 8])
        WFG = sb("WFG", [128, 8, 8])
        WRT = sb("WRT", [128, 8, 8])
        W8 = [sb(f"W8{i}", [128, 8, 8], FR) for i in range(4)]
        CNT = sb("CNT", [1, 1], mybir.dt.int32)
        MH = sb("MH", [128, 8])
        SM = sb("SM", [128, 1024])
        WHB = [sb(f"WHB{i}", [128, 2048], FR) for i in range(2)]
        WLB = [sb(f"WLB{i}", [128, 2048], FR) for i in range(2)]

        with ExitStack() as part:
            AR1 = part.enter_context(nc.sbuf_tensor("AR1", [128, 18 * 1024], F32))
            YH = part.enter_context(nc.sbuf_tensor("YH", [128, 4, S], FR))
            YL = part.enter_context(nc.sbuf_tensor("YL", [128, 4, S], FR))
        with ExitStack() as part:
            AR2 = part.enter_context(nc.sbuf_tensor("AR2", [128, 19 * 1024], F32))
        with ExitStack() as part:
            AR3 = part.enter_context(nc.sbuf_tensor("AR3", [128, 14 * 1024 + 512], F32))
        with ExitStack() as part:
            def pt(name, shape, dt=F32):
                return part.enter_context(nc.sbuf_tensor(name, shape, dt))

            HID = pt("HID", [128, 2, 512])
            HTH = pt("HTH", [128, 2, 512], FR)
            HTL = pt("HTL", [128, 2, 512], FR)
            WHX = [pt(f"WHX{i}", [128, 2048], FR) for i in range(2)]
            WLX = [pt(f"WLX{i}", [128, 2048], FR) for i in range(2)]
            HH = pt("HH", [128, 2, D], FR)
            HL = pt("HL", [128, 2, D], FR)
            with ExitStack() as part2:
                LZ = part2.enter_context(nc.sbuf_tensor("LZ", [128, 2, D], F32))
                LT = part2.enter_context(nc.sbuf_tensor("LT", [128, 4, 512], F32))
            EH = pt("EH", [128, 8, CAP], FR)
            EL = pt("EL", [128, 8, CAP], FR)
            ZH = pt("ZH", [128, D], FR)
            ZL = pt("ZL", [128, D], FR)
            PO = pt("PO", [128, 2, CAP], FR)
            POT = pt("POT", [128, 2, 128], FR)
        PS = [ctx.enter_context(nc.psum_tensor(f"PS{i}", [128, 512], F32)) for i in range(8)]

        sems = {n: sem(n) for n in ["s_pe", "s_dve", "s_act", "s_pool", "s_sp", "s_c", "s_x", "s_v", "s_b", "s_m", "s_ln", "s_out", "s_lv", "o_pe", "o_dve", "o_act", "o_w0", "o_w1", "o_w2"]
                + [f"s_w{i}" for i in range(NSLOT)]}

        def program(name_, e):
            pe, dve, act, pool, sp = (Engine(sems["s_" + n], e if n == name_ else None) for n in ("pe", "dve", "act", "pool", "sp"))

            ident = CT[:, C_ID:C_ID + 128]
            sm_at = [0]
            area = [AR1]

            def small(n):
                a = sm_at[0]
                if a + n > 512:
                    a = 0
                sm_at[0] = a + n
                return SM[:, a:a + n]

            def arena(at, n):
                return area[0][:, at:at + n]

            def join():
                toks = [e.last() for e in (pe, dve, act, pool)]
                for x in (pe, dve, act, pool):
                    x.wait(*toks)
                return toks

            def cols(name, c0, c1):
                return (name, c0, I[name].rearrange("(t p) n -> p t n", p=128)[:, :, c0:c1], 8, c1 - c0)

            def rows(name, t0, t1):
                return (name, t0, I[name].rearrange("(t p) n -> p t n", p=128)[:, t0:t1, :], t1 - t0, D)

            def ffn_list(jobs, n):
                ls, held = [], []
                for g, u, d in jobs:
                    for c in range(0, n, 512):
                        m = min(512, n - c)
                        ls += [cols(g, c, c + m), cols(u, c, c + m)] + held
                        held = [rows(d, c // 128, (c + m) // 128)]
                return ls + held

            WL = [cols("w_mem_kv", 0, 512), cols("w_mem_kv", 512, 1024)]
            WL += [cols("w_in", c, c + 512) for c in (3080, 0, 512, 1024, 5640, 6152)] + [rows("w_br_mem", 0, 4)]
            WL += [cols("w_in", c, c + 512) for c in (1536, 2048, 2560, 3592, 4104)] + [rows("w_br_moba", 0, 4)]
            WL += [cols("w_in", c, c + 512) for c in (4616, 5128)] + [rows("w_br_fox", 0, 4)]
            WL += [cols("w_out", 0, 512), cols("w_out", 512, 1024)]
            WL += ffn_list([("w_gate", "w_up", "w_down")], FF)
            WL += [cols("hg_w_in_2", c, c + 512) for c in (1024, 1536, 0, 512, 3072, 3584, 2048, 2560)]
            WL += [cols("hg_w_out_2", 0, 512), cols("hg_w_out_2", 512, 1024)]
            WL += ffn_list([("ffn_w_gate_2", "ffn_w_up_2", "ffn_w_down_2")], FF)
            WL += [cols("da_w_in_2", c, c + 512) for c in (0, 1024, 2048, 512, 1536, 2560)]
            WL += [cols("da_w_out_2", 0, 512), cols("da_w_out_2", 512, 1024)]
            WL += ffn_list([(f"moe_w_gate_2.{e}", f"moe_w_up_2.{e}", f"moe_w_down_2.{e}") for e in range(NE)], FFE)

            slot_sem = [DmaSem(sems[f"s_w{i}"]) for i in range(NSLOT)]
            arrived = {}

            def load(i, *waits):
                if i < len(WL):
                    _, _, src, t, n = WL[i]
                    dst = ring[:, i % NSLOT, 0:t * n].rearrange("p (t n) -> p t n", t=t)
                    arrived[i] = slot_sem[i % NSLOT].start(sp, dst, src, *waits)

            groups = {(0,): (0, 0), (1,): (0, 1024), (2,): (1, 0), (3,): (1, 1024), (0, 1): (0, 0), (2, 3): (1, 0), (4,): (2, 0), (5,): (3, 0)}
            store = [(WHB[i], WLB[i]) for i in range(2)] + [(WHX[i], WLX[i]) for i in range(2)]
            slot_free = [[] for _ in range(6)]
            slot_turn = [0] * 6
            extra_on = [False]
            piece_at = [0, 0]
            piece = {}
            low = []
            turn_n = [0]

            def in_ffn(i):
                return "gate" in WL[i][0] or "up" in WL[i][0] or "down" in WL[i][0]

            PIECES = [(i, j, 2 if in_ffn(i) else 4) for i in range(len(WL)) for j in range(2 if in_ffn(i) else 4)]

            def queue_low(keep):
                while len(low) > keep:
                    k, hi, lo, src, t_hi, t_w, fr = low.pop(0)
                    t = dve.go(lambda e: e.tensor_tensor(lo, src, hi.bitcast(F32), ALU.subtract), t_hi, t_w, fr)
                    piece[k][3].append(t)
                    i, j, np_ = PIECES[k]
                    if j == np_ - 1:
                        load(i + NSLOT, t, t_hi)

            def split_ahead():
                while piece_at[0] < len(PIECES):
                    k = piece_at[0]
                    i, j, np_ = PIECES[k]
                    if i not in arrived:
                        queue_low(0)
                        if i not in arrived:
                            return
                    able = ((0, 1), (2, 3)) if np_ == 2 else ((0,), (1,), (2,), (3,))
                    if np_ == 2 and extra_on[0]:
                        able += ((4,), (5,))
                    able = [g for g in able if all(slot_free[x] is not None for x in g)]
                    if not able:
                        return
                    g = min(able, key=lambda g: max(slot_turn[x] for x in g))
                    turn_n[0] += 1
                    fr = []
                    for x in g:
                        slot_turn[x] = turn_n[0]
                        fr = fr + slot_free[x]
                        slot_free[x] = None
                    _, _, _, t, n = WL[i]
                    m = t * n // np_
                    src = ring[:, i % NSLOT, j * m:j * m + m]
                    b, at = groups[g]
                    hi, lo = (x[:, at:at + m] for x in store[b])
                    t_hi = act.go(lambda e: e.activation(hi, src, ACT.Copy), arrived[i], fr)
                    piece[k] = (g, hi, lo, [t_hi])
                    low.append((k, hi, lo, src, t_hi, arrived[i], fr))
                    piece_at[0] += 1
                    queue_low(1 if extra_on[0] else 0)

            def parts():
                return PIECES[piece_at[1]][2]

            def take(name, c0):
                split_ahead()
                k = piece_at[1]
                piece_at[1] += 1
                if len(piece[k][3]) < 2:
                    queue_low(0)
                i, j, np_ = PIECES[k]
                assert WL[i][:2] == (name, c0), (WL[i][:2], name, c0)
                g, hi, lo, toks = piece[k]
                hi, lo = (x.rearrange("p (t n) -> p t n", t=WL[i][3] // np_) for x in (hi, lo))
                return hi, lo, toks, g

            paused = [False]

            def taken(g, tok):
                for x in g:
                    slot_free[x] = [tok]
                if not paused[0]:
                    split_ahead()

            def go_on():
                paused[0] = False
                split_ahead()

            new, active = [], []
            steps = [None]

            def advance():
                for u in list(active):
                    u[1].pop(0)()
                    if not u[1]:
                        active.remove(u)

            def begin():
                u = new.pop(0)
                u[1].pop(0)()
                if u[1]:
                    active.append(u)

            def unit_hook(j):
                if j % 2:
                    advance()
                    if new:
                        n = len(active)
                        begin()
                        if new and len(active) == n:
                            begin()

            def step_hook(j):
                if steps[0] is not None and next(steps[0], "end") == "end":
                    steps[0] = None

            def drain(*banks):
                while any(not banks or u[0] in banks for u in new + active):
                    advance()
                    if new and any(not banks or u[0] in banks for u in new):
                        begin()

            def drain_steps():
                while steps[0] is not None:
                    if next(steps[0], "end") == "end":
                        steps[0] = None
                    advance()

            s_c, s_x, s_v, s_b, s_m, s_ln, s_o, s_lv = (DmaSem(sems["s_" + n]) for n in ("c", "x", "v", "b", "m", "ln", "out", "lv"))
            MEMR = arena(0, 2048).rearrange("p (a n) -> p a n", a=2)
            t_m = s_m.start(act, MEMR, I["mem"].rearrange("(a p) n -> p a n", p=128))
            t_mh = pool.go(lambda e: e.memset(MH[:, :], -0.5))
            act.go(lambda e: e.activation(SM[:, 1016:1024], MH[:, :], ACT.Exp), t_mh)
            z_vs = pool.go(lambda e: e.memset(VS[:, 0:128], 0.0))
            t_c = s_c.start(act, CT[:, :], table[:, 0:C_KEEP])
            for at, name, n in ((V_MIX, "g_mix", 8), (V_MEM, "g_mem", 8), (V_FFN, "g_ffn", 8), (V_LNG, "ln_g_2", 32),
                                (V_LNB, "ln_b_2", 32), (V_LB, "hg_lb_2", 24), (V_QC, "g_q_mem", 1), (V_KC, "g_k_mem", 1)):
                t_v = s_v.start(act, VS[at:at + n, 0:128], I[name].rearrange("(a b) -> a b", b=128), z_vs)
            for at, name in ((V_QF, "g_q_fox"), (V_KF, "g_k_fox")):
                for k in range(2):
                    t_v = s_v.start(act, VS[at:at + 1, 64 * k:64 * k + 64], I[name].rearrange("(a b) -> a b", a=1), z_vs)
            load(0, t_v)
            t_x = s_x.start(sp, H[:, :, :], I["x"].rearrange("(a p) n -> p a n", p=128))
            for i in range(1, NSLOT):
                load(i, t_v)
            LEVS = arena(4096, 1024)
            t_c2 = s_lv.start(sp, LEVS, table[:, C_KEEP:C_END])

            def bcast(ap, n):
                return ap.rearrange("(a b) -> a b", a=1).to_broadcast([128, n])

            for dst, name, n in ((GM[:, 0, :], "g_q_moba", 64), (GM[:, 1, :], "g_k_moba", 64), (NG[:, 0, :], "hg_norm_g_2", 128),
                                 (NG[:, 1, :], "da_norm_g_2", 128), (LAMB[:, :], "da_lam_2", 256), (BFG[:, :], "b_forget", 8)):
                t_b = s_b.start(pool, dst, bcast(I[name], n))
            t_b = s_b.start(pool, WFG[:, :, :], I["w_in"].rearrange("(t p) n -> p t n", p=128)[:, :, 3072:3080])
            t_b = s_b.start(pool, WRT[:, :, :], I["moe_w_router_2"].rearrange("(t p) n -> p t n", p=128))

            t_idb = dve.go(lambda e: e.tensor_copy(IDB[:, :], ident), t_c)
            t_csb = dve.go(lambda e: e.memset(CSB[:, 0:128], 0.0))
            t_csb = dve.go(lambda e: e.tensor_copy(CSB[:, 128:256], CT[:, C_CAUS:C_CAUS + 128]), t_c)

            free = [[] for _ in range(8)]

            def rsqrt(x, n, scale, eps, *waits):
                v, r = small(n), small(n)
                t = dve.go(lambda e: e.tensor_scalar(v, x, scale, eps, ALU.mult, ALU.add), *waits)
                t = pool.go(lambda e: e.tensor_tensor(r, v, MH[:, 0:n], ALU.pow), t, t_mh)
                return r, t

            def mm3(o, xh, xl, wh, wl, start, stop, mark):
                pe.raw(lambda e: e.matmul(o, xh, wh, start=start, stop=False))
                pe.raw(lambda e: e.matmul(o, xh, wl, start=False, stop=False))
                f = lambda e: e.matmul(o, xl, wh, start=False, stop=stop)
                return pe.go(f) if mark else pe.raw(f)

            def token_mm(banks, name, c0, xh, xl, n, ready, between=None, after=None):
                out_ = []
                np_ = parts()
                if np_ == 4:
                    drain(*banks)
                for h2 in range(np_):
                    hi, lo, t_w, p = take(name, c0)
                    nk = hi.shape[1]
                    for tt, b in enumerate(banks):
                        pe.wait(*t_w)
                        if h2 == 0:
                            pe.wait(free[b])
                        for j in range(nk):
                            kt = nk * h2 + j
                            pe.wait(ready[kt // 2])
                            xs = slice(128 * tt, 128 * tt + 128)
                            t = mm3(PS[b][:, 0:n], xh[:, kt, xs], xl[:, kt, xs], hi[:, j, 0:n], lo[:, j, 0:n], h2 == 0 and j == 0,
                                    h2 == np_ - 1 and j == nk - 1, j == nk - 1)
                        if h2 == np_ - 1:
                            out_.append(t)
                    if h2 == np_ - 1 and after is not None:
                        after(out_)
                    if np_ == 4:
                        unit_hook(h2)
                    taken(p, t)
                    if np_ == 4:
                        step_hook(h2)
                    if between is not None and h2 == 0:
                        between()
                return out_

            def narrow_mm(bank, i, stage, *waits):
                pe.wait(free[bank], t_w8)
                for kt in range(8):
                    pe.wait(waits[kt // 2])
                    t = mm3(PS[bank][0:8, 0:256], W8[2 * i][:, kt, :], W8[2 * i + 1][:, kt, :], XH[:, kt, :], XL[:, kt, :], kt == 0, kt == 7, kt == 7)
                t = dve.go(lambda e: e.tensor_copy(stage, PS[bank][0:8, 0:256]), t)
                pe.wait(t)
                pe.raw(lambda e: e.transpose(PS[bank][:, 256:264], stage[:, 0:128], ident[0:8, 0:8]))
                return pe.go(lambda e: e.transpose(PS[bank][:, 264:272], stage[:, 128:256], ident[0:8, 0:8]))

            def to_columns(src, ready, hi, lo, scale, shift, banks=(0, 1, 2, 3), tmp=None, halves=False):
                done = []
                w = [pe_hold[0]]

                def lows(j, b, t):
                    tm = tmp[:, j, :].rearrange("p (a n) -> p a n", a=2)
                    h2, l2 = hi[:, 2 * j:2 * j + 2, :], lo[:, 2 * j:2 * j + 2, :]
                    t1 = act.go(lambda e: e.activation(h2, tm, ACT.Copy), *t, *w)
                    t2 = dve.go(lambda e: e.tensor_tensor(l2, tm, h2.bitcast(F32), ALU.subtract), t1, *w)
                    done.append([t1, t2])

                last_ = None
                for j in range(4):
                    b = banks[j % len(banks)]
                    pe.wait(free[b], t_c, ready[j // 2] if halves else ready)
                    for a in range(2):
                        for tt in range(2):
                            kt = 2 * j + a
                            o = PS[b][:, 256 * a + 128 * tt:256 * a + 128 * tt + 128]
                            f = lambda e: e.transpose(o, src[:, tt, 128 * kt:128 * kt + 128], ident)
                            if a == 1 and tt == 1:
                                t = pe.go(f)
                            else:
                                pe.raw(f)
                    ps = PS[b][:, :].rearrange("p (a n) -> p a n", a=2)
                    h2, l2 = hi[:, 2 * j:2 * j + 2, :], lo[:, 2 * j:2 * j + 2, :]
                    if shift is not None:
                        tm = tmp[:, j, :].rearrange("p (a n) -> p a n", a=2)
                        c0, c1 = 2 * j, 2 * j + 1
                        tk = [dve.go(lambda e: e.tensor_scalar(tm[:, 0, :], ps[:, 0, :], scale[:, c0:c1], shift[:, c0:c1], ALU.mult, ALU.add), t, t_vt)]
                        tk.append(act.go(lambda e: e.activation(tm[:, 1, :], ps[:, 1, :], ACT.Identity, bias=shift[:, c1:c1 + 1], scale=scale[:, c1:c1 + 1]), *tk, t_vt))
                        free[b] = tk
                        if last_ is not None:
                            lows(*last_)
                        last_ = (j, b, tk)
                    elif scale is not None:
                        t1 = [act.go(lambda e: e.activation(h2[:, a, :], ps[:, a, :], ACT.Copy, scale=scale[:, 2 * j + a:2 * j + a + 1]), t, t_vt, *w) for a in range(2)]
                        t2 = [dve.go(lambda e: e.scalar_tensor_tensor(out=l2[:, a, :], in0=ps[:, a, :], scalar=scale[:, 2 * j + a:2 * j + a + 1], in1=h2[:, a, :].bitcast(F32),
                                                                      op0=ALU.mult, op1=ALU.subtract), *t1, t_vt, *w) for a in range(2)]
                        free[b] = t1 + t2
                        done.append(t1 + t2)
                    else:
                        t1 = act.go(lambda e: e.activation(h2, ps, ACT.Copy), t, *w)
                        t2 = dve.go(lambda e: e.tensor_tensor(l2, ps, h2.bitcast(F32), ALU.subtract), t1, *w)
                        free[b] = [t1, t2]
                        done.append([t1, t2])
                if last_ is not None:
                    lows(*last_)
                return done

            pe_hold = [None]

            def hold():
                pe_hold[0] = pe.last()

            def rms_columns(src, tmp, hi, lo, gain, *waits):
                ss = small(2)
                tok = []
                for tt in range(2):
                    tok.append(act.go(lambda e, tt=tt: e.activation(tmp[:, tt, :], src[:, tt, :], ACT.Square, accum_out=ss[:, tt:tt + 1]), *waits))
                r, t = rsqrt(ss, 2, 1.0 / D, 1e-6, *tok)
                z = [dve.go(lambda e, tt=tt: e.tensor_scalar(tmp[:, tt, :], src[:, tt, :], r[:, tt:tt + 1], None, ALU.mult), t, *waits) for tt in range(2)]
                return z, lambda: to_columns(tmp, z, hi, lo, gain, None)

            tmpA = arena(6144, 2048).rearrange("p (a n) -> p a n", a=2)
            tmpB = arena(2048, 2048).rearrange("p (a n) -> p a n", a=2)
            _, mem_columns = rms_columns(MEMR, tmpB, XH, XL, VT[:, V_MEM:V_MEM + 8], t_m)
            t = pe.go(lambda e: e.transpose(PS[0][:, 0:128], VS[:, 0:128], ident), t_v, t_c)
            t_vt = act.go(lambda e: e.activation(VT[:, :], PS[0][:, 0:128], ACT.Copy), t)
            free[0] = [t_vt]

            mt = mem_columns()

            def ar(at, a, n):
                return arena(at, a * n).rearrange("p (a n) -> p a n", a=a)

            GATE = [ar(2048, 2, D), ar(0, 2, D), ar(0, 2, D)]
            MRG = ar(4096, 2, D)
            QT = {n: ar(6144 + 1024 * i, 4, S) for i, n in enumerate(("qm", "km", "qf", "kf", "qc", "kc"))}
            VR = {n: ar(12288 + 1024 * i, 2, 512) for i, n in enumerate(("vm", "vf", "vc"))}
            XN = ar(15360, 2, 512)
            SQ = ar(16384, 2, 512)
            PB = XN
            PTB = ar(17408, 2, 512)
            YR = BC[:, :, 0:512]
            xn_free, sq_free = [[], []], [[], []]
            unit = [0]
            tr_bank = 3
            col_done = {n: [] for n in QT}
            row_done = {n: [] for n in VR}

            def qk_unit(kind, nh, bank, tt, t_mm, gain_col, gain_row):
                dh = 512 // nh
                i = unit[0] % 2
                unit[0] += 1
                sq, xn = SQ[:, i, :], XN[:, i, :]
                ss = small(nh)
                t = act.go(lambda e: e.activation(sq, PS[bank][:, :], ACT.Square), t_mm, sq_free[i])
                t = dve.go(lambda e: e.tensor_reduce(ss, sq.rearrange("p (h d) -> p h d", h=nh), AX.X, ALU.add), t)
                r, t = rsqrt(ss, nh, 1.0 / dh, 1e-6, t)
                yield
                rb = r.unsqueeze(2).to_broadcast([128, nh, dh])
                t = dve.go(lambda e: e.tensor_tensor(xn.rearrange("p (h d) -> p h d", h=nh), PS[bank][:, :].rearrange("p (h d) -> p h d", h=nh), rb, ALU.mult),
                           t, xn_free[i])
                free[bank] = [t]
                sq_free[i] = [t]
                if gain_row is not None:
                    g = gain_row.unsqueeze(1).to_broadcast([128, 8, 64])
                    x3 = xn.rearrange("p (h d) -> p h d", h=8)
                    t = dve.go(lambda e: e.tensor_tensor(x3, x3, g, ALU.mult), t, t_b)
                    cs = CT[:, C_RM + 32 * tt:C_RM + 32 * tt + 16].unsqueeze(1).to_broadcast([128, 8, 16])
                    ns = CT[:, C_RM + 32 * tt + 16:C_RM + 32 * tt + 24].unsqueeze(1).to_broadcast([128, 8, 8])
                    sn = CT[:, C_RM + 32 * tt + 24:C_RM + 32 * tt + 32].unsqueeze(1).to_broadcast([128, 8, 8])
                    u = sq[:, 0:128].rearrange("p (h d) -> p h d", h=8)
                    w = sq[:, 128:256].rearrange("p (h d) -> p h d", h=8)
                    t1 = pool.go(lambda e: e.tensor_tensor(u[:, :, 0:8], x3[:, :, 8:16], ns, ALU.mult), t, t_c)
                    t1 = pool.go(lambda e: e.tensor_tensor(u[:, :, 8:16], x3[:, :, 0:8], sn, ALU.mult), t)
                    t2 = pool.go(lambda e: e.tensor_tensor(w, x3[:, :, 0:16], cs, ALU.mult), t)
                    t = pool.go(lambda e: e.tensor_tensor(x3[:, :, 0:16], w, u, ALU.add), t1, t2)
                    sq_free[i] = [t]
                yield
                b = tr_bank
                pe.wait(free[b], t, t_c)
                for j in range(4):
                    f = lambda e, j=j: e.transpose(PS[b][:, 128 * j:128 * j + 128], xn[:, 128 * j:128 * j + 128], ident)
                    if j < 3:
                        pe.raw(f)
                    else:
                        t = pe.go(f)
                xn_free[i] = [t]
                dst = QT[kind][:, :, 128 * tt:128 * tt + 128]
                src = PS[b][:, :].rearrange("p (j n) -> p j n", j=4)
                if gain_col is None:
                    t = act.go(lambda e: e.activation(dst, src, ACT.Copy), t)
                else:
                    t = act.go(lambda e: e.activation(dst, src, ACT.Copy, scale=VT[:, gain_col:gain_col + 1]), t, t_vt)
                free[b] = [t]
                col_done[kind].append(t)

            pj = [0]

            def pj_bank(banks=(0, 1, 2, 3)):
                b = banks[pj[0] % len(banks)]
                pj[0] += 1
                return b

            def two_tiles(name, c0, ready, then, bset=((0, 1), (6, 7))):
                bs = bset[pj[0] % 2]
                pj[0] += 1

                def after(toks):
                    for tt in range(2):
                        new.append([bs[tt], then(bs[tt], tt, toks[tt])])

                token_mm(bs, name, c0, XH, XL, 512, ready, after=after)

            def stages(n, gen):
                return [lambda: next(gen, None)] * n

            def v_unit(kind):
                def f(b, tt, t):
                    def s0():
                        t1 = act.go(lambda e: e.activation(VR[kind][:, tt, :], PS[b][:, :], ACT.Copy), t)
                        free[b] = [t1]
                        row_done[kind].append(t1)
                    return [s0]
                return f

            def q_unit(kind, nh, gc, gr):
                return lambda b, tt, t: stages(3, qk_unit(kind, nh, b, tt, t, gc, gr))

            def forget_unit():
                t = narrow_mm(tr_bank, 0, NCT, *xt)
                z, a1, a2, a3 = (small(16).rearrange("p (a h) -> p a h", a=2) for _ in range(4))
                lg = SM[:, 960:976].rearrange("p (a h) -> p a h", a=2)
                t = dve.go(lambda e: e.tensor_tensor(z, PS[tr_bank][:, 256:272].rearrange("p (a h) -> p a h", a=2), BFG[:, :].unsqueeze(1).to_broadcast([128, 2, 8]), ALU.add), t, t_b)
                free[tr_bank] = [t]
                tn = dve.go(lambda e: e.tensor_scalar(a1, z, 0.0, None, ALU.min), t)
                t = act.go(lambda e: e.activation(a2, z, ACT.Abs), t)
                t = act.go(lambda e: e.activation(a2, a2, ACT.Exp, scale=-1.0), t)
                t = act.go(lambda e: e.activation(a3, a2, ACT.Ln, bias=1.0), t)
                yield
                t = dve.go(lambda e: e.tensor_tensor(lg, a1, a3, ALU.subtract), t, tn)
                LG.extend([(lg[:, 0, :], t), (lg[:, 1, :], t)])
                yield
                b = tr_bank
                pe.wait(free[b], LG[0][1], LG[1][1], t_one, t_c)
                pe.raw(lambda e: e.matmul(PS[b][0:8, 0:128], LG[0][0], triu, start=True, stop=True))
                pe.raw(lambda e: e.matmul(PS[b][0:8, 128:256], LG[0][0], ONE, start=True, stop=False))
                pe.raw(lambda e: e.matmul(PS[b][0:8, 128:256], LG[1][0], triu, start=False, stop=True))
                pe.raw(lambda e: e.matmul(PS[b][:, 256:264], triu, LG[0][0], start=True, stop=True))
                pe.raw(lambda e: e.matmul(PS[b][:, 264:272], ONE, LG[0][0], start=True, stop=False))
                t = pe.go(lambda e: e.matmul(PS[b][:, 264:272], triu, LG[1][0], start=False, stop=True))
                cum["n"] = dve.go(lambda e: e.tensor_scalar(NCT, PS[b][0:8, 0:256], -8.0, None, ALU.mult), t)
                cum["r"] = dve.go(lambda e: e.tensor_copy(CUMR, PS[b][:, 256:272].rearrange("p (a h) -> p a h", a=2)), t)
                free[b] = [cum["n"], cum["r"]]

            LG, cum = [], {}
            triu = CT[:, C_TRIU:C_TRIU + 128]
            CUMR = SM[:, 980:996].rearrange("p (a h) -> p a h", a=2)
            NCT = VS[0:8, 0:256]
            ONE = arena(17408, 128)
            t_one = pool.go(lambda e: e.memset(ONE, 1.0))
            SEL = ar(16384, 8, 128)[0:8]

            gate_tok = {}

            gate_wait = [None]

            def gate_unit(i, c):
                def f(b, tt, t):
                    g = GATE[i][:, tt, 512 * c:512 * c + 512]
                    def s0():
                        t1 = act.go(lambda e: e.activation(g, PS[b][:, :], ACT.Tanh, scale=0.5), t, gate_wait[0])
                        free[b] = [t1]
                        gate_tok[(i, tt, c)] = t1
                    def s1():
                        gate_tok[(i, tt, c)] = dve.go(lambda e: e.tensor_scalar(g, g, 0.5, 0.5, ALU.mult, ALU.add), gate_tok[(i, tt, c)])
                    return [s0, s1]
                return f

            def gate(i, c):
                two_tiles("w_in", 3592 + 1024 * i + 512 * c, xt, gate_unit(i, c))

            m_tok = {}

            def branch(i, name):
                bs = {(0, 0): 0, (0, 1): 1, (1, 0): 6, (1, 1): 7}
                drain(0, 1, 6, 7)
                for h2 in range(4):
                    hi, lo, t_w, p = take(name, 0)
                    for tt in range(2):
                        for c in range(2):
                            b = bs[(tt, c)]
                            pe.wait(*t_w, yt_tok["y"])
                            if h2 == 0:
                                pe.wait(free[b])
                            xs = slice(128 * tt, 128 * tt + 128)
                            t = mm3(PS[b][:, :], YH[:, h2, xs], YL[:, h2, xs], hi[:, 0, 512 * c:512 * c + 512], lo[:, 0, 512 * c:512 * c + 512], h2 == 0, h2 == 3, True)
                            if h2 == 3:
                                g = GATE[i][:, tt, 512 * c:512 * c + 512]
                                m = MRG[:, tt, 512 * c:512 * c + 512]
                                if (tt, c) not in m_tok:
                                    t1 = dve.go(lambda e: e.tensor_tensor(m, PS[b][:, :], g, ALU.mult), t, gate_tok[(i, tt, c)], t_lev)
                                    m_tok[(tt, c)] = t1
                                else:
                                    t1 = dve.go(lambda e: e.tensor_tensor(g, PS[b][:, :], g, ALU.mult), t, gate_tok[(i, tt, c)])
                                    m_tok[(tt, c)] = (dve if i == 1 else pool).go(lambda e: e.tensor_tensor(m, m, g, ALU.add), t1, m_tok[(tt, c)])
                                free[b] = [t1]
                    unit_hook(h2)
                    taken(p, t)
                    step_hook(h2)
                yt_tok["read"] = t

            def blocks(causal):
                return [(0, 0, 1), (1, 0, 1), (1, 1, 1)] if causal else [(0, 0, 1), (0, 1, 1), (1, 0, 1), (1, 1, 1)]

            def attention(nh, causal, scores, values, comps, weight, out_banks, dv, PBs, PTs, sbank=(2,), tbank=(3,), free_in=(), can=lambda step: True, lag=1):
                k0 = 128 if causal else 256
                width = k0 + 256
                nblk = 3 if causal else 4
                blk = [(0, 0), (1, 0), (1, 1)] if causal else [(0, 0), (0, 1), (1, 0), (1, 1)]
                ptok, pfree = {}, [list(free_in) for _ in PBs]
                ttok, tfree = {}, [list(free_in) for _ in PTs]
                stat, mixed = {}, {}
                n = 0
                for step in range(nh + lag + 1):
                    while not can(step):
                        yield
                        yield
                    if lag <= step < nh + lag:
                        h = step - lag
                        p, slot, ready = mixed[h]
                        tb = tbank[h % len(tbank)]
                        pe.wait(free[tb], ready)
                        for j in range(nblk):
                            f = lambda e, j=j, p=p, tb=tb: e.transpose(PS[tb][:, 128 * j:128 * j + 128], p[:, 128 * j:128 * j + 128], ident)
                            if j < nblk - 1:
                                pe.raw(f)
                            else:
                                t = pe.go(f)
                        for (_, sl, _, _) in stat[h]:
                            pfree[sl] = [t]
                        pt = PTs[h % 2]
                        t = act.go(lambda e, pt=pt, tb=tb: e.activation(pt[:, 0:width], PS[tb][:, 0:width], ACT.Copy), t, tfree[h % 2])
                        free[tb] = [t]
                        ttok[h] = t
                    if step > lag:
                        h = step - lag - 1
                        pt = PTs[h % 2]
                        per = 512 // dv
                        ob = out_banks[h // per]
                        co = dv * (h % per)
                        if h % per == 0:
                            pe.wait(free[ob[0]], free[ob[1]])
                        pe.wait(ttok[h])
                        for j, (q, k) in enumerate(blk):
                            last = (j == nblk - 1)
                            v = values(h, k)
                            f = lambda e: e.matmul(
                                PS[ob[q]][:, co:co + dv], pt[:, 128 * j:128 * j + 128], v, start=(k == 0),
                                stop=(k == 1 or (causal and q == 0)))
                            if last:
                                t = pe.go(f)
                            else:
                                pe.raw(f)
                        tfree[h % 2] = [t]
                        if h % per == per - 1:
                            weight["done"](h // per, ob, t)
                    if step < nh:
                        h = step
                        p_list = []
                        for c in range(comps):
                            sbk = sbank[n % len(sbank)]
                            t = scores(h, c, sbk)
                            mx, rs = small(2), SM[:, 512 + 32 * (h % 8) + 2 * c:512 + 32 * (h % 8) + 2 * c + 2]
                            nm = small(2)
                            p = PBs[n % len(PBs)]
                            pf = pfree[n % len(PBs)]
                            t0 = dve.go(lambda e, mx=mx, sbk=sbk: e.tensor_reduce(mx[:, 0:1], PS[sbk][:, 0:k0], AX.X, ALU.max), t)
                            t1 = dve.go(lambda e, mx=mx, sbk=sbk: e.tensor_reduce(mx[:, 1:2], PS[sbk][:, k0:width], AX.X, ALU.max), t)
                            nm, scale, t0 = weight["bias"](h, mx, nm, t0, t1)
                            ta = []
                            for q, (a0, a1) in enumerate(((0, k0), (k0, width))):
                                ta.append(act.go(lambda e, p=p, a0=a0, a1=a1, sbk=sbk, nm=nm, rs=rs, q=q: e.activation(
                                    p[:, a0:a1], PS[sbk][:, a0:a1], ACT.Exp, bias=nm[:, q:q + 1], scale=scale, accum_out=rs[:, q:q + 1]), t0, pf))
                            free[sbk] = ta
                            p_list.append((p, n % len(PBs), ta, rs))
                            n += 1
                        stat[h] = p_list
                    yield
                    if step < nh:
                        mixed[step] = weight["combine"](step, stat[step], k0, width)
                    yield

            def scaled_bias(scale):
                def f(h, mx, nm, t0, t1):
                    t = dve.go(lambda e: e.tensor_scalar(nm, mx, -scale, None, ALU.mult), t0, t1)
                    return nm, scale, t
                return f

            def keep_p(h, st, k0, width):
                p, slot, ta, rs = st[0]
                return p, slot, ta

            yt_tok = {}

            def head_scores(qk, kk, extra=None):
                def f(h, c, bank):
                    o, j = 64 * (h % 2), h // 2
                    q, k = QT[qk], QT[kk]
                    pe.wait(free[bank], col_done[qk], col_done[kk], t_idb, t_csb)
                    for a, b_, qt, n in ((0, 128, 0, 128), (128, 384, 1, 256)):
                        pe.raw(lambda e, a=a, b_=b_, qt=qt, n=n: e.matmul(PS[bank][:, a:b_], q[o:o + 64, j, 128 * qt:128 * qt + 128], k[o:o + 64, j, 0:n], start=True, stop=False))
                        if extra is not None:
                            extra(h, bank, a, b_, n)
                        g = lambda e: e.matmul(PS[bank][:, a:b_], IDB[:, :], CSB[:, 256 - n:256], start=False, stop=True)
                        if a:
                            t = pe.go(g)
                        else:
                            pe.raw(g)
                    return t
                return f

            def fox_extra(h, bank, a, b_, n):
                pe.wait(cum["sel"], cum["n"])
                pe.raw(lambda e: e.matmul(PS[bank][:, a:b_], SEL[:, h, :], NCT[:, 0:n], start=False, stop=False))

            def branch_done(i):
                def f(g, ob, t):
                    nh = 8 if i < 2 else 4
                    dh = 512 // nh
                    ri, rr = small(16), small(16)
                    rv = SM[:, 512:768].rearrange("p (h x) -> p h x", x=32)[:, 0:nh, 0:2]
                    rq = ri[:, 0:2 * nh].rearrange("p (h q) -> p h q", h=nh)
                    t0 = dve.go(lambda e: e.reciprocal(rq, rv), t)
                    tk = []
                    for q in range(2):
                        rb = rq[:, :, q:q + 1].to_broadcast([128, nh, dh])
                        tk.append(dve.go(lambda e, q=q, rb=rb: e.tensor_tensor(YR[:, q, :].rearrange("p (h d) -> p h d", h=nh), PS[ob[q]][:, :].rearrange("p (h d) -> p h d", h=nh), rb, ALU.mult), t0, yt_tok.get("yr")))
                        free[ob[q]] = [tk[-1]]
                    tr = []
                    ev = []
                    for half in range(2):
                        b = (2, 3)[half]
                        pe.wait(free[b], tk)
                        for a in range(2):
                            for tt in range(2):
                                j = 2 * half + a
                                f_ = lambda e, b=b, a=a, tt=tt, j=j: e.transpose(PS[b][:, 256 * a + 128 * tt:256 * a + 128 * tt + 128], YR[:, tt, 128 * j:128 * j + 128], ident)
                                if a and tt:
                                    t = pe.go(f_)
                                else:
                                    pe.raw(f_)
                        src = PS[b][:, :].rearrange("p (a n) -> p a n", a=2)
                        h2, l2 = YH[:, 2 * half:2 * half + 2, :], YL[:, 2 * half:2 * half + 2, :]
                        t1 = act.go(lambda e: e.activation(h2, src, ACT.Copy), t, yt_tok.get("read"))
                        t2 = dve.go(lambda e: e.tensor_tensor(l2, src, h2.bitcast(F32), ALU.subtract), t1)
                        free[b] = [t1, t2]
                        ev += [t1, t2]
                    yt_tok["yr"] = t
                    yt_tok["y"] = ev
                return f

            def fox_bias(h, mx, nm, t0, t1):
                cq = CUMR[:, :, h]
                w = small(2)
                t = dve.go(lambda e: e.scalar_tensor_tensor(out=w, in0=mx, scalar=0.125, in1=cq, op0=ALU.mult, op1=ALU.add), t0, t1, cum["r"])
                t = dve.go(lambda e: e.tensor_tensor(nm, cq, w, ALU.subtract), t)
                return nm, 0.125, t

            def mem_scores(h, c, bank):
                pe.wait(free[bank], col_done["qc"], col_done["kc"])
                for qt in range(2):
                    f = lambda e, qt=qt: e.matmul(PS[bank][:, 256 * qt:256 * qt + 256], QT["qc"][:, h, 128 * qt:128 * qt + 128], QT["kc"][:, h, :], start=True, stop=True)
                    if qt:
                        t = pe.go(f)
                    else:
                        pe.raw(f)
                return t

            def values(kind, dh):
                def f(h, k):
                    pe.wait(row_done[kind])
                    return VR[kind][:, k, dh * h:dh * h + dh]
                return f

            two_tiles("w_mem_kv", 0, mt, q_unit("kc", 4, V_KC, None))
            _, x_columns = rms_columns(H, tmpA, XH, XL, VT[:, V_MIX:V_MIX + 8], t_x)
            two_tiles("w_mem_kv", 512, mt, v_unit("vc"))
            hold()
            xt = x_columns()
            for i, w in enumerate((WFG, WRT)):
                t = dve.go(lambda e: e.tensor_copy(W8[2 * i][:, :, :], w[:, :, :]), t_b)
                t_w8 = dve.go(lambda e: e.tensor_tensor(W8[2 * i + 1][:, :, :], w[:, :, :], W8[2 * i][:, :, :].bitcast(F32), ALU.subtract), t)
            t_lev = pool.go(lambda e: e.tensor_copy(LEVM[:, :], LEVS), t_c2)
            two_tiles("w_in", 3080, xt, q_unit("qc", 4, V_QC, None))
            two_tiles("w_in", 0, xt, q_unit("qm", 8, None, GM[:, 0, :]))
            PM, PMT = ar(2048, 2, 512), ar(3072, 2, 512)
            PMs, PMTs = [PM[:, 0, :], PM[:, 1, :]], [PMT[:, 0, :], PMT[:, 1, :]]
            steps[0] = attention(4, False, mem_scores, values("vc", 128), 1,
                                 dict(bias=scaled_bias(128.0 ** -0.5), combine=keep_p, done=branch_done(2)), [(4, 5)], 128, PMs, PMTs,
                                 free_in=[pe.last()], can=lambda step: len(col_done["qc"]) == 2)
            two_tiles("w_in", 512, xt, q_unit("km", 8, None, GM[:, 1, :]))
            two_tiles("w_in", 1024, xt, v_unit("vm"))
            new.append([None, stages(3, forget_unit())])
            gate(2, 0)
            drain_steps()
            steps[0] = attention(8, True, head_scores("qm", "km"), values("vm", 64), 1,
                                 dict(bias=scaled_bias(0.125), combine=keep_p, done=branch_done(0)), [(4, 5)], 64, PMs, PMTs,
                                 free_in=[pe.last()], can=lambda step: len(col_done["km"]) == 2)
            gate(2, 1)
            drain()
            branch(2, "w_br_mem")
            two_tiles("w_in", 1536, xt, q_unit("qf", 8, V_QF, None))
            two_tiles("w_in", 2048, xt, q_unit("kf", 8, V_KF, None))
            two_tiles("w_in", 2560, xt, v_unit("vf"))
            drain_steps()
            gate_wait[0] = list(m_tok.values()) + [pe.last()]
            PBs = [PB[:, 0, :], PB[:, 1, :]]
            PTs = [PTB[:, 0, :], PTB[:, 1, :]]

            def fox():
                while len(col_done["kf"]) < 2 or "r" not in cum:
                    yield
                    yield
                cum["sel"] = dve.go(lambda e: e.tensor_copy(SEL, CT[0:8, C_ID:C_ID + 8].unsqueeze(2).to_broadcast([8, 8, 128])), sq_free[0], sq_free[1], t_c)
                yield from attention(8, True, head_scores("qf", "kf", fox_extra), values("vf", 64), 1,
                                     dict(bias=fox_bias, combine=keep_p, done=branch_done(1)), [(4, 5)], 64, PBs, PTs, free_in=[pe.last()])

            steps[0] = fox()
            gate(0, 0)
            gate(0, 1)
            drain(6, 7, 0, 1)
            branch(0, "w_br_moba")
            gate(1, 0)
            gate(1, 1)
            drain_steps()
            drain()
            branch(1, "w_br_fox")
            hold()
            mg = to_columns(MRG, [[m_tok[(0, c)], m_tok[(1, c)]] for c in range(2)], XH, XL, None, None, banks=(2, 3, 4, 5), halves=True)

            def moments():
                return {"st": [small(12), small(12)], "t": [[], []]}

            def accumulate(tt, c, b, t, alpha, stat, square):
                x = H[:, tt, 512 * c:512 * c + 512]
                t = dve.go(lambda e: e.scalar_tensor_tensor(out=x, in0=x, scalar=alpha, in1=PS[b][:, :], op0=ALU.mult, op1=ALU.add), t, pool.last())
                free[b] = [t]
                if stat is None:
                    return t
                if square:
                    t1 = act.go(lambda e: e.activation(BC[:, tt, 512:1024], x, ACT.Square, accum_out=stat["st"][tt][:, c:c + 1]), t)
                else:
                    t1 = dve.go(lambda e: e.bn_stats(stat["st"][tt][:, 6 * c:6 * c + 6], x), t)
                stat["t"][tt].append(t1)
                return t

            ln_tok = {}

            def load_vectors(k, *waits):
                for j, nm_ in enumerate(("ln_g_2", "ln_b_2")):
                    ln_tok[k] = s_ln.start(pool, BC[:, j, :], bcast(I[nm_][k * D:k * D + D], D), *waits)

            def layer_norm(k, ready, stat, turn_=True):
                z = LZ
                hold()
                mv, nb = small(4), small(2)
                m3 = mv.rearrange("p (a x) -> p a x", a=2)
                t = []
                for tt in range(2):
                    st = stat["st"][tt]
                    t.append(dve.go(lambda e: e.bn_aggr(m3[:, tt, :], st), stat["t"][tt]))
                v, r = small(2), small(2)
                t = dve.go(lambda e: e.tensor_scalar(v, m3[:, :, 1], 1.0, 1e-5, ALU.mult, ALU.add), *t)
                t = pool.go(lambda e: e.tensor_tensor(r, v, MH[:, 0:2], ALU.pow), t, t_mh)
                t = dve.go(lambda e: e.scalar_tensor_tensor(out=nb, in0=m3[:, :, 0], scalar=-1.0, in1=r, op0=ALU.mult, op1=ALU.mult), t)
                zt = [dve.go(lambda e: e.tensor_scalar(z[:, 0, :], H[:, 0, :], r[:, 0:1], nb[:, 0:1], ALU.mult, ALU.add), t),
                      act.go(lambda e: e.activation(z[:, 1, :], H[:, 1, :], ACT.Identity, bias=nb[:, 1:2], scale=r[:, 1:2]), t)]
                cols_ = to_columns(z, zt, XH, XL, VT[:, V_LNG + 8 * k:V_LNG + 8 * k + 8], VT[:, V_LNB + 8 * k:V_LNB + 8 * k + 8], tmp=LT) if turn_ else None
                if k < 2:
                    go_on()
                rows_ = []
                for tt in range(2):
                    for c in range(2):
                        x = dve if (k == 3 and (tt, c) != (1, 1)) or (k == 2 and (tt, c) == (1, 1)) else pool
                        cs = slice(512 * c, 512 * c + 512)
                        t = x.go(lambda e: e.tensor_tensor(H[:, tt, cs], z[:, tt, cs], BC[:, 0, cs], ALU.mult), ln_tok[k], zt)
                        rows_.append(x.go(lambda e: e.tensor_tensor(H[:, tt, cs], H[:, tt, cs], BC[:, 1, cs], ALU.add), t))
                return cols_, rows_

            def residual(name, ready, alpha, stat, square=False):
                toks = []
                for c in range(2):
                    bs = ((0, 1), (6, 7))[c]

                    def after(ts):
                        paused[0] = c == 1
                        for tt, b in enumerate(bs):
                            toks.append(accumulate(tt, c, b, ts[tt], alpha, stat, square))

                    token_mm(bs, name, 512 * c, XH, XL, 512, ready, after=after)
                return toks

            st1 = moments()
            x1 = residual("w_out", mg, 1.0, st1, True)
            join()

            def swiglu(names, n, ready):
                g_n, u_n, d_n = names
                nch = -(-n // 512)
                hid_free, t_free = [[], []], [[], []]
                hid_tok, turned = [None, None], [None, None]

                def turn(c):
                    m = min(512, n - 512 * c)
                    for tt in range(2):
                        b = 6 + tt
                        pe.wait(free[b], hid_tok[tt])
                        for j in range(m // 128):
                            f = lambda e: e.transpose(PS[b][:, 128 * j:128 * j + 128], HID[:, tt, 128 * j:128 * j + 128], ident)
                            if j == m // 128 - 1:
                                t = pe.go(f)
                            else:
                                pe.raw(f)
                        hid_free[tt] = [t]
                        t1 = act.go(lambda e: e.activation(HTH[:, tt, 0:m], PS[b][:, 0:m], ACT.Copy), t, t_free[tt])
                        t2 = dve.go(lambda e: e.tensor_tensor(HTL[:, tt, 0:m], PS[b][:, 0:m], HTH[:, tt, 0:m].bitcast(F32), ALU.subtract), t1, t_free[tt])
                        free[b] = [t1, t2]
                        turned[tt] = [t1, t2]

                def down(c):
                    m = min(512, n - 512 * c)
                    for h2 in range(2):
                        hi, lo, t_w, p = take(d_n, 4 * c)
                        nj = hi.shape[1]
                        for tt in range(2):
                            pe.wait(*t_w, turned[tt])
                            if c == 0 and h2 == 0:
                                pe.wait(free[2 * tt], free[2 * tt + 1])
                            for jj in range(nj):
                                j = nj * h2 + jj
                                xs = slice(128 * j, 128 * j + 128)
                                for half_ in range(2):
                                    cs = slice(512 * half_, 512 * half_ + 512)
                                    t = mm3(PS[2 * tt + half_][:, :], HTH[:, tt, xs], HTL[:, tt, xs], hi[:, jj, cs], lo[:, jj, cs],
                                            c == 0 and j == 0, c == nch - 1 and j == m // 128 - 1, jj == nj - 1 and half_ == 1)
                            t_free[tt] = [t]
                        taken(p, t)
                    return [t_free[0], t_free[1]]

                for c in range(nch + 1):
                    if c < nch:
                        m = min(512, n - 512 * c)
                        gt = token_mm((4, 5), g_n, 512 * c, XH, XL, m, ready, between=(lambda: turn(c - 1)) if c else None)
                        for tt in range(2):
                            t = act.go(lambda e: e.activation(HID[:, tt, 0:m], PS[4 + tt][:, 0:m], ACT.Silu), gt[tt], hid_free[tt])
                            free[4 + tt] = [t]
                            hid_tok[tt] = t
                        ut = token_mm((6, 7), u_n, 512 * c, XH, XL, m, ready)
                        for tt in range(2):
                            t = dve.go(lambda e: e.tensor_tensor(HID[:, tt, 0:m], PS[6 + tt][:, 0:m], HID[:, tt, 0:m], ALU.mult), ut[tt], hid_tok[tt])
                            free[6 + tt] = [t]
                            hid_tok[tt] = t
                    else:
                        turn(c - 1)
                    if c:
                        t = down(c - 1)
                return t

            ss = small(2)
            t = [dve.go(lambda e: e.tensor_tensor(ss[:, tt:tt + 1], st1["st"][tt][:, 0:1], st1["st"][tt][:, 1:2], ALU.add), st1["t"][tt]) for tt in range(2)]
            r, t = rsqrt(ss, 2, 1.0 / D, 1e-6, *t)
            z = [dve.go(lambda e: e.tensor_scalar(LZ[:, 0, :], H[:, 0, :], r[:, 0:1], None, ALU.mult), t),
                 act.go(lambda e: e.activation(LZ[:, 1, :], H[:, 1, :], ACT.Copy, scale=r[:, 1:2]), t)]
            xt = to_columns(LZ, z, XH, XL, VT[:, V_FFN:V_FFN + 8], None)
            go_on()
            extra_on[0] = True
            t_last = swiglu(("w_gate", "w_up", "w_down"), FF, xt)
            extra_on[0] = False

            def add_out(t, alpha, stat):
                return [accumulate(tt, c, 2 * tt + c, t[tt], alpha, stat, False) for tt in range(2) for c in range(2)]

            xo = add_out(t_last, 1.0, None)
            join()

            xt = to_columns(H, xo, XH, XL, None, None)
            area[0] = AR2

            def tokens8(at):
                return ar(at, 8, S)

            SG, KK, LF, CC, QQ, QS, KS = (tokens8(2048 * i) for i in range(7))
            EE, DD = SG, LF
            STT = arena(14336, 3072).rearrange("p (a h n) -> p a h n", a=3, h=8)
            VV = ar(17408, 2, D)
            GN = BC
            lbm, lbe, lbs, lb, oml = small(8), SM[:, 880:904], small(8), SM[:, 904:912], SM[:, 912:920]
            L3 = VT[:, V_LB:V_LB + 24].rearrange("p (a h) -> p a h", a=3)
            E3 = lbe.rearrange("p (a h) -> p a h", a=3)
            t = dve.go(lambda e: e.tensor_tensor(lbm, L3[:, 0, :], L3[:, 1, :], ALU.max), t_vt)
            t = dve.go(lambda e: e.tensor_tensor(lbm, lbm, L3[:, 2, :], ALU.max), t)
            t = dve.go(lambda e: e.tensor_tensor(E3, L3, lbm.unsqueeze(1).to_broadcast([128, 3, 8]), ALU.subtract), t)
            t = act.go(lambda e: e.activation(lbe, lbe, ACT.Exp), t)
            t = dve.go(lambda e: e.tensor_tensor(lbs, E3[:, 0, :], E3[:, 1, :], ALU.add), t)
            t = dve.go(lambda e: e.tensor_tensor(lbs, lbs, E3[:, 2, :], ALU.add), t)
            t = dve.go(lambda e: e.reciprocal(lbs, lbs), t)
            t = dve.go(lambda e: e.tensor_tensor(lb, E3[:, 0, :], lbs, ALU.mult), t)
            t_lb = dve.go(lambda e: e.tensor_scalar(oml, lb, -1.0, 1.0, ALU.mult, ALU.add), t)

            def by_columns(name, c0, h0, then):
                bs = ((0, 1, 2, 3), (4, 5, 6, 7))[pj[0] % 2]
                pj[0] += 1
                out_ = []
                for h2 in range(4):
                    hi, lo, t_w, p = take(name, c0)
                    for a, b in enumerate(bs):
                        pe.wait(*t_w, *xt[0:h2 + 1])
                        if h2 == 0:
                            pe.wait(free[b])
                        ws = slice(128 * a, 128 * a + 128)
                        for j in range(2):
                            kt = 2 * h2 + j
                            t = mm3(PS[b][:, 0:256], hi[:, j, ws], lo[:, j, ws], XH[:, kt, :], XL[:, kt, :], kt == 0, kt == 7, j == 1)
                        if h2 == 3:
                            out_.append(t)
                            then(b, h0 + a, t)
                    taken(p, t)
                    step_hook(h2)

            sg_tok = []

            def f_done(b, h, t):
                t = act.go(lambda e: e.activation(SG[:, h, :], PS[b][:, 0:256], ACT.Sigmoid), t)
                free[b] = [t]
                sg_tok.append(dve.go(lambda e: e.tensor_scalar(SG[:, h, :], SG[:, h, :], oml[:, h:h + 1], lb[:, h:h + 1], ALU.mult, ALU.add), t, t_lb))

            by_columns("hg_w_in_2", 1024, 0, f_done)
            by_columns("hg_w_in_2", 1536, 4, f_done)
            t_kk = pool.go(lambda e: e.tensor_scalar(KK, SG, -1.0, 1.0, ALU.mult, ALU.add), *sg_tok)
            RM = QS
            t_rm = pool.go(lambda e: e.memset(RM, 1.0))
            t_rm = pool.go(lambda e: e.memset(RM.rearrange("p h (a n) -> p (h a) n", a=2)[:, :, 0:1], 0.0), t_rm)
            t_ks0 = pool.go(lambda e: e.memset(KS, 0.0))
            t_st0 = pool.go(lambda e: e.memset(STT, 0.0))
            q_tok = []

            def q_done(b, h, t):
                q_tok.append(act.go(lambda e: e.activation(QQ[:, h, :], PS[b][:, 0:256], ACT.Silu), t))
                free[b] = [q_tok[-1]]

            t_lf = act.go(lambda e: e.activation(LF, SG, ACT.Ln), *sg_tok)
            by_columns("hg_w_in_2", 0, 0, q_done)
            flat = lambda x: x.rearrange("p h n -> p (h n)")
            t_cc = dve.go(lambda e: e.tensor_tensor_scan(flat(CC), flat(RM), flat(LF), 0.0, ALU.mult, ALU.add), t_lf, t_rm)
            t_qs0 = pool.go(lambda e: e.memset(QS, 0.0), t_cc)

            vg_tok, g_tok = [], {}

            def v_unit2(c):
                def f(b, tt, t):
                    def s0():
                        t1 = act.go(lambda e: e.activation(VV[:, tt, 512 * c:512 * c + 512], PS[b][:, :], ACT.Copy), t)
                        free[b] = [t1]
                        vg_tok.append(t1)
                    return [s0]
                return f

            def g_unit(c):
                def f(b, tt, t):
                    g = GN[:, tt, 512 * c:512 * c + 512]
                    g4 = g.rearrange("p (h d) -> p h d", h=4)
                    tok = {}

                    def s0():
                        tok["a"] = act.go(lambda e: e.activation(g, PS[b][:, :], ACT.Tanh, scale=0.5), t)
                        free[b] = [tok["a"]]

                    def s1():
                        t1 = dve.go(lambda e: e.tensor_scalar(g, g, 0.5, 0.5, ALU.mult, ALU.add), tok["a"])
                        g_tok[(tt, c)] = pool.go(lambda e: e.tensor_tensor(g4, g4, NG[:, 0, :].unsqueeze(1).to_broadcast([128, 4, 128]), ALU.mult), t1, t_b)
                    return [s0, s1]
                return f

            st_tok = [t_st0]
            mb = [4, 5, 6, 7]
            L = {"n": 0, "qs": [t_qs0], "ks": [t_ks0], "dd": [t_cc], "ee": [t_kk, t_lf]}

            def views(b2, *xs):
                return [flat(x).rearrange("p (y x b) -> p y x b", x=2, b=b2) for x in xs]

            def level_exps(b2):
                cv, dv_, ev = views(b2, CC, DD, EE)
                if b2 == 128:
                    ref = cv[:, :, 0, 127:128].to_broadcast([128, 8, 128])
                    t_d = dve.go(lambda e: e.tensor_tensor(dv_[:, :, 0, :], cv[:, :, 0, :], ref, ALU.subtract), t_cc, *L["dd"])
                    t_el = act.go(lambda e: e.activation(ev[:, :, 0, :], dv_[:, :, 0, :], ACT.Exp, scale=-1.0), t_d, *L["ee"])
                    t_er = act.go(lambda e: e.activation(ev[:, :, 1, :], cv[:, :, 1, :], ACT.Exp), t_cc, *L["ee"])
                else:
                    c3, d3 = (flat(x).rearrange("p (y z) -> p y z", z=2 * b2) for x in (CC, DD))
                    ref = c3[:, :, b2 - 1:b2].to_broadcast([128, 1024 // b2, 2 * b2])
                    t_d = dve.go(lambda e: e.tensor_tensor(d3, c3, ref, ALU.subtract), t_cc, *L["dd"])
                    t_el = act.go(lambda e: e.activation(ev[:, :, 0, :], dv_[:, :, 0, :], ACT.Exp, scale=-1.0), t_d, *L["ee"])
                    t_er = act.go(lambda e: e.activation(ev[:, :, 1, :], dv_[:, :, 1, :], ACT.Exp), t_d, *L["ee"])
                L["dd"] = [t_el, t_er]

            def level_operands(b2):
                ev, qv, kv, qsv, ksv = views(b2, EE, QQ, KK, QS, KS)
                t_q = dve.go(lambda e: e.tensor_tensor(qsv[:, :, 1, :], qv[:, :, 1, :], ev[:, :, 1, :], ALU.mult), *L["dd"], *q_tok, *L["qs"])
                t_k = pool.go(lambda e: e.tensor_tensor(ksv[:, :, 0, :], kv[:, :, 0, :], ev[:, :, 0, :], ALU.mult), *L["dd"], *L["ks"])
                L["ee"] = [t_q, t_k]
                L["rd"] = [t_q, t_k, t_qs0, t_ks0]

            def level_scores(b2, i):
                a_q, a_k, rd = (QS, KS, L["rd"]) if b2 else (QQ, KK, [*q_tok, t_kk])
                for s_t, t_t in ([(0, 1)] if b2 == 128 else [(0, 0), (1, 1)]):
                    for g in range(2):
                        b = mb[L["n"] % 4]
                        L["n"] += 1
                        pe.wait(free[b], *rd)
                        for j in range(4):
                            h = 4 * g + j
                            f = lambda e: e.matmul(PS[b][:, 128 * j:128 * j + 128], a_k[:, h, 128 * s_t:128 * s_t + 128], a_q[:, h, 128 * t_t:128 * t_t + 128], start=True, stop=True)
                            if j == 3:
                                t = pe.go(f)
                            else:
                                pe.raw(f)
                        src = PS[b][:, :].rearrange("p (j n) -> p j n", j=4)
                        if b2 == 128:
                            t1 = act.go(lambda e: e.activation(STT[:, 2, 4 * g:4 * g + 4, :], src, ACT.Copy), t, t_st0)
                        elif b2 == 64:
                            t1 = act.go(lambda e: e.activation(STT[0:64, s_t, 4 * g:4 * g + 4, 64:128], src[0:64, :, 64:128], ACT.Copy), t, t_st0)
                        else:
                            mk = LEVM[:, 128 * i:128 * i + 128].unsqueeze(1).to_broadcast([128, 4, 128])
                            t1 = dve.go(lambda e: e.copy_predicated(STT[:, s_t, 4 * g:4 * g + 4, :], mk, src), t, t_st0, *st_tok[-4:])
                        free[b] = [t1]
                        st_tok.append(t1)
                L["qs"] = L["ks"] = [t]

            def levels():
                before = None
                for i, b2 in enumerate((128, 64, 32, 16, 8, 4, 2, 1, 0)):
                    if b2:
                        level_exps(b2)
                    if before is not None:
                        level_scores(*before)
                    yield
                    while len(q_tok) < 8:
                        yield
                    if b2:
                        level_operands(b2)
                    before = (b2, i - 1)
                    yield
                level_scores(*before)

            steps[0] = levels()
            by_columns("hg_w_in_2", 512, 4, q_done)
            for c in range(2):
                two_tiles("hg_w_in_2", 3072 + 512 * c, xt, g_unit(c), bset=((0, 1), (2, 3)))
            for c in range(2):
                two_tiles("hg_w_in_2", 2048 + 512 * c, xt, v_unit2(c), bset=((0, 1), (2, 3)))
            drain()
            drain_steps()
            OR = ar(4096, 2, D)
            SQ2 = ar(0, 2, D)
            o_tok, ob, ts_, rr, ss = [], [], [], [], small(16)
            for tt in range(2):
                for g in range(2):
                    b = pj_bank((0, 1, 2, 3))
                    pe.wait(free[b], *st_tok, *vg_tok)
                    for j in range(4):
                        h = 4 * g + j
                        v0, v1 = VV[:, 0, 128 * h:128 * h + 128], VV[:, 1, 128 * h:128 * h + 128]
                        o = PS[b][:, 128 * j:128 * j + 128]
                        if tt == 0:
                            f = lambda e, o=o, h=h, v0=v0, v1=v1: e.matmul(o, STT[:, 0, h, :], v0, start=True, stop=True)
                        else:
                            pe.raw(lambda e, o=o, h=h, v0=v0, v1=v1: e.matmul(o, STT[:, 2, h, :], v0, start=True, stop=False))
                            f = lambda e, o=o, h=h, v0=v0, v1=v1: e.matmul(o, STT[:, 1, h, :], v1, start=False, stop=True)
                        if j == 3:
                            t = pe.go(f)
                        else:
                            pe.raw(f)
                    sq = SQ2[:, tt, 512 * g:512 * g + 512]
                    t1 = act.go(lambda e: e.activation(sq, PS[b][:, :], ACT.Square), t, *L["ee"])
                    t1 = dve.go(lambda e: e.tensor_reduce(ss[:, 4 * len(ob):4 * len(ob) + 4], sq.rearrange("p (h d) -> p h d", h=4), AX.X, ALU.add), t1)
                    ob.append((tt, g, b))
                    ts_.append(t1)
                r, t = rsqrt(ss[:, 8 * tt:8 * tt + 8], 8, 1.0 / 128, 1e-5, *ts_)
                rr.append((r, t))
            for tt, g, b in sorted(ob, key=lambda x: x[1]):
                r, t = rr[tt]
                ov = OR[:, tt, 512 * g:512 * g + 512]
                t = dve.go(lambda e: e.tensor_tensor(ov.rearrange("p (h d) -> p h d", h=4), PS[b][:, :].rearrange("p (h d) -> p h d", h=4),
                                                     r[:, 4 * g:4 * g + 4].unsqueeze(2).to_broadcast([128, 4, 128]), ALU.mult), t, *L["dd"])
                free[b] = [t]
                o_tok.append(dve.go(lambda e: e.tensor_tensor(ov, ov, GN[:, tt, 512 * g:512 * g + 512], ALU.mult), t, g_tok[(tt, g)]))
            hold()
            ot = to_columns(OR, [o_tok[0:2], o_tok[2:4]], XH, XL, None, None, banks=(4, 5, 6, 7), halves=True)
            stat_0 = moments()
            load_vectors(0, *o_tok)
            h1 = residual("hg_w_out_2", ot, ALPHA, stat_0)
            join()

            xt, rt = layer_norm(0, h1, stat_0)
            load_vectors(1, *rt)
            extra_on[0] = True
            t_last = swiglu(("ffn_w_gate_2", "ffn_w_up_2", "ffn_w_down_2"), FF, xt)
            extra_on[0] = False
            stat_1 = moments()
            xo = add_out(t_last, ALPHA, stat_1)
            join()
            xt, rt = layer_norm(1, xo, stat_1)
            load_vectors(2, *rt)

            area[0] = AR3
            QD, KD = tokens8(0), tokens8(2048)
            VD = ar(4096, 2, D)
            RX = ar(6144, 2, 512)
            RU = ar(7168, 2, 512)
            OD = ar(8192, 2, D)
            lp, ls, le, nl = SM[:, 768:896], small(2), small(2), SM[:, 920:921]
            L4 = LAMB[:, :].rearrange("p (a b d) -> p a b d", a=2, b=2)
            t = dve.go(lambda e: e.tensor_tensor(lp.rearrange("p (a d) -> p a d", a=2), L4[:, :, 0, :], L4[:, :, 1, :], ALU.mult), t_b)
            t = dve.go(lambda e: e.tensor_reduce(ls, lp.rearrange("p (a d) -> p a d", a=2), AX.X, ALU.add), t)
            t = act.go(lambda e: e.activation(le, ls, ACT.Exp), t)
            t = dve.go(lambda e: e.tensor_tensor(nl, le[:, 1:2], le[:, 0:1], ALU.subtract), t)
            t_nl = dve.go(lambda e: e.tensor_scalar(nl, nl, -LAM_INIT, None, ALU.add), t)
            t_ng = dve.go(lambda e: e.tensor_scalar(NG[:, 1, :], NG[:, 1, :], 1.0 - LAM_INIT, None, ALU.mult), t_b)
            rx_free = [[], []]
            qd_tok = [[], []]

            def rope_unit(dst, tt, c, b, t, i):
                x, u = RX[:, i, :].rearrange("p (g d) -> p g d", g=8), RU[:, i, :].rearrange("p (g d) -> p g d", g=8)
                ps = PS[b][:, :].rearrange("p (g d) -> p g d", g=8)
                a = C_RD + 128 * tt
                cs = CT[:, a:a + 64].unsqueeze(1).to_broadcast([128, 8, 64])
                ns = CT[:, a + 64:a + 96].unsqueeze(1).to_broadcast([128, 8, 32])
                sn = CT[:, a + 96:a + 128].unsqueeze(1).to_broadcast([128, 8, 32])
                t1 = dve.go(lambda e: e.tensor_tensor(x, ps, cs, ALU.mult), t, rx_free[i])
                t2 = dve.go(lambda e: e.tensor_tensor(u[:, :, 0:32], ps[:, :, 32:64], ns, ALU.mult), t)
                t3 = dve.go(lambda e: e.tensor_tensor(u[:, :, 32:64], ps[:, :, 0:32], sn, ALU.mult), t)
                free[b] = [t1, t2, t3]
                t = pool.go(lambda e: e.tensor_tensor(x, x, u, ALU.add), t1, t2, t3)
                yield
                tb = 2 + i
                pe.wait(free[tb], t)
                for j in range(4):
                    f = lambda e, j=j: e.transpose(PS[tb][:, 128 * j:128 * j + 128], RX[:, i, 128 * j:128 * j + 128], ident)
                    if j == 3:
                        t = pe.go(f)
                    else:
                        pe.raw(f)
                rx_free[i] = [t]
                t = act.go(lambda e: e.activation(dst[:, 4 * c:4 * c + 4, 128 * tt:128 * tt + 128], PS[tb][:, :].rearrange("p (j n) -> p j n", j=4), ACT.Copy), t)
                free[tb] = [t]
                qd_tok[c].append(t)

            vd_tok = [[], []]

            def da_in(k, c):
                def v_stage(b, tt, t):
                    t1 = act.go(lambda e: e.activation(VD[:, tt, 512 * c:512 * c + 512], PS[b][:, :], ACT.Copy), t)
                    free[b] = [t1]
                    vd_tok[c].append(t1)

                def then(b, tt, t):
                    if k == 2:
                        return [lambda: v_stage(b, tt, t)]
                    return stages(2, rope_unit((QD, KD)[k], tt, c, b, t, tt))
                two_tiles("da_w_in_2", 1024 * k + 512 * c, xt, then)

            def da_scores(h, c, bank):
                o = 64 * c
                pe.wait(free[bank], *qd_tok[h // 4])
                for a, b_, qt, n in ((0, 128, 0, 128), (128, 384, 1, 256)):
                    pe.raw(lambda e, a=a, b_=b_, qt=qt, n=n: e.matmul(PS[bank][:, a:b_], QD[o:o + 64, h, 128 * qt:128 * qt + 128], KD[o:o + 64, h, 0:n], start=True, stop=False))
                    g = lambda e: e.matmul(PS[bank][:, a:b_], IDB[:, :], CSB[:, 256 - n:256], start=False, stop=True)
                    if a:
                        t = pe.go(g)
                    else:
                        pe.raw(g)
                return t

            def da_combine(h, st, k0, width):
                (p0, s0, ta0, rs0), (p1, s1, ta1, rs1) = st
                r0, r1 = small(2), small(2)
                t = dve.go(lambda e: e.reciprocal(r0, rs0), *ta0)
                t1 = dve.go(lambda e: e.reciprocal(r1, rs1), *ta1)
                t1 = dve.go(lambda e: e.tensor_scalar(r1, r1, nl, None, ALU.mult), t1, t_nl)
                out_ = []
                for q, (a, b_) in enumerate(((0, k0), (k0, width))):
                    t2 = dve.go(lambda e, q=q, a=a, b_=b_: e.tensor_scalar(p1[:, a:b_], p1[:, a:b_], r1[:, q:q + 1], None, ALU.mult), t1)
                    out_.append(dve.go(lambda e, q=q, a=a, b_=b_: e.scalar_tensor_tensor(out=p0[:, a:b_], in0=p0[:, a:b_], scalar=r0[:, q:q + 1], in1=p1[:, a:b_], op0=ALU.mult, op1=ALU.add), t, t2))
                return p0, s0, out_

            od_tok = []

            def da_done(g, ob, t):
                ss = small(8)
                ts_ = []
                for q in range(2):
                    sq = TQ[:, q, :]
                    t1 = act.go(lambda e: e.activation(sq, PS[ob[q]][:, :], ACT.Square), t, tq_free[q])
                    ts_.append(dve.go(lambda e: e.tensor_reduce(ss[:, 4 * q:4 * q + 4], sq.rearrange("p (h d) -> p h d", h=4), AX.X, ALU.add), t1))
                    tq_free[q] = [ts_[-1]]
                r, t0 = rsqrt(ss, 8, 1.0 / 128, 1e-5, *ts_)
                for q in range(2):
                    b = ob[q]
                    ov = OD[:, q, 512 * g:512 * g + 512].rearrange("p (h d) -> p h d", h=4)
                    t1 = dve.go(lambda e: e.tensor_tensor(ov, PS[b][:, :].rearrange("p (h d) -> p h d", h=4), r[:, 4 * q:4 * q + 4].unsqueeze(2).to_broadcast([128, 4, 128]), ALU.mult), t0)
                    free[b] = [t1]
                    od_tok.append(dve.go(lambda e: e.tensor_tensor(ov, ov, NG[:, 1, :].unsqueeze(1).to_broadcast([128, 4, 128]), ALU.mult), t1, t_ng))

            TQ = ar(10240, 2, 512)
            tq_free = [[], []]
            DP = [ar(11264, 2, 512), ar(12288, 2, 512)]
            DPT = ar(13312, 2, 512)
            def da_values(h, k):
                pe.wait(*vd_tok[h // 4])
                return VD[:, k, 128 * h:128 * h + 128]

            sbank, tbank = [3, 2], [2]
            for c in range(2):
                da_in(0, c)
                da_in(1, c)
                da_in(2, c)
                if c == 0:
                    drain()
                    steps[0] = attention(8, True, da_scores, da_values, 2,
                                         dict(bias=scaled_bias(0.125), combine=da_combine, done=da_done), [(4, 5), (4, 5)], 128,
                                         [DP[0][:, 0, :], DP[0][:, 1, :], DP[1][:, 0, :], DP[1][:, 1, :]], [DPT[:, 0, :], DPT[:, 1, :]], sbank, tbank,
                                         can=lambda step: (step < 4 or len(qd_tok[1]) == 4) and (step < 7 or len(vd_tok[1]) == 2), lag=2)
            drain()
            sbank[:], tbank[:] = [0, 1, 3, 6], [2, 7]
            drain_steps()
            hold()
            ot = to_columns(OD, [od_tok[0:2], od_tok[2:4]], XH, XL, None, None, banks=(2, 3, 4, 5), halves=True)
            stat_2 = moments()
            h1 = residual("da_w_out_2", ot, ALPHA, stat_2)
            join()
            xt, rt = layer_norm(2, h1, stat_2)
            load_vectors(3, *rt)

            G = SM[:, 928:944].rearrange("p (a e) -> p a e", a=2)
            MK = SM[:, 944:960].rearrange("p (a e) -> p a e", a=2)
            t_hh, t_hl = [], []
            for tt in range(2):
                t_hh.append(act.go(lambda e: e.activation(HH[:, tt, :], H[:, tt, :], ACT.Copy), *rt[2 * tt:2 * tt + 2]))
                if tt == 0:
                    t_hl.append(dve.go(lambda e: e.tensor_tensor(HL[:, 0, :], H[:, 0, :], HH[:, 0, :].bitcast(F32), ALU.subtract), t_hh[0], *rt[0:2]))
            t = narrow_mm(4, 1, LAMB[0:8, :], *xt)
            lg, mx, nm, e2 = small(16), small(16), small(2), small(2)
            lg2, mx2 = (x.rearrange("p (a e) -> p a e", a=2) for x in (lg, mx))
            c4, q4 = (x.rearrange("p (t a b) -> p t a b", t=2, a=8) for x in (SM[:, 768:896], VS[:, 0:128]))
            tri = CT[:, C_TRI8:C_TRI8 + 64].rearrange("p (a b) -> p a b", a=8)
            t = dve.go(lambda e: e.tensor_copy(lg, PS[4][:, 256:272]), t)
            free[4] = [t]
            tm = [dve.go(lambda e: e.max(mx2[:, tt, :], lg2[:, tt, :]), t) for tt in range(2)]
            td = []
            for tt in range(2):
                oth = lg2[:, tt, :].unsqueeze(1).to_broadcast([128, 8, 8])
                own = lg2[:, tt, :].unsqueeze(2).to_broadcast([128, 8, 8])
                t1 = dve.go(lambda e: e.tensor_tensor(c4[:, tt], oth, own, ALU.is_gt), t)
                t2 = dve.go(lambda e: e.tensor_tensor(q4[:, tt], oth, own, ALU.is_equal), t)
                t2 = dve.go(lambda e: e.tensor_tensor(q4[:, tt], q4[:, tt], tri, ALU.mult), t2)
                td.append(dve.go(lambda e: e.tensor_tensor(c4[:, tt], c4[:, tt], q4[:, tt], ALU.add), t2, t1))
            t3 = dve.go(lambda e: e.tensor_scalar(nm, mx2[:, :, 0], -1.0, None, ALU.mult), *tm)
            t2 = dve.go(lambda e: e.tensor_reduce(MK, c4, AX.X, ALU.add), *td)
            t_mk = dve.go(lambda e: e.tensor_scalar(MK, MK, 2.0, None, ALU.is_lt), t2)
            t4 = [act.go(lambda e: e.activation(e2[:, tt:tt + 1], mx2[:, tt, 1:2], ACT.Exp, bias=nm[:, tt:tt + 1]), t3) for tt in range(2)]
            t5 = [act.go(lambda e: e.activation(lg2[:, tt, :], lg2[:, tt, :], ACT.Exp, bias=nm[:, tt:tt + 1]), t3, *td) for tt in range(2)]
            ones_m = HID[:, 0, 0:128]
            t_hl.append(dve.go(lambda e: e.tensor_tensor(HL[:, 1, :], H[:, 1, :], HH[:, 1, :].bitcast(F32), ALU.subtract), t_hh[1], *rt[2:4]))
            t_on = pool.go(lambda e: e.memset(ones_m, 1.0), *xt)
            POS = SM[:, 976:992].rearrange("p (a e) -> p a e", a=2)
            pe.wait(free[4], t_on, t_mk)
            pe.raw(lambda e: e.matmul(PS[4][:, 0:8], triu, MK[:, 0, :], start=True, stop=True))
            pe.raw(lambda e: e.matmul(PS[4][:, 8:16], ones_m, MK[:, 0, :], start=True, stop=False))
            pe.raw(lambda e: e.matmul(PS[4][:, 8:16], triu, MK[:, 1, :], start=False, stop=True))
            pe.raw(lambda e: e.matmul(PS[4][0:1, 16:24], ones_m[:, 0:1], MK[:, 0, :], start=True, stop=False))
            t_cnt = pe.go(lambda e: e.matmul(PS[4][0:1, 16:24], ones_m[:, 0:1], MK[:, 1, :], start=False, stop=True))
            most = small(1)
            t = dve.go(lambda e: e.tensor_reduce(most[0:1, :], PS[4][0:1, 16:24], AX.X, ALU.max), t_cnt)
            t_most = dve.go(lambda e: e.tensor_copy(CNT[:, :], most[0:1, :]), t)
            t = dve.go(lambda e: e.tensor_tensor(POS, PS[4][:, 0:16].rearrange("p (a e) -> p a e", a=2), MK, ALU.mult), t_cnt)
            free[4] = [t]
            t_pos = dve.go(lambda e: e.tensor_scalar(POS, POS, -1.0, None, ALU.add), t)
            iota = CT[:, C_IOTA:C_IOTA + CAP]
            t = dve.go(lambda e: e.tensor_scalar(e2, e2, 1.0, None, ALU.add), *t4)
            t = dve.go(lambda e: e.reciprocal(e2, e2), t)
            g_tok2 = [dve.go(lambda e: e.scalar_tensor_tensor(out=G[:, tt, :], in0=lg2[:, tt, :], scalar=e2[:, tt:tt + 1], in1=MK[:, tt, :], op0=ALU.mult, op1=ALU.mult), t, *t5)
                      for tt in range(2)]
            extra_on[0] = True
            M = {"po_free": [], "pot_free": [], "e_free": [], "hid_free": [[], []], "t_free": [[], []], "hid": [None, None],
                 "turned": [None, None], "n": 0, "z_free": [], "h": {}}

            def lists(ex):
                M["po"] = [dve.go(lambda e: e.tensor_scalar(PO[:, tt, :], iota, POS[:, tt, ex:ex + 1], None, ALU.is_equal), t_pos, M["po_free"]) for tt in range(2)]

            def gather(ex):
                pe.wait(M["po"], t_hh, t_hl)
                out_ = []
                for q in range(2):
                    for n, (src, dst) in enumerate(((HH, EH), (HL, EL))):
                        b = 6 + n
                        pe.wait(free[b])
                        for j in range(4):
                            d = 4 * q + j
                            for tt in range(2):
                                f = lambda e: e.matmul(PS[b][:, 128 * j:128 * j + CAP], src[:, tt, 128 * d:128 * d + 128], PO[:, tt, :], start=(tt == 0), stop=(tt == 1))
                                if j == 3 and tt == 1:
                                    t = pe.go(f)
                                else:
                                    pe.raw(f)
                        ps = PS[b][:, :].rearrange("p (j n) -> p j n", j=4)
                        if n == 0:
                            t = act.go(lambda e: e.activation(dst[:, 4 * q:4 * q + 4, :], ps, ACT.Copy), t, M["e_free"])
                        else:
                            t = dve.go(lambda e: e.tensor_copy(dst[:, 4 * q:4 * q + 4, :], ps), t, M["e_free"])
                        free[b] = [t]
                        out_.append(t)
                M["e"] = out_

            def scatter_lists(ex):
                pe.wait(free[7], M["po"], *g_tok2)
                for tt in range(2):
                    pe.raw(lambda e: e.transpose(PS[7][:, 128 * tt:128 * tt + 128], PO[:, tt, :].bitcast(F32), ident))
                pe.raw(lambda e: e.matmul(PS[7][:, 256:257], PO[:, 0, :].bitcast(F32), G[:, 0, ex:ex + 1], start=True, stop=False))
                t = pe.go(lambda e: e.matmul(PS[7][:, 256:257], PO[:, 1, :].bitcast(F32), G[:, 1, ex:ex + 1], start=False, stop=True))
                M["po_free"] = [t]
                M["pot"] = dve.go(lambda e: e.tensor_copy(POT[:, :, :], PS[7][:, 0:256].rearrange("p (a n) -> p a n", a=2)), t, M["pot_free"])
                GS = SM[:, 992 + ex:993 + ex]
                M["gs"] = dve.go(lambda e: e.tensor_copy(GS, PS[7][:, 256:257]), t)
                free[7] = [M["pot"], M["gs"]]

            def moe_mm(b, name, c0):
                for h2 in range(2):
                    hi, lo, t_w, p = take(name, c0)
                    pe.wait(*t_w, M["e"][2 * h2:2 * h2 + 2])
                    if h2 == 0:
                        pe.wait(free[b])
                    for j in range(4):
                        kt = 4 * h2 + j
                        t = mm3(PS[b][:, :], EH[:, kt, :], EL[:, kt, :], hi[:, j, :], lo[:, j, :], kt == 0, kt == 7, j == 3)
                    taken(p, t)
                M["e_free"] = [t]
                return t

            def moe_turn():
                i = (M["n"] - 1) % 2
                pe.wait(free[6], M["hid"][i])
                for j in range(4):
                    f = lambda e: e.transpose(PS[6][:, 128 * j:128 * j + 128], HID[:, i, 128 * j:128 * j + 128], ident)
                    if j == 3:
                        t = pe.go(f)
                    else:
                        pe.raw(f)
                M["hid_free"][i] = [t]
                t1 = act.go(lambda e: e.activation(HTH[:, i, :], PS[6][:, :], ACT.Copy), t, M["t_free"][i])
                t2 = dve.go(lambda e: e.tensor_tensor(HTL[:, i, :], PS[6][:, :], HTH[:, i, :].bitcast(F32), ALU.subtract), t1, M["t_free"][i])
                free[6] = [t1, t2]
                M["turned"][i] = [t1, t2]

            def moe_down(ex, c, i):
                for h2 in range(2):
                    hi, lo, t_w, p = take(f"moe_w_down_2.{ex}", 4 * c)
                    pe.wait(*t_w, M["turned"][i])
                    if c == 0 and h2 == 0:
                        pe.wait(free[4], free[5])
                    for jj in range(2):
                        j = 2 * h2 + jj
                        xs = slice(128 * j, 128 * j + 128)
                        for q in range(2):
                            cs = slice(512 * q, 512 * q + 512)
                            t = mm3(PS[4 + q][:, :], HTH[:, i, xs], HTL[:, i, xs], hi[:, jj, cs], lo[:, jj, cs], c == 0 and j == 0, c == 6 and j == 3, jj == 1 and q == 1)
                    taken(p, t)
                M["t_free"][i] = [t]
                if c == 6:
                    GS = SM[:, 992 + ex:993 + ex]
                    M["z"] = []
                    for q in range(2):
                        cs = slice(512 * q, 512 * q + 512)
                        t1 = act.go(lambda e: e.activation(ZH[:, cs], PS[4 + q][:, :], ACT.Copy, scale=GS), t, M["gs"], M["z_free"])
                        t2 = dve.go(lambda e: e.scalar_tensor_tensor(out=ZL[:, cs], in0=PS[4 + q][:, :], scalar=GS, in1=ZH[:, cs].bitcast(F32), op0=ALU.mult, op1=ALU.subtract),
                                    t1, M["gs"], M["z_free"])
                        free[4 + q] = [t1, t2]
                        M["z"] += [t1, t2]

            def combine(k, b=7):
                tt, q = k // 2, k % 2
                cs = slice(512 * q, 512 * q + 512)
                pe.wait(free[b], M["z"], M["pot"])
                pe.raw(lambda e: e.matmul(PS[b][:, :], POT[:, tt, :], ZH[:, cs], start=True, stop=False))
                t = pe.go(lambda e: e.matmul(PS[b][:, :], POT[:, tt, :], ZL[:, cs], start=False, stop=True))
                if k == 3:
                    M["z_free"] = [t]
                    M["pot_free"] = [t]
                x = H[:, tt, cs]
                M["h"][k] = dve.go(lambda e: e.tensor_tensor(x, x, PS[b][:, :], ALU.add), t, t_h, M["h"].get(k))
                free[b] = [M["h"][k]]

            lists(0)
            go_on()
            gather(0)
            t_h = dve.go(lambda e: e.tensor_scalar(H[:, :, :], H[:, :, :], ALPHA, None, ALU.mult), t_hh, t_hl)
            prev = None
            for ex in range(NE):
                for c in range(7):
                    i = M["n"] % 2
                    gb, ub = i, 2 + i
                    gt = moe_mm(gb, f"moe_w_gate_2.{ex}", 512 * c)
                    t = act.go(lambda e: e.activation(HID[:, i, :], PS[gb][:, :], ACT.Silu), gt, M["hid_free"][i], t_cnt)
                    free[gb] = [t]
                    if prev is not None:
                        moe_turn()
                    ut = moe_mm(ub, f"moe_w_up_2.{ex}", 512 * c)
                    t = dve.go(lambda e: e.tensor_tensor(HID[:, i, :], PS[ub][:, :], HID[:, i, :], ALU.mult), ut, t)
                    free[ub] = [t]
                    M["hid"][i] = t
                    if c == 6 and ex < NE - 1:
                        gather(ex + 1)
                    if ex and 1 <= c <= 4:
                        combine(c - 1)
                    if c == 5:
                        scatter_lists(ex)
                        if ex < NE - 1:
                            lists(ex + 1)
                    if prev is not None:
                        moe_down(*prev)
                    prev = (ex, c, i)
                    M["n"] += 1
            moe_turn()
            moe_down(*prev)
            stat_3 = moments()
            for k in range(4):
                combine(k, (7, 0, 1, 2)[k])
                tt, c = k // 2, k % 2
                stat_3["t"][tt].append(dve.go(lambda e: e.bn_stats(stat_3["st"][tt][:, 6 * c:6 * c + 6], H[:, tt, 512 * c:512 * c + 512]), M["h"][k]))
            xo = list(M["h"].values())

            def second_pass():
                e_, d_, a_, w_ = (Engine(sems["o_" + n], x.e) for n, x in (("pe", pe), ("dve", dve), ("act", act), ("w0", sp)))
                ws = [DmaSem(sems[f"o_w{i}"]) for i in range(3)]
                before = [x.last() for x in (pe, dve, act, pool)]
                for x in (e_, d_, a_, w_):
                    x.wait(*before)
                XO = LZ[:, 0, :].rearrange("p (k n) -> p k n", k=8)
                ZO = LZ[:, 1, :]
                HO, TO = LT[:, 0, :], LT[:, 1, :]
                P2 = HID[:, 0, 0:256].rearrange("p (a n) -> p a n", a=2)
                P2T = HID[:, 0, 256:512].rearrange("p (a n) -> p a n", a=2)
                GO = HID[:, 1, 0:1]
                POS2 = HID[:, 1, 8:24].rearrange("p (a n) -> p a n", a=2)
                t_pos2 = d_.go(lambda e: e.tensor_scalar(POS2, POS[:, :, :], float(-LIM), None, ALU.add))

                def chain(x, fs, *waits):
                    x.wait(*waits)
                    for f in fs[:-1]:
                        x.raw(f)
                    return x.go(fs[-1])

                def mm(o, l, r, a, b):
                    return lambda e: e.matmul(o, l, r, start=a, stop=b)

                used_ = [None, None, None]
                for ex in range(NE):
                    for tt in range(2):
                        t = d_.go(lambda e: e.tensor_scalar(P2[:, tt, :], iota, POS2[:, tt, ex:ex + 1], None, ALU.is_equal), t_pos2, e_.last())
                    ms = []
                    for k in range(8):
                        o = PS[k // 4][:, 128 * (k % 4):128 * (k % 4) + 128]
                        ks = slice(128 * k, 128 * k + 128)
                        for n, (src, tt) in enumerate(((HH, 0), (HL, 0), (HH, 1), (HL, 1))):
                            ms.append(mm(o, src[:, tt, ks].bitcast(F32), P2[:, tt, :], n == 0, n == 3))
                    for tt in range(2):
                        ms.append(lambda e, tt=tt: e.transpose(PS[2][:, 128 * tt:128 * tt + 128], P2[:, tt, :], ident))
                    for tt in range(2):
                        ms.append(mm(PS[2][:, 256:257], P2[:, tt, :], G[:, tt, ex:ex + 1], tt == 0, tt == 1))
                    t = chain(e_, ms, t)
                    for q in range(2):
                        d_.go(lambda e: e.tensor_copy(XO[:, 4 * q:4 * q + 4, :], PS[q][:, :].rearrange("p (j n) -> p j n", j=4)), t)
                    d_.go(lambda e: e.tensor_copy(P2T, PS[2][:, 0:256].rearrange("p (a n) -> p a n", a=2)), t)
                    t_g = d_.go(lambda e: e.tensor_copy(GO, PS[2][:, 256:257]), t)
                    for c in range(7):
                        n0 = 512 * c
                        srcs = [I[f"moe_w_gate_2.{ex}"].rearrange("(t p) n -> p t n", p=128)[:, :, n0:n0 + 512],
                                I[f"moe_w_up_2.{ex}"].rearrange("(t p) n -> p t n", p=128)[:, :, n0:n0 + 512],
                                I[f"moe_w_down_2.{ex}"].rearrange("(t p) n -> p t n", p=128)[:, 4 * c:4 * c + 4, :]]
                        wv = [ring[:, i, :].rearrange("p (t n) -> p t n", t=8 if i < 2 else 4) for i in range(3)]
                        tw = [ws[i].start(w_, wv[i], srcs[i], used_[i]) for i in range(3)]
                        tk = []
                        for i in range(2):
                            tk.append(chain(e_, [mm(PS[3 + i][:, :], XO[:, k, :], wv[i][:, k, :], k == 0, k == 7) for k in range(8)], tw[i], t_g))
                            used_[i] = tk[i]
                        t = a_.go(lambda e: e.activation(HO, PS[3][:, :], ACT.Silu), tk[0])
                        t = d_.go(lambda e: e.tensor_tensor(HO, PS[4][:, :], HO, ALU.mult), t, tk[1])
                        t = chain(e_, [lambda e, j=j: e.transpose(PS[5][:, 128 * j:128 * j + 128], HO[:, 128 * j:128 * j + 128], ident) for j in range(4)], t)
                        t = a_.go(lambda e: e.activation(TO, PS[5][:, :], ACT.Copy), t)
                        t = chain(e_, [mm(PS[6 + q][:, :], TO[:, 128 * j:128 * j + 128], wv[2][:, j, 512 * q:512 * q + 512], c == 0 and j == 0, c == 6 and j == 3)
                                       for j in range(4) for q in range(2)], t, tw[2])
                        used_[2] = t
                    for q in range(2):
                        t1 = d_.go(lambda e: e.tensor_scalar(ZO[:, 512 * q:512 * q + 512], PS[6 + q][:, :], GO, None, ALU.mult), t)
                    for k in range(4):
                        tt, cs = k // 2, slice(512 * (k % 2), 512 * (k % 2) + 512)
                        t = e_.go(lambda e: e.matmul(PS[k][:, :], P2T[:, tt, :], ZO[:, cs], start=True, stop=True), t1)
                        x = H[:, tt, cs]
                        t = d_.go(lambda e: e.tensor_tensor(x, x, PS[k][:, :], ALU.add), t)
                        if ex == NE - 1:
                            d_.go(lambda e: e.bn_stats(stat_3["st"][tt][:, 6 * (k % 2):6 * (k % 2) + 6], x), t)
                    e_.wait(d_.last())
                    a_.wait(d_.last())
                for x in (e_, d_, a_, w_):
                    x.wait(d_.last(), e_.last(), a_.last())

            for x in (pe, dve, act, sp):
                x.wait(t_most)
            live = [x for x in (pe, dve, act, sp) if x.e is not None]
            if live:
                n_most = live[0].e.value_load(CNT[0:1, 0:1], min_val=0, max_val=S)
                with live[0].e.If(n_most > LIM):
                    second_pass()
            join()
            xt, rt = layer_norm(3, xo, stat_3, turn_=False)
            for tt in range(2):
                t = s_o.start(act, out[128 * tt:128 * tt + 128, :], H[:, tt, :], *rt[2 * tt:2 * tt + 2])
            act.wait(t)
            for x in (pe, dve, pool, sp):
                x.wait(t)

        block = ctx.enter_context(nc.Block())

        @block.sync
        def _(e):
            program("sp", e)

        @block.scalar
        def _(e):
            program("act", e)

        @block.gpsimd
        def _(e):
            program("pool", e)

        @block.tensor
        def _(e):
            program("pe", e)

        @block.vector
        def _(e):
            program("dve", e)


_FLAT = ("g_mix", "b_forget", "g_q_moba", "g_k_moba", "g_q_fox", "g_k_fox", "g_q_mem", "g_k_mem", "g_mem", "g_ffn",
         "hg_lb_2", "hg_norm_g_2", "da_lam_2", "da_norm_g_2", "ln_g_2", "ln_b_2")
_ROWS = ("x", "mem", "w_in", "w_mem_kv", "w_br_moba", "w_br_fox", "w_br_mem", "w_out", "w_gate", "w_up", "w_down",
         "hg_w_in_2", "hg_w_out_2", "da_w_in_2", "da_w_out_2", "ffn_w_gate_2", "ffn_w_up_2", "ffn_w_down_2",
         "moe_w_router_2")
_EXPERT = ("moe_w_gate_2", "moe_w_up_2", "moe_w_down_2")


def kernel(**inputs):
    import concourse.bacc as _bacc
    from concourse.bass_utils import run_bass_kernel_spmd as _run

    nc = _bacc.Bacc("TRN2", target_bir_lowering=False, num_devices=1)
    arrays, I = {}, {}
    for name in _FLAT + _ROWS + _EXPERT:
        a = np.ascontiguousarray(inputs[name])
        if name in _FLAT:
            a = a.reshape(-1)
        elif name in _ROWS:
            a = a.reshape(a.shape[-2], a.shape[-1])
        else:
            a = a.reshape(a.shape[-3], a.shape[-2], a.shape[-1])
        arrays["in_" + name] = a
        ap = nc.dram_tensor("in_" + name, a.shape, mybir.dt.from_np(a.dtype), kind="ExternalInput").ap()
        I[name] = ap
        if name in _EXPERT:
            for e in range(NE):
                I[f"{name}.{e}"] = ap[e, :, :]
    c = constant_table()
    arrays["in_table"] = c
    table = nc.dram_tensor("in_table", c.shape, F32, kind="ExternalInput").ap()
    out = nc.dram_tensor("out_0", (S, D), F32, kind="ExternalOutput").ap()
    build(nc, I, table, out)
    r = _run(nc, [arrays], core_ids=[0])
    return np.asarray(r.results[0]["out_0"]).reshape(1, S, D)
```
